# Optimizing a Trainium2 kernel written in Bass

```python
import jax, jax.numpy as jnp
from jax import lax
import numpy as np

D_MODEL = 1024
BATCH = 1
SEQ = 256
DEPTH = 2

N_EVEN = (DEPTH + 1) // 2
N_ODD = DEPTH // 2
D_PLE = 256
D_FF = 4 * D_MODEL
DN_ALPHA = (2.0 * DEPTH) ** 0.25
DN_BETA = (8.0 * DEPTH) ** -0.25
LN_EPS = 1e-5
NEG = -1e30

A_HEADS = 4
A_DH = D_MODEL // 8
A_W = A_HEADS * A_DH
A_CONV = 4
A_CHUNK = 64

B_HEADS = 8
B_DH = 64
B_W = B_HEADS * B_DH
B_KV = 2
B_HPG = B_HEADS // B_KV
B_KVW = B_KV * B_DH
B_CMP_LEN = 32
B_CMP_STRIDE = 16
B_CMP_HID = 128
B_SEL_BLK = 64
B_SEL_N = 16
B_WIN = 512
B_QBLK = 64

C_HEADS = 8
C_DN = 128
C_DR = 64
C_DV = 128
C_QL = 512
C_KVL = 256
C_IDX_HEADS = 8
C_IDX_DH = 64
C_IDX_DR = 32
C_TOPK = 256
C_QBLK = 128
ROPE_BASE = 10000.0

EVEN_SIZES = (A_W, A_W, A_W, A_W, A_HEADS, A_HEADS, B_W, B_KVW, B_KVW, B_KVW, B_KVW, B_KVW, B_KVW, 3 * B_HEADS)
ODD_SIZES = (C_QL, C_KVL, C_DR, C_IDX_DH, C_IDX_HEADS)


def _split(z, sizes):
    out, o = [], 0
    for s in sizes:
        out.append(z[..., o:o + s])
        o += s
    return out

def _layer_norm(x, g, b):
    xf = x.astype(jnp.float32)
    mu = xf.mean(-1, keepdims=True)
    var = jnp.square(xf - mu).mean(-1, keepdims=True)
    return ((xf - mu) * lax.rsqrt(var + LN_EPS) * g + b).astype(x.dtype)

def _rms_norm(x, g):
    xf = x.astype(jnp.float32)
    return (xf * lax.rsqrt(jnp.square(xf).mean(-1, keepdims=True) + LN_EPS) * g).astype(x.dtype)

def _masked_softmax(s, mask):
    s = jnp.where(mask, s.astype(jnp.float32), NEG)
    return jnp.where(mask, jax.nn.softmax(s, axis=-1), 0.0)

def _causal_dwconv(x, w):
    k = w.shape[0]
    return lax.conv_general_dilated(x, w[:, None, :].astype(x.dtype), window_strides=(1,), padding=[(k - 1, 0)],
                                    dimension_numbers=('NWC', 'WIO', 'NWC'), feature_group_count=x.shape[-1])

def _rope_tables(pos, d):
    inv = ROPE_BASE ** (-jnp.arange(0, d, 2, dtype=jnp.float32) / d)
    ang = pos.astype(jnp.float32)[..., None] * inv
    return jnp.cos(ang), jnp.sin(ang)

def _rope(x, cos, sin):
    h = x.shape[-1] // 2
    c, s = cos.astype(x.dtype), sin.astype(x.dtype)
    x1, x2 = x[..., :h], x[..., h:]
    return jnp.concatenate([x1 * c - x2 * s, x1 * s + x2 * c], -1)

def _mlstm(q, k, v, o, ig, fg, conv_w, norm_g):
    B, T, _ = q.shape
    dt = q.dtype
    qk = jax.nn.silu(_causal_dwconv(jnp.concatenate([q, k], -1), conv_w))
    q, k = qk[..., :A_W], qk[..., A_W:]
    N = T // A_CHUNK

    def heads(u):
        return u.astype(jnp.float32).reshape(B, N, A_CHUNK, A_HEADS, A_DH).transpose(1, 0, 3, 2, 4)

    def gate(u):
        return u.astype(jnp.float32).reshape(B, N, A_CHUNK, A_HEADS).transpose(1, 0, 3, 2)

    xs = (heads(q) * A_DH ** -0.5, heads(k), heads(v), gate(ig), jax.nn.log_sigmoid(gate(fg)))
    causal = jnp.tril(jnp.ones((A_CHUNK, A_CHUNK), bool))

    def step(carry, inp):
        C, n, m = carry
        qc, kc, vc, ic, lf = inp
        b = jnp.cumsum(lf, axis=-1)
        D = jnp.where(causal, b[..., :, None] - b[..., None, :] + ic[..., None, :], NEG)
        m_inter = b + m[..., None]
        m_t = jnp.maximum(m_inter, D.max(-1))
        e_inter = jnp.exp(m_inter - m_t)
        S = jnp.einsum('bhld,bhsd->bhls', qc, kc) * jnp.exp(D - m_t[..., None])
        num = e_inter[..., None] * jnp.einsum('bhld,bhvd->bhlv', qc, C) + jnp.einsum('bhls,bhsv->bhlv', S, vc)
        den = e_inter * jnp.einsum('bhld,bhd->bhl', qc, n) + S.sum(-1)
        hc = num / jnp.maximum(jnp.abs(den), jnp.exp(-m_t))[..., None]
        bL = b[..., -1]
        dec = bL[..., None] - b + ic
        m_new = jnp.maximum(bL + m, dec.max(-1))
        w = jnp.exp(dec - m_new[..., None])
        e_st = jnp.exp(bL + m - m_new)
        C_new = e_st[..., None, None] * C + jnp.einsum('bhs,bhsv,bhsd->bhvd', w, vc, kc)
        n_new = e_st[..., None] * n + jnp.einsum('bhs,bhsd->bhd', w, kc)
        return (C_new, n_new, m_new), hc

    init = (jnp.zeros((B, A_HEADS, A_DH, A_DH), jnp.float32), jnp.zeros((B, A_HEADS, A_DH), jnp.float32),
            jnp.zeros((B, A_HEADS), jnp.float32))
    _, hs = lax.scan(step, init, xs)
    hs = hs.transpose(1, 0, 3, 2, 4).reshape(B, T, A_HEADS, A_DH)
    mu = hs.mean(-1, keepdims=True)
    var = jnp.square(hs - mu).mean(-1, keepdims=True)
    hn = ((hs - mu) * lax.rsqrt(var + LN_EPS)).reshape(B, T, A_W) * norm_g
    return (hn * jax.nn.sigmoid(o.astype(jnp.float32))).astype(dt)

def _nsa(q, kc_raw, vc_raw, ks, vs, kw, vw, g_pre, cmp_pos, cmp_w1, cmp_w2):
    B, T, _ = q.shape
    dt = q.dtype
    q = q.reshape(B, T, B_KV, B_HPG, B_DH) * B_DH ** -0.5
    r = lambda u: u.reshape(B, T, B_KV, B_DH)
    M = (T - B_CMP_LEN) // B_CMP_STRIDE + 1
    NSB = T // B_SEL_BLK
    n_sel = min(B_SEL_N, NSB)
    win = jnp.arange(M)[:, None] * B_CMP_STRIDE + jnp.arange(B_CMP_LEN)[None, :]

    def compress(u, j):
        blk = u[:, win] + cmp_pos[j][None, None, :, None, :].astype(dt)
        blk = blk.transpose(0, 1, 3, 2, 4).reshape(B, M, B_KV, B_CMP_LEN * B_DH)
        return jax.nn.gelu(blk @ cmp_w1[j]) @ cmp_w2[j]

    k_cmp = compress(r(kc_raw), 0)
    v_cmp = compress(r(vc_raw), 1)
    cmp_end = jnp.arange(M) * B_CMP_STRIDE + B_CMP_LEN - 1
    mi, jb = jnp.arange(M), jnp.arange(NSB)
    overlap = ((mi[:, None] * B_CMP_STRIDE < (jb[None, :] + 1) * B_SEL_BLK) &
               (mi[:, None] * B_CMP_STRIDE + B_CMP_LEN > jb[None, :] * B_SEL_BLK)).astype(jnp.float32)
    ks_blk = r(ks).reshape(B, NSB, B_SEL_BLK, B_KV, B_DH).transpose(0, 3, 1, 2, 4)
    vs_blk = r(vs).reshape(B, NSB, B_SEL_BLK, B_KV, B_DH).transpose(0, 3, 1, 2, 4)
    kw_pad = jnp.pad(r(kw), ((0, 0), (B_WIN, 0), (0, 0), (0, 0)))
    vw_pad = jnp.pad(r(vw), ((0, 0), (B_WIN, 0), (0, 0), (0, 0)))
    gates = jax.nn.sigmoid(g_pre.astype(jnp.float32)).reshape(B, T, B_KV, B_HPG, 3)
    bi = jnp.arange(B)[:, None, None, None]
    gi = jnp.arange(B_KV)[None, :, None, None]
    wlen = B_WIN + B_QBLK

    def block(c):
        s0 = c * B_QBLK
        tq = s0 + jnp.arange(B_QBLK)
        qb = lax.dynamic_slice_in_dim(q, s0, B_QBLK, 1)
        s = jnp.einsum('bqghd,bmgd->bqghm', qb, k_cmp)
        p_cmp = _masked_softmax(s, (cmp_end[None, :] <= tq[:, None])[None, :, None, None, :])
        o_cmp = jnp.einsum('bqghm,bmgd->bqghd', p_cmp.astype(dt), v_cmp)
        imp = p_cmp.sum(3) @ overlap
        cur = tq[:, None] // B_SEL_BLK
        forced = (jb[None, :] == 0) | (jb[None, :] == cur) | (jb[None, :] == cur - 1)
        valid = jb[None, :] * B_SEL_BLK <= tq[:, None]
        score = jnp.where(forced[None, :, None, :], 1e6, imp)
        score = jnp.where(valid[None, :, None, :], score, NEG)
        _, idx = lax.top_k(score, n_sel)
        idx = idx.transpose(0, 2, 1, 3)
        k_sel = ks_blk[bi, gi, idx].reshape(B, B_KV, B_QBLK, n_sel * B_SEL_BLK, B_DH)
        v_sel = vs_blk[bi, gi, idx].reshape(B, B_KV, B_QBLK, n_sel * B_SEL_BLK, B_DH)
        kpos = (idx[..., None] * B_SEL_BLK + jnp.arange(B_SEL_BLK)).reshape(B, B_KV, B_QBLK, n_sel * B_SEL_BLK)
        s = jnp.einsum('bgqhd,bgqkd->bgqhk', qb.transpose(0, 2, 1, 3, 4), k_sel)
        p = _masked_softmax(s, (kpos <= tq[None, None, :, None])[:, :, :, None, :])
        o_sel = jnp.einsum('bgqhk,bgqkd->bqghd', p.astype(dt), v_sel)
        kwb = lax.dynamic_slice_in_dim(kw_pad, s0, wlen, 1)
        vwb = lax.dynamic_slice_in_dim(vw_pad, s0, wlen, 1)
        wpos = s0 - B_WIN + jnp.arange(wlen)
        wmask = (wpos[None, :] <= tq[:, None]) & (wpos[None, :] > tq[:, None] - B_WIN) & (wpos[None, :] >= 0)
        s = jnp.einsum('bqghd,bkgd->bqghk', qb, kwb)
        p = _masked_softmax(s, wmask[None, :, None, None, :])
        o_win = jnp.einsum('bqghk,bkgd->bqghd', p.astype(dt), vwb)
        gb = lax.dynamic_slice_in_dim(gates, s0, B_QBLK, 1).astype(dt)
        o = gb[..., 0:1] * o_cmp + gb[..., 1:2] * o_sel + gb[..., 2:3] * o_win
        return o.reshape(B, B_QBLK, B_W)

    out = lax.map(block, jnp.arange(T // B_QBLK))
    return out.transpose(1, 0, 2, 3).reshape(B, T, B_W)

def _even_mixer(h, w_in, a_conv, a_i_b, a_f_b, a_norm, b_cmp_pos, b_cmp_w1, b_cmp_w2, b_g_b, w_out):
    aq, ak, av, ao, ai, af, bq, bkc, bvc, bks, bvs, bkw, bvw, bg = _split(h @ w_in, EVEN_SIZES)
    ya = _mlstm(aq, ak, av, ao, ai + a_i_b, af + a_f_b, a_conv, a_norm)
    yb = _nsa(bq, bkc, bvc, bks, bvs, bkw, bvw, bg + b_g_b, b_cmp_pos, b_cmp_w1, b_cmp_w2)
    return jnp.concatenate([ya, yb], -1) @ w_out

def _odd_mixer(h, pos, w_in, q_norm, kv_norm, w_qb, w_uk, w_uv, w_iq, ik_g, ik_b, w_out):
    B, T, _ = h.shape
    dt = h.dtype
    cq, ckv, kr, ik, iw = _split(h @ w_in, ODD_SIZES)
    cq = _rms_norm(cq, q_norm)
    ckv = _rms_norm(ckv, kv_norm)
    cos, sin = _rope_tables(pos, C_DR)
    qf = (cq @ w_qb).reshape(B, T, C_HEADS, C_DN + C_DR)
    q_rope = _rope(qf[..., C_DN:], cos[:, :, None], sin[:, :, None])
    k_rope = _rope(kr, cos, sin)
    q_abs = jnp.einsum('bthd,chd->bthc', qf[..., :C_DN], w_uk)
    qa = jnp.concatenate([q_abs, q_rope], -1) * (C_DN + C_DR) ** -0.5
    kv_cat = jnp.concatenate([ckv, k_rope], -1)
    icos, isin = _rope_tables(pos, C_IDX_DR)
    qi = (cq @ w_iq).reshape(B, T, C_IDX_HEADS, C_IDX_DH)
    qi = jnp.concatenate([_rope(qi[..., :C_IDX_DR], icos[:, :, None], isin[:, :, None]), qi[..., C_IDX_DR:]], -1)
    ki = _layer_norm(ik, ik_g, ik_b)
    ki = jnp.concatenate([_rope(ki[..., :C_IDX_DR], icos, isin), ki[..., C_IDX_DR:]], -1)
    wi = iw * (C_IDX_HEADS ** -0.5 * C_IDX_DH ** -0.5)
    k_sel = min(C_TOPK, T // 4)
    kpos = jnp.arange(T)
    bidx = jnp.arange(B)[:, None, None]

    def block(c):
        s0 = c * C_QBLK
        tq = s0 + jnp.arange(C_QBLK)
        qib = lax.dynamic_slice_in_dim(qi, s0, C_QBLK, 1)
        wib = lax.dynamic_slice_in_dim(wi, s0, C_QBLK, 1)
        isc = jnp.einsum('bqh,bqhs->bqs', wib, jax.nn.relu(jnp.einsum('bqhd,bsd->bqhs', qib, ki))).astype(jnp.float32)
        isc = jnp.where(kpos[None, None, :] <= tq[None, :, None], isc, NEG)
        _, idx = lax.top_k(isc, k_sel)
        g = kv_cat[bidx, idx]
        qab = lax.dynamic_slice_in_dim(qa, s0, C_QBLK, 1)
        s = jnp.einsum('bqhc,bqkc->bqhk', qab, g)
        pr = _masked_softmax(s, (idx <= tq[None, :, None])[:, :, None, :])
        return jnp.einsum('bqhk,bqkc->bqhc', pr.astype(dt), g[..., :C_KVL])

    o_lat = lax.map(block, jnp.arange(T // C_QBLK))
    o_lat = o_lat.transpose(1, 0, 2, 3, 4).reshape(B, T, C_HEADS, C_KVL)
    o = jnp.einsum('bthc,chv->bthv', o_lat, w_uv).reshape(B, T, C_HEADS * C_DV)
    return o @ w_out

def first_inputs(seed: int = 0) -> dict:
    key = jax.random.key(seed)
    keys = iter(jax.random.split(key, 64))

    def nrm(shape, scale):
        return jax.random.normal(next(keys), shape, jnp.float32) * scale

    E, O, L, D = N_EVEN, N_ODD, DEPTH, D_MODEL
    sD = D ** -0.5
    x = nrm((BATCH, SEQ, D), 1.0)
    p = nrm((DEPTH, BATCH, SEQ, D_PLE), 1.0)
    positions = jnp.broadcast_to(jnp.arange(SEQ, dtype=jnp.int32), (BATCH, SEQ))
    seg = lambda n, sc=1.0: nrm((E, D, n), sD * sc)
    e_w_in = jnp.concatenate([seg(A_W), seg(A_W), seg(A_W, DN_BETA), seg(A_W), seg(A_HEADS), seg(A_HEADS),
                              seg(B_W), seg(B_KVW), seg(B_KVW, DN_BETA), seg(B_KVW), seg(B_KVW, DN_BETA),
                              seg(B_KVW), seg(B_KVW, DN_BETA), seg(3 * B_HEADS)], axis=-1)
    e_a_conv = nrm((E, A_CONV, 2 * A_W), A_CONV ** -0.5)
    e_a_i_b = nrm((E, A_HEADS), 0.1)
    e_a_f_b = jnp.linspace(3.0, 6.0, A_HEADS, dtype=jnp.float32)[None] + nrm((E, A_HEADS), 0.1)
    e_a_norm = 1.0 + nrm((E, A_W), 0.02)
    e_b_cmp_pos = nrm((E, 2, B_CMP_LEN, B_DH), 0.1)
    e_b_cmp_w1 = nrm((E, 2, B_CMP_LEN * B_DH, B_CMP_HID), (B_CMP_LEN * B_DH) ** -0.5)
    e_b_cmp_w2 = nrm((E, 2, B_CMP_HID, B_DH), B_CMP_HID ** -0.5) * jnp.array([1.0, DN_BETA], jnp.float32)[None, :, None, None]
    e_b_g_b = nrm((E, 3 * B_HEADS), 0.1)
    e_w_out = nrm((E, A_W + B_W, D), (A_W + B_W) ** -0.5 * DN_BETA)
    o_w_in = jnp.concatenate([nrm((O, D, n), sD) for n in ODD_SIZES], axis=-1)
    o_q_norm = 1.0 + nrm((O, C_QL), 0.02)
    o_kv_norm = 1.0 + nrm((O, C_KVL), 0.02)
    o_w_qb = nrm((O, C_QL, C_HEADS * (C_DN + C_DR)), C_QL ** -0.5)
    o_w_uk = nrm((O, C_KVL, C_HEADS, C_DN), C_KVL ** -0.5)
    o_w_uv = nrm((O, C_KVL, C_HEADS, C_DV), C_KVL ** -0.5 * DN_BETA)
    o_w_iq = nrm((O, C_QL, C_IDX_HEADS * C_IDX_DH), C_QL ** -0.5)
    o_ik_g = 1.0 + nrm((O, C_IDX_DH), 0.02)
    o_ik_b = nrm((O, C_IDX_DH), 0.02)
    o_w_out = nrm((O, C_HEADS * C_DV, D), (C_HEADS * C_DV) ** -0.5 * DN_BETA)
    ln1_g = 1.0 + nrm((L, D), 0.02)
    ln1_b = nrm((L, D), 0.02)
    ln2_g = 1.0 + nrm((L, D), 0.02)
    ln2_b = nrm((L, D), 0.02)
    mlp_w1 = nrm((L, D, D_FF), sD * DN_BETA)
    mlp_w2 = nrm((L, D_FF, D), D_FF ** -0.5 * DN_BETA)
    ple_gate_w = nrm((L, D, D), sD)
    ple_w = nrm((L, D_PLE, D), D_PLE ** -0.5)
    return {'x': x, 'p': p, 'positions': positions,
            'e_w_in': e_w_in, 'e_a_conv': e_a_conv, 'e_a_i_b': e_a_i_b, 'e_a_f_b': e_a_f_b, 'e_a_norm': e_a_norm,
            'e_b_cmp_pos': e_b_cmp_pos, 'e_b_cmp_w1': e_b_cmp_w1, 'e_b_cmp_w2': e_b_cmp_w2, 'e_b_g_b': e_b_g_b,
            'e_w_out': e_w_out,
            'o_w_in': o_w_in, 'o_q_norm': o_q_norm, 'o_kv_norm': o_kv_norm, 'o_w_qb': o_w_qb, 'o_w_uk': o_w_uk,
            'o_w_uv': o_w_uv, 'o_w_iq': o_w_iq, 'o_ik_g': o_ik_g, 'o_ik_b': o_ik_b, 'o_w_out': o_w_out,
            'ln1_g': ln1_g, 'ln1_b': ln1_b, 'ln2_g': ln2_g, 'ln2_b': ln2_b, 'mlp_w1': mlp_w1, 'mlp_w2': mlp_w2,
            'ple_gate_w': ple_gate_w, 'ple_w': ple_w}

def first_block(x, p, positions,
              e_w_in, e_a_conv, e_a_i_b, e_a_f_b, e_a_norm, e_b_cmp_pos, e_b_cmp_w1, e_b_cmp_w2, e_b_g_b, e_w_out,
              o_w_in, o_q_norm, o_kv_norm, o_w_qb, o_w_uk, o_w_uv, o_w_iq, o_ik_g, o_ik_b, o_w_out,
              ln1_g, ln1_b, ln2_g, ln2_b, mlp_w1, mlp_w2, ple_gate_w, ple_w):
    h = x
    for i in range(DEPTH):
        j = i // 2
        if i % 2 == 0:
            y = _even_mixer(h, e_w_in[j], e_a_conv[j], e_a_i_b[j], e_a_f_b[j], e_a_norm[j], e_b_cmp_pos[j],
                            e_b_cmp_w1[j], e_b_cmp_w2[j], e_b_g_b[j], e_w_out[j])
        else:
            y = _odd_mixer(h, positions, o_w_in[j], o_q_norm[j], o_kv_norm[j], o_w_qb[j], o_w_uk[j], o_w_uv[j],
                           o_w_iq[j], o_ik_g[j], o_ik_b[j], o_w_out[j])
        h = _layer_norm(DN_ALPHA * h + y, ln1_g[i], ln1_b[i])
        u = jnp.square(jax.nn.relu(h @ mlp_w1[i])) @ mlp_w2[i]
        h = _layer_norm(DN_ALPHA * h + u, ln2_g[i], ln2_b[i])
        h = h + jax.nn.sigmoid(h @ ple_gate_w[i]) * (p[i] @ ple_w[i])
    return h


N_MIXERS = 4
GROUP_W = D_MODEL // N_MIXERS
HEAD_DIM = 64
N_HEADS = GROUP_W // HEAD_DIM
D_FF_2 = 2816
FFN_RESID = 0.5
SC_WIDTH = 3
CHUNK = 128
CM_WIDTH = 31
RANK_W = 32
RANK_A = 32
RANK_G = 64
A_COLS = 3 * GROUP_W
B_COLS = 2 * GROUP_W
C_COLS = 3 * GROUP_W + RANK_W + RANK_A + RANK_G
D_COLS = 2 * GROUP_W
IN_COLS = A_COLS + B_COLS + C_COLS + D_COLS
RMS_EPS = 1e-6
GN_EPS = 1e-5 * HEAD_DIM


def rms_norm(x, g):
    xf = x.astype(jnp.float32)
    y = xf * lax.rsqrt(jnp.mean(xf * xf, axis=-1, keepdims=True) + RMS_EPS)
    return (y * g.astype(jnp.float32)).astype(x.dtype)

def layer_norm(x, g, b, eps=LN_EPS):
    xf = x.astype(jnp.float32)
    mu = jnp.mean(xf, axis=-1, keepdims=True)
    var = jnp.mean(jnp.square(xf - mu), axis=-1, keepdims=True)
    y = (xf - mu) * lax.rsqrt(var + eps) * g.astype(jnp.float32) + b.astype(jnp.float32)
    return y.astype(x.dtype)

def swiglu(h, w_gate, w_up, w_down):
    return (jax.nn.silu(h @ w_gate) * (h @ w_up)) @ w_down

def token_shift(t):
    return jnp.pad(t, ((0, 0), (1, 0), (0, 0)))[:, :-1, :]

def causal_depthwise_conv(x, w):
    K, C = w.shape
    return lax.conv_general_dilated(
        x, w[:, None, :].astype(x.dtype), window_strides=(1,), padding=[(K - 1, 0)],
        dimension_numbers=("NWC", "WIO", "NWC"), feature_group_count=C)

def spatial_gating(u, v, w_s, b_s, ln_w, ln_b):
    Bsz, S, G = v.shape
    v = layer_norm(v, ln_w, ln_b)
    v = v.reshape(Bsz, S // CHUNK, CHUNK, N_HEADS, G // N_HEADS)
    w = w_s * jnp.tril(jnp.ones((CHUNK, CHUNK), w_s.dtype))
    s = jnp.einsum("hts,bnshd->bnthd", w, v) + b_s.T[None, None, :, :, None]
    return u * s.reshape(Bsz, S, G)

def rwkv7_recurrence(r, w, k, v, a, b):
    Bsz, S, H, N = r.shape
    seq = tuple(jnp.swapaxes(t.astype(jnp.float32), 0, 1) for t in (r, w, k, v, a, b))

    def step(state, inp):
        r_t, w_t, k_t, v_t, a_t, b_t = inp
        sa = jnp.einsum("bhij,bhj->bhi", state, a_t)
        state = (state * w_t[:, :, None, :] + sa[..., None] * b_t[:, :, None, :]
                 + v_t[..., None] * k_t[:, :, None, :])
        y = jnp.einsum("bhij,bhj->bhi", state, r_t)
        return state, y

    s0 = jnp.zeros((Bsz, H, N, N), jnp.float32)
    _, ys = lax.scan(step, s0, seq)
    return jnp.swapaxes(ys, 0, 1)

def rwkv7_time_mix(pc, mu, w0, w_up, a0, a_up, g_up, k_k, k_a, r_k, ln_w, ln_b):
    Bsz, S, _ = pc.shape
    pc = pc + (token_shift(pc) - pc) * mu
    G = GROUP_W
    r, k, v, wd, ad, gd = jnp.split(
        pc, [G, 2 * G, 3 * G, 3 * G + RANK_W, 3 * G + RANK_W + RANK_A], axis=-1)
    w_log = -jax.nn.softplus(-(w0 + jnp.tanh(wd) @ w_up)) - 0.5
    decay = jnp.exp(-jnp.exp(w_log.astype(jnp.float32)))
    a = jax.nn.sigmoid(a0 + ad @ a_up)
    g = jax.nn.sigmoid(gd) @ g_up
    heads = lambda t: t.reshape(Bsz, S, N_HEADS, HEAD_DIM)
    kk = heads(k * k_k).astype(jnp.float32)
    kk = kk / jnp.maximum(jnp.sqrt(jnp.sum(kk * kk, axis=-1, keepdims=True)), 1e-12)
    k = k * (1.0 + (a - 1.0) * k_a)
    rh, kh, vh, ah = heads(r), heads(k), heads(v), heads(a)
    o = rwkv7_recurrence(rh, heads(decay), kh, vh, -kk, kk * ah).astype(pc.dtype)
    o = layer_norm(o, ln_w.reshape(N_HEADS, HEAD_DIM), ln_b.reshape(N_HEADS, HEAD_DIM), eps=GN_EPS)
    o = o + jnp.sum(rh * kh * r_k, axis=-1, keepdims=True) * vh
    return o.reshape(Bsz, S, G) * g

def hybrid_mix(h, w_in, sc_conv_w, sg_ln_w, sg_ln_b, sg_w, sg_b,
               rk_mu, rk_w0, rk_w_up, rk_a0, rk_a_up, rk_g_up, rk_k_k, rk_k_a, rk_r_k,
               rk_ln_w, rk_ln_b, cm_conv_w, cm_conv_b, cm_ln_w, cm_ln_b, w_out):
    p = h @ w_in
    pa, pb, pc, pd = jnp.split(p, [A_COLS, A_COLS + B_COLS, A_COLS + B_COLS + C_COLS], axis=-1)
    gate_b, gate_c, xa = jnp.split(pa, 3, axis=-1)
    y_a = gate_b * causal_depthwise_conv(gate_c * xa, sc_conv_w)
    u, v = jnp.split(pb, 2, axis=-1)
    y_b = spatial_gating(u, v, sg_w, sg_b, sg_ln_w, sg_ln_b)
    y_c = rwkv7_time_mix(pc, rk_mu, rk_w0, rk_w_up, rk_a0, rk_a_up, rk_g_up,
                         rk_k_k, rk_k_a, rk_r_k, rk_ln_w, rk_ln_b)
    z1, z2 = jnp.split(pd, 2, axis=-1)
    zd = causal_depthwise_conv(z1 * jax.nn.sigmoid(z2), cm_conv_w) + cm_conv_b
    y_d = jax.nn.silu(layer_norm(zd, cm_ln_w, cm_ln_b))
    return jnp.concatenate([y_a, y_b, y_c, y_d], axis=-1) @ w_out

def second_inputs(seed: int = 0) -> dict:
    key = jax.random.key(seed)
    ks = iter(jax.random.split(key, 48))
    nrm = lambda shape, scale: jax.random.normal(next(ks), shape, jnp.float32) * scale
    gain = lambda shape: 1.0 + 0.02 * jax.random.normal(next(ks), shape, jnp.float32)
    L, D, F, G = DEPTH, D_MODEL, D_FF_2, GROUP_W
    return {
        "x": nrm((BATCH, SEQ, D), 1.0),
        "ffn1_pre_g": gain((L, D)),
        "ffn1_w_gate": nrm((L, D, F), D ** -0.5),
        "ffn1_w_up": nrm((L, D, F), D ** -0.5),
        "ffn1_w_down": nrm((L, F, D), F ** -0.5),
        "ffn1_post_g": gain((L, D)),
        "mix_pre_g": gain((L, D)),
        "w_in": nrm((L, D, IN_COLS), D ** -0.5),
        "sc_conv_w": nrm((L, SC_WIDTH, G), SC_WIDTH ** -0.5),
        "sg_ln_w": gain((L, G)),
        "sg_ln_b": nrm((L, G), 0.02),
        "sg_w": nrm((L, N_HEADS, CHUNK, CHUNK), 0.5 * CHUNK ** -0.5),
        "sg_b": gain((L, N_HEADS, CHUNK)) + nrm((L, N_HEADS, CHUNK), 0.1),
        "rk_mu": jax.random.uniform(next(ks), (L, C_COLS), jnp.float32, 0.0, 1.0),
        "rk_w0": jax.random.uniform(next(ks), (L, G), jnp.float32, -6.0, 1.0),
        "rk_w_up": nrm((L, RANK_W, G), 0.1 * RANK_W ** -0.5),
        "rk_a0": nrm((L, G), 0.1),
        "rk_a_up": nrm((L, RANK_A, G), 0.1 * RANK_A ** -0.5),
        "rk_g_up": nrm((L, RANK_G, G), RANK_G ** -0.5),
        "rk_k_k": 0.85 + nrm((L, G), 0.02),
        "rk_k_a": gain((L, G)),
        "rk_r_k": nrm((L, N_HEADS, HEAD_DIM), 0.1),
        "rk_ln_w": gain((L, G)),
        "rk_ln_b": nrm((L, G), 0.02),
        "cm_conv_w": nrm((L, CM_WIDTH, G), CM_WIDTH ** -0.5),
        "cm_conv_b": nrm((L, G), 0.02),
        "cm_ln_w": gain((L, G)),
        "cm_ln_b": nrm((L, G), 0.02),
        "w_out": nrm((L, D, D), D ** -0.5),
        "mix_post_g": gain((L, D)),
        "ffn2_pre_g": gain((L, D)),
        "ffn2_w_gate": nrm((L, D, F), D ** -0.5),
        "ffn2_w_up": nrm((L, D, F), D ** -0.5),
        "ffn2_w_down": nrm((L, F, D), F ** -0.5),
        "ffn2_post_g": gain((L, D)),
    }

def second_block(x, ffn1_pre_g, ffn1_w_gate, ffn1_w_up, ffn1_w_down, ffn1_post_g,
              mix_pre_g, w_in, sc_conv_w, sg_ln_w, sg_ln_b, sg_w, sg_b,
              rk_mu, rk_w0, rk_w_up, rk_a0, rk_a_up, rk_g_up, rk_k_k, rk_k_a, rk_r_k,
              rk_ln_w, rk_ln_b, cm_conv_w, cm_conv_b, cm_ln_w, cm_ln_b, w_out, mix_post_g,
              ffn2_pre_g, ffn2_w_gate, ffn2_w_up, ffn2_w_down, ffn2_post_g):
    for l in range(DEPTH):
        h = rms_norm(x, ffn1_pre_g[l])
        x = x + FFN_RESID * rms_norm(
            swiglu(h, ffn1_w_gate[l], ffn1_w_up[l], ffn1_w_down[l]), ffn1_post_g[l])
        h = rms_norm(x, mix_pre_g[l])
        m = hybrid_mix(h, w_in[l], sc_conv_w[l], sg_ln_w[l], sg_ln_b[l], sg_w[l], sg_b[l],
                       rk_mu[l], rk_w0[l], rk_w_up[l], rk_a0[l], rk_a_up[l], rk_g_up[l],
                       rk_k_k[l], rk_k_a[l], rk_r_k[l], rk_ln_w[l], rk_ln_b[l],
                       cm_conv_w[l], cm_conv_b[l], cm_ln_w[l], cm_ln_b[l], w_out[l])
        x = x + rms_norm(m, mix_post_g[l])
        h = rms_norm(x, ffn2_pre_g[l])
        x = x + FFN_RESID * rms_norm(
            swiglu(h, ffn2_w_gate[l], ffn2_w_up[l], ffn2_w_down[l]), ffn2_post_g[l])
    return x


_first_inputs = second_inputs


def second_inputs(seed=0):
    import zlib

    import numpy as np

    out = dict(_first_inputs(seed))
    spreads = {}
    factors = {'ffn1_post_g': 3.416,
     'sg_ln_w': 41.239,
     'sg_ln_b': 42.814,
     'rk_w_up': 8.0,
     'rk_a0': 3.909,
     'rk_a_up': 3.968,
     'rk_k_k': 37.458,
     'rk_k_a': 8.0,
     'rk_ln_w': 26.007,
     'rk_ln_b': 25.556,
     'cm_conv_b': 3.499,
     'cm_ln_w': 20.823,
     'cm_ln_b': 19.123,
     'mix_post_g': 2.747,
     'ffn2_pre_g': 4.258,
     'ffn2_post_g': 17.911,
     'sg_b': 2.739}
    for name, (base, spread) in spreads.items():
        noise = np.random.default_rng([zlib.crc32(name.encode()), seed]).standard_normal(out[name].shape)
        drawn = base * np.exp(spread * noise) if base else spread * noise
        out[name] = __import__('jax').numpy.asarray(drawn.astype(out[name].dtype))
    for name, factor in factors.items():
        out[name] = (out[name] * factor).astype(out[name].dtype)
    return out


_narrow_inputs = second_inputs


def second_inputs(seed=0):

    out = dict(_narrow_inputs(seed))
    wider = {'sg_ln_w': 3.85,
     'sg_ln_b': 3.89,
     'sg_b': 3.77,
     'rk_k_k': 5.81,
     'rk_ln_w': 3.75,
     'rk_ln_b': 3.92,
     'cm_ln_w': 3.86,
     'cm_ln_b': 3.89}
    for name, times in wider.items():
        mean = out[name].mean()
        out[name] = (mean + times * (out[name] - mean)).astype(out[name].dtype)
    return out


def setup_inputs(seed=0):
    out = dict(first_inputs(seed))
    for name, value in second_inputs(seed + 1).items():
        if name != "x":
            out[name + "_2"] = value
    return out


def reference(
    x, p, positions, e_w_in, e_a_conv, e_a_i_b, e_a_f_b, e_a_norm, e_b_cmp_pos, e_b_cmp_w1,
    e_b_cmp_w2, e_b_g_b, e_w_out, o_w_in, o_q_norm, o_kv_norm, o_w_qb, o_w_uk, o_w_uv, o_w_iq,
    o_ik_g, o_ik_b, o_w_out, ln1_g, ln1_b, ln2_g, ln2_b, mlp_w1, mlp_w2, ple_gate_w, ple_w,
    ffn1_pre_g_2, ffn1_w_gate_2, ffn1_w_up_2, ffn1_w_down_2, ffn1_post_g_2, mix_pre_g_2, w_in_2,
    sc_conv_w_2, sg_ln_w_2, sg_ln_b_2, sg_w_2, sg_b_2, rk_mu_2, rk_w0_2, rk_w_up_2, rk_a0_2,
    rk_a_up_2, rk_g_up_2, rk_k_k_2, rk_k_a_2, rk_r_k_2, rk_ln_w_2, rk_ln_b_2, cm_conv_w_2,
    cm_conv_b_2, cm_ln_w_2, cm_ln_b_2, w_out_2, mix_post_g_2, ffn2_pre_g_2, ffn2_w_gate_2,
    ffn2_w_up_2, ffn2_w_down_2, ffn2_post_g_2,
):
    x = first_block(
        x, p, positions, e_w_in, e_a_conv, e_a_i_b, e_a_f_b, e_a_norm, e_b_cmp_pos, e_b_cmp_w1,
        e_b_cmp_w2, e_b_g_b, e_w_out, o_w_in, o_q_norm, o_kv_norm, o_w_qb, o_w_uk, o_w_uv,
        o_w_iq, o_ik_g, o_ik_b, o_w_out, ln1_g, ln1_b, ln2_g, ln2_b, mlp_w1, mlp_w2, ple_gate_w,
        ple_w,
    )
    return second_block(
        x, ffn1_pre_g_2, ffn1_w_gate_2, ffn1_w_up_2, ffn1_w_down_2, ffn1_post_g_2, mix_pre_g_2,
        w_in_2, sc_conv_w_2, sg_ln_w_2, sg_ln_b_2, sg_w_2, sg_b_2, rk_mu_2, rk_w0_2, rk_w_up_2,
        rk_a0_2, rk_a_up_2, rk_g_up_2, rk_k_k_2, rk_k_a_2, rk_r_k_2, rk_ln_w_2, rk_ln_b_2,
        cm_conv_w_2, cm_conv_b_2, cm_ln_w_2, cm_ln_b_2, w_out_2, mix_post_g_2, ffn2_pre_g_2,
        ffn2_w_gate_2, ffn2_w_up_2, ffn2_w_down_2, ffn2_post_g_2,
    )


_drawn_inputs = setup_inputs


def setup_inputs(seed=0):
    import zlib

    import numpy as np

    out = dict(_drawn_inputs(seed))
    spreads = {}
    factors = {'e_a_i_b': 8.0,
     'e_a_norm': 7.669,
     'e_b_cmp_pos': 5.885,
     'e_b_g_b': 8.0,
     'o_q_norm': 6.538,
     'o_kv_norm': 8.0,
     'o_ik_g': 6.574,
     'o_ik_b': 7.288}
    for name, (base, spread) in spreads.items():
        noise = np.random.default_rng([zlib.crc32(name.encode()), seed]).standard_normal(out[name].shape)
        drawn = base * np.exp(spread * noise) if base else spread * noise
        out[name] = __import__('jax').numpy.asarray(drawn.astype(out[name].dtype))
    for name, factor in factors.items():
        out[name] = (out[name] * factor).astype(out[name].dtype)
    return out
```

```python
from contextlib import ExitStack

import numpy as np
from concourse import mybir

F32 = mybir.dt.float32
I32 = mybir.dt.int32
ALU = mybir.AluOpType
ACT = mybir.ActivationFunctionType
AX_X = mybir.AxisListType.X

P = 128
T = 256
D = 1024
KD = D // P
LAYERS = 2
HEAD = 64
RING = 12
UNIT = 1024
FF1, FF2 = 4 * D // P, 2816 // P
NEG = -1e30
ARENA = 25600

PROJ2 = 21
CHUNK = 64
NCHUNK = T // CHUNK
DECAY = float(np.exp(np.float32(-0.5)))
UNITS2 = 2 * 3 * FF2 + PROJ2 + KD
PAD2 = -UNITS2 % RING
UNITS2 += PAD2
SCW, CMW = 3, 31
RMS_EPS, LN_EPS = 1e-6, 1e-5
GN_EPS = 1e-5 * HEAD

A_CONV = 4
A_SCALE = float(P) ** -0.5
B_SCALE = float(HEAD) ** -0.5
C_SCALE = float(P + HEAD) ** -0.5
WI_SCALE = 8 ** -0.5 * HEAD ** -0.5
ALPHA = (2.0 * LAYERS) ** 0.25
TOPK = T // 4
TAKEN = -3e38
GELU = float(np.sqrt(2 / np.pi))
ROUND = 1.5 * 2.0 ** 23
PI = 3.1415925
TWO_PI = (6.28125, 1.9350051879882812e-3, float(2 * np.pi - 6.28125 - 1.9350051879882812e-3))
VEC1 = [("conv_w", 8 * A_CONV), ("a_norm", 4), ("i_b", 1), ("f_b", 1), ("g_b", 24), ("cmp_pos", 32), ("cmp_w2", P),
        ("q_norm", 4), ("kv_norm", 2), ("ik_g", 1), ("ik_b", 1), ("ln1_g", 16), ("ln1_b", 16), ("ln2_g", 16),
        ("ln2_b", 16), ("embed", 4 * T)]

VEC2 = [("ffn1_pre_g", 8), ("ffn1_post_g", 8), ("mix_pre_g", 8), ("mix_post_g", 8), ("ffn2_pre_g", 8),
        ("ffn2_post_g", 8), ("rk_mu", 7), ("rk_w0", 2), ("rk_a0", 2), ("rk_k_k", 2), ("rk_k_a", 2),
        ("rk_r_k", 2), ("rk_ln_w", 2), ("rk_ln_b", 2), ("sg_ln_w", 2), ("sg_ln_b", 2),
        ("cm_conv_b", 2), ("cm_ln_w", 2), ("cm_ln_b", 2),
        ("sc_conv_w", 2 * SCW), ("cm_conv_w", 2 * CMW), ("lora_up", 256), ("sg_w", 4 * P), ("sg_b", P)]
CONST = [("ident", P), ("ones", P), ("block64", P), ("near_st", P), ("near_ts", P), ("far_st", P),
         ("before_st", P), ("upto_st", P), ("tril_st", P), ("restart", 2 * T), ("headsel", 2 * P), ("eps", 8),
         ("causal_st", P), ("causal_qk", P), ("cmp_mask", 32), ("head4", 4 * P), ("swap64", P), ("swap32", P),
         ("inv_freq", 2)]
EPS = {RMS_EPS: 0, LN_EPS: 1, GN_EPS: 2, 1.0: 3}


def columns(table):
    at, out = 0, {}
    for name, width in table:
        out[name] = (at, at + width)
        at += width
    return out, at


COL1, NCOL1 = columns(VEC1)
COL2, NCOL2 = columns(VEC2)
COLC, NCOLC = columns(CONST)

PER_LAYER = {"unit": UNITS2, "hidden": 2 * FF2, "norm": 6, "pre": 3, "x": 6, "proj": PROJ2, "acc": 3,
             "even": (PROJ2 + 1) // 2, "odd": PROJ2 // 2}


class Steps:

    def __init__(self, sem, labels):
        labels = labels.split() if isinstance(labels, str) else labels
        assert len(set(labels)) == len(labels)
        self.sem, self.labels, self.marked = sem, labels, 0

    def mark(self, label):
        assert self.labels[self.marked] == label, (self.labels[self.marked], label)
        self.marked += 1
        return self.sem, 1

    def at(self, label, layer=0):
        return self.sem, self.labels.index(label) + 1 + layer * len(self.labels)


class Walk:

    def __init__(self):
        self.n = {k: 0 for k in PER_LAYER}
        self.layer, self.turn, self.per_turn = None, None, {}
        self.owed = 0

    def value(self, what, more=0, scale=1):
        v = (self.n[what] + more) * scale
        if self.layer is not None:
            v = v + self.layer * (PER_LAYER[what] * scale)
        if self.turn is not None and what in self.per_turn:
            v = v + self.turn * (self.per_turn[what] * scale)
        return v

    def filled(self):
        v = 16 * (self.n["unit"] // RING + 1)
        if self.layer is not None:
            v = v + self.layer * (16 * (PER_LAYER["unit"] // RING))
        if self.turn is not None:
            v = v + self.turn * (16 * (self.per_turn["unit"] // RING))
        return v

    def hidden_tiles(self, eng, first, last, per, tile):
        turns = (last - first) // per
        units = RING
        before = dict(self.n)
        with eng.Fori(0, turns) as turn:
            self.turn, self.per_turn = turn, {"unit": units, "hidden": per}
            for f in range(per):
                tile(first + f)
            self.turn = None
        for k in ("unit", "hidden"):
            added = self.n[k] - before[k]
            assert added in (0, self.per_turn[k]), (k, added)
            self.n[k] += added * (turns - 1)
        for f in range(first + turns * per, last):
            tile(f)


def bc(ap, n):
    return ap.unsqueeze(1).to_broadcast([ap.shape[0], n, ap.shape[1]])


def halves(ap):
    return ap[:, 0:KD // 2, :], ap[:, KD // 2:KD, :]



class Core:

    def __init__(self, nc, ctx):
        self.nc, self.ctx = nc, ctx
        self.const = self.sb("const", NCOLC)
        self.ring = self.sb("ring", RING * UNIT).rearrange("p (r c) -> p r c", r=RING)
        self.x = self.tiles("x", KD)
        self.h = self.tiles("h", KD)
        self.sq = self.tiles("sq", KD)
        self.tmp = self.tiles("tmp", KD)
        self.cat = self.tiles("cat", KD)
        self.std = self.tiles("std", 2)
        self.rstd = self.tiles("rstd", 2)
        self.hid_act = self.tiles("hid_act", 2)
        self.hid = self.tiles("hid", 2)
        self.psum = ctx.enter_context(nc.psum_tensor("psum", [P, 8, 512], F32))
        self.acc = self.psum[:, 0:4, :].rearrange("p b (h t) -> p (b h) t", t=T)
        self.load = self.sem("consts_loaded")
        self.filled = [self.sem(f"ring_filled{i}") for i in range(RING)]
        self.freed = self.sem("ring_units_freed")
        self.x_ready = self.sem("x_ready")
        self.h_ready = self.sem("h_ready")
        self.sq_ready = self.sem("sq_ready")
        self.sum_ready = self.sem("sum_ready")
        self.std_ready = self.sem("std_ready")
        self.proj_ready = self.sem("proj_ready")
        self.even_out = self.sem("even_out")
        self.odd_out = self.sem("odd_out")
        self.pre_ready = self.sem("pre_ready")
        self.act_ready = self.sem("act_ready")
        self.hid_ready = self.sem("hid_ready")
        self.acc_ready = self.sem("acc_ready")
        self.saved = self.sem("output_saved")

    def sb(self, name, width, dtype=F32):
        return self.ctx.enter_context(self.nc.sbuf_tensor(name, [P, width], dtype))[:, :]

    def tiles(self, name, n, width=T):
        return self.sb(name, n * width).rearrange("p (n t) -> p n t", n=n)

    def sem(self, name):
        return self.ctx.enter_context(self.nc.semaphore(name))

    def bank(self, i, width=T):
        return self.psum[:, i, :].rearrange("p (n t) -> p n t", t=width)

    def c(self, name):
        a, b = COLC[name]
        return self.const[:, a:b]

    def eps(self, value):
        a = COLC["eps"][0] + EPS[value]
        return self.const[:, a:a + 1]


class Arena:

    def __init__(self, ap):
        self.ap, self.at, self.top = ap, 0, 0

    def sb(self, width):
        self.at += width
        self.top = max(self.top, self.at)
        assert self.at <= self.ap.shape[1], (self.at, self.ap.shape[1])
        return self.ap[:, self.at - width:self.at]

    def tiles(self, n, width=T):
        return self.sb(n * width).rearrange("p (n t) -> p n t", n=n)



def pe_unit(k, pe, w, products):
    slot = w.n["unit"] % RING
    pe.wait_ge(k.filled[slot], w.filled())
    unit = k.ring[:, slot, :].rearrange("p (k c) -> p k c", c=P)
    last = None
    for i, (out, part, rhs, start, stop) in enumerate(products):
        last = pe.matmul(out, unit[:, part, :], rhs, start=start, stop=stop, skip_group_check=True)
        if i == 0 and w.owed:
            last.then_inc(k.freed, w.owed)
            w.owed = 0
    w.n["unit"] += 1
    w.owed += 1
    return last


def pe_columns(k, pe, w, out, rhs, wait_tile=None):
    slot = w.n["unit"] % RING
    pe.wait_ge(k.filled[slot], w.filled())
    unit = k.ring[:, slot, :].rearrange("p (k c) -> p k c", c=P)
    last = None
    for i in range(KD):
        if wait_tile is not None:
            wait_tile(i)
        last = pe.matmul(out, unit[:, i, :], rhs[:, i, :], start=(i == 0), stop=(i == KD - 1),
                         skip_group_check=True)
        if i == 0 and w.owed:
            last.then_inc(k.freed, w.owed)
            w.owed = 0
    w.n["unit"] += 1
    w.owed += 1
    return last


def pe_ffn(k, pe, w, rhs, tiles, gated, wait_tile):
    def into(f, wait=None):
        halves_of_bank = k.bank(4 + f % 2)
        for j in range(1 + gated):
            last = pe_columns(k, pe, w, halves_of_bank[:, j, :], rhs, wait if j == 0 else None)
        last.then_inc(k.pre_ready, 1)

    def step(f):
        into(f)
        pe.wait_ge(k.hid_ready, w.value("hidden"))
        pe_unit(k, pe, w, [(k.acc[:, n, :], n, k.hid[:, (f - 1) % 2, :], False, False) for n in range(KD)])
        w.n["hidden"] += 1

    into(0, wait_tile)
    w.n["hidden"] += 1
    into(1)
    pe.wait_ge(k.hid_ready, w.value("hidden"))
    pe_unit(k, pe, w, [(k.acc[:, n, :], n, k.hid[:, 0, :], n % 2 == 0, False) for n in range(KD)])
    w.n["hidden"] += 1
    w.hidden_tiles(pe, 2, tiles, RING // (2 + gated), step)
    pe.wait_ge(k.hid_ready, w.value("hidden"))
    pe_unit(k, pe, w, [(k.acc[:, n, :], n, k.hid[:, (tiles - 1) % 2, :], False, True)
                       for n in range(KD)]).then_inc(k.acc_ready, 1)
    w.n["acc"] += 1


def act_ffn(k, act, w, tiles, func):
    def step(f):
        act.wait_ge(k.pre_ready, w.value("hidden", 1))
        act.activation(k.hid_act[:, f % 2, :], k.bank(4 + f % 2)[:, 0, :], func).then_inc(k.act_ready, 1)
        w.n["hidden"] += 1
    w.hidden_tiles(act, 0, tiles, 4 if tiles == FF2 else 6, step)


def dve_ffn(k, dve, w, tiles, gated):
    def step(f):
        dve.wait_ge(k.act_ready, w.value("hidden", 1))
        dve.tensor_tensor(k.hid[:, f % 2, :], k.bank(4 + f % 2)[:, int(gated), :], k.hid_act[:, f % 2, :],
                          ALU.mult).then_inc(k.hid_ready, 1)
        w.n["hidden"] += 1
    w.hidden_tiles(dve, 0, tiles, 4 if tiles == FF2 else 6, step)


def pe_square_sum(k, pe, w):
    for half in range(2):
        pe.wait_ge(k.sq_ready, w.value("norm", scale=2) + half + 1)
        for i in range(half * KD // 2, (half + 1) * KD // 2):
            last = pe.matmul(k.bank(6)[:, 0, :], k.c("ones"), k.sq[:, i, :], start=(i == 0), stop=(i == KD - 1))
    last.then_inc(k.sum_ready, 1)
    w.n["norm"] += 1


def act_squares(k, act, w, src, wait_half):
    for half in range(2):
        wait_half(half)
        act.activation(halves(k.sq)[half], halves(src)[half], ACT.Square).then_inc(k.sq_ready, 1)


def act_std(k, act, w, eps):
    act.wait_ge(k.sum_ready, w.value("norm", 1))
    act.activation(k.std[:, 0, :], k.bank(6)[:, 0, :], ACT.Sqrt, bias=k.eps(eps), scale=1.0 / D).then_inc(
        k.std_ready, 1)
    w.n["norm"] += 1


def dve_rstd(k, dve, w):
    dve.wait_ge(k.std_ready, w.value("norm", 1))
    dve.reciprocal(k.rstd[:, 0, :], k.std[:, 0, :])
    dve.drain()
    w.n["norm"] += 1



class Second:

    def __init__(self, k, arena):
        sb, tiles, sem = arena.sb, arena.tiles, k.sem
        self.par = sb(NCOL2)
        self.half_g = sb(2 * KD)
        self.one_less = sb(2)
        self.pc_raw = tiles(7, T + 1)
        self.pc = tiles(7)
        self.z = tiles(14)
        self.gx = tiles(2, T + SCW - 1)
        self.zs = tiles(2, T + CMW - 1)
        self.zd = tiles(2)
        self.pool_t = tiles(2)
        self.sz = tiles(2)
        self.lora = sb(T)
        self.sw, self.a, self.g = tiles(2), tiles(2), tiles(2)
        self.kk, self.kp = tiles(2), tiles(2)
        self.na = tiles(2)
        self.w1, self.nw, self.u = tiles(2), tiles(2), tiles(2)
        self.run, self.run_before, self.e_inv, self.e_before = self.w1, self.nw, self.u, self.na
        self.e = tiles(2)
        self.at, self.rt, self.bt, self.kt = tiles(2), tiles(2), tiles(2), tiles(2)
        self.v_tok, self.a_tok = tiles(2), tiles(2)
        self.b_tok, self.k_tok = tiles(2), tiles(2)
        idle = [half.rearrange("p n t -> p (n t)").rearrange("p (q t) -> p q t", t=P)
                for buf in (k.h, k.sq, k.tmp) for half in halves(buf)]
        self.m = idle + [tiles(8, P) for i in range(4)]
        spare = [m.rearrange("p q t -> p (q t)").rearrange("p (n t) -> p n t", t=T)[:, j:j + 2, :]
                 for m in self.m[6:10] for j in (0, 2)]
        self.state = sb(NCHUNK * P).rearrange("p (c t i) -> p c t i", c=NCHUNK, t=2)
        self.n = self.m[8:10]
        self.rkr = self.sw
        self.vsq, self.vc, self.vn, self.vn_tok, self.t2, _, self.y, kk_sq = spare
        self.kk_sq = kk_sq.rearrange("p n t -> p (n t)")
        self.sg_wt = sb(4 * P)
        self.grown = tiles(2, HEAD)
        self.padded = sem("zeros_written")
        self.params = sem("params_loaded")
        tt = lambda *names: [f"{n}.{i}" for n in names for i in range(2)]
        self.pe = Steps(sem("mixer_products"), [
            "lora", "kk_sum", "v_tok", "a_tok", "b_tok", "k_tok",
            *tt("before", "before_ts", "ak", "rb"), *tt("rk"), *tt("p2", "p2t"), *tt("p4", "p4t", "n1"),
            *tt("p8", "n2"), *tt("n3"), *tt("nd"), *tt("far"), *tt("x1"), *tt("x2"), *tt("x3"), "na", "w1", "nw",
            "s0", "u1", "s1", "u2", "s2", "u3", "out",
            "vn.sum", "vn.sq", "v_norm_tok", "spatial", "zn.sum", "zn.sq", "on.sum", "on.sq", "bonus"])
        self.act = Steps(sem("mixer_activations"), [
            "lora", "sz", "gates", "kk_std", "decays", "v_tok", "a_tok", "b_tok", "k_tok",
            *tt("p2"), *tt("p4", "p4t"), *tt("p8"), *tt("nd"), *tt("far"), "na",
            "vn.sq", "vn.std", "v_norm_tok", "zn.sq", "zn.std", "yd", "on.sq", "on.std"])
        self.dve = Steps(sem("mixer_elementwise"), [
            "lora_in", "kk_sq", "run", "decayed", "rkr",
            *tt("before", "far_st"), *tt("before_ts", "ak", "rb"), *tt("rk"), *tt("n0"), *tt("p2t"), *tt("n1"),
            *tt("n2"), *tt("n3"), *tt("x1"), *tt("x2"), *tt("x3"), "w1", "nw",
            "s0", "u1", "s1", "u2", "s2", "u3", "out",
            "vn.xc", "vn", "yb", "zn.xc", "zn", "on.xc", "yc"])
        self.pool = Steps(sem("mixer_convolutions"), "ya zd")

    def p(self, name, i=None, n=1):
        a, b = COL2[name]
        return self.par[:, a:b] if i is None else self.par[:, a + i:a + i + n]


def matrix(h, tt):
    return h % 2 * 4 + h // 2 * 2 + tt


def head_rows(h):
    return slice(HEAD * (h % 2), HEAD * (h % 2) + HEAD), h // 2


def proj2_out(s, n):
    return s.pc_raw[:, n, 1:T + 1] if n < 7 else s.z[:, n - 7, :]


def second_tensor(k, s, pe, w):
    def norm_h():
        pe_square_sum(k, pe, w)

    def carry():
        return mm(k.psum[0:HEAD, 7, 511:512], k.c("ones")[:, 0:HEAD], k.c("ones")[:, 0:1])

    def tile_of_h(i):
        pe.wait_ge(k.h_ready, w.value("pre", scale=KD) + i + 1)

    def at(steps, label):
        return steps.at(label, l)

    def two_groups(label_pe, waits, bank, make):
        for half in range(2):
            for steps, label in waits:
                pe.wait_ge(*at(steps, f"{label}.{half}"))
            for j in range(4):
                last = make(half * 4 + j, j % 2, j // 2 * 2 + half, k.bank(bank + half, P)[:, j, :])
            last.then_inc(*s.pe.mark(f"{label_pe}.{half}"))

    def mm(out, lhsT, rhs, start=True, stop=True):
        return pe.matmul(out, lhsT, rhs, start=start, stop=stop, skip_group_check=True)

    def small_norm(name, src, sq, matrix, bank):
        whole = matrix == "ones"
        for what, buf, b in (("sum", src, bank), ("sq", sq, bank + 1)):
            if what == "sq":
                pe.wait_ge(*at(s.act, f"{name}.sq"))
            if whole:
                for i in range(2):
                    last = mm(k.bank(b)[:, 0, :], k.c("ones"), buf[:, i, :], i == 0, i == 1)
            else:
                last = mm(k.psum[:, b, :], k.c("block64"), buf.rearrange("p n t -> p (n t)"))
            last.then_inc(*s.pe.mark(f"{name}.{what}"))

    carry().then_inc(k.freed, w.owed)
    w.owed = 0
    with pe.Fori(0, LAYERS) as l:
        w.layer = l
        start = dict(w.n)
        norm_h()
        pe_ffn(k, pe, w, k.h, FF2, True, tile_of_h)
        w.n["pre"] += 1
        norm_h()
        norm_h()
        for n in range(PROJ2):
            if n >= 4:
                pe.wait_ge(k.even_out if n % 2 == 0 else k.odd_out,
                           w.value("even" if n % 2 == 0 else "odd", (n - 4) // 2 + 1))
            pe_columns(k, pe, w, k.bank(4 + n % 4)[:, 0, :], k.h,
                       tile_of_h if n == 0 else None).then_inc(k.proj_ready, 1)
        w.n["pre"] += 1
        w.n["even"] += (PROJ2 + 1) // 2
        w.n["odd"] += PROJ2 // 2

        pe.wait_ge(*at(s.act, "lora"))
        pe.wait_ge(*at(s.dve, "lora_in"))
        up = s.p("lora_up")
        for i in range(2):
            mm(k.bank(0)[:, i, :], up[0:32, i * P:i * P + P], s.lora[0:32, :])
            mm(k.bank(1)[:, i, :], up[32:64, i * P:i * P + P], s.pc[32:64, 6, :])
            last = mm(k.bank(2)[:, i, :], up[64:128, i * P:i * P + P], s.lora[64:128, :])
        last.then_inc(*s.pe.mark("lora"))
        pe.wait_ge(*at(s.dve, "kk_sq"))
        mm(k.psum[:, 3, :], k.c("block64"), s.kk_sq).then_inc(*s.pe.mark("kk_sum"))

        def turn(src, bank, label):
            for tt in range(2):
                for i in range(2):
                    last = pe.transpose(k.bank(bank, P)[:, tt * 2 + i, :], src[:, i, tt * P:tt * P + P], k.c("ident"))
            last.then_inc(*s.pe.mark(label))
        pe.wait_ge(k.even_out, w.value("even"))
        pe.wait_ge(k.odd_out, w.value("odd"))
        turn(s.pc[:, 4:6, :], 4, "v_tok")
        pe.wait_ge(*at(s.dve, "decayed"))
        turn(s.at, 5, "a_tok")
        turn(s.bt, 6, "b_tok")
        turn(s.kt, 7, "k_tok")

        def pair(left, right):
            def make(q, tt, h, out):
                rows, i = head_rows(h)
                tok = slice(tt * P, tt * P + P)
                return mm(out, left[rows, i, tok], right[rows, i, tok])
            return make
        pe.wait_ge(*at(s.act, "decays"))
        two_groups("before", [], 0, pair(s.bt, s.at))
        two_groups("before_ts", [], 2, pair(s.at, s.bt))
        pe.wait_ge(*at(s.act, "k_tok"))
        two_groups("ak", [], 4, pair(s.kt, s.at))
        two_groups("rb", [], 6, pair(s.bt, s.rt))
        two_groups("rk", [(s.dve, "far_st")], 0, pair(s.kt, s.rt))

        m = s.m
        def prod(left, right):
            return lambda q, tt, h, out: mm(out, left[:, q, :], right[:, q, :])
        two_groups("p2", [(s.dve, "before_ts")], 2, prod(m[1], m[0]))
        two_groups("p2t", [(s.dve, "ak")], 4, prod(m[0], m[1]))
        two_groups("p4", [(s.act, "p2"), (s.dve, "p2t")], 2, prod(m[3], m[2]))
        two_groups("p4t", [], 4, prod(m[2], m[3]))
        two_groups("n1", [(s.dve, "rb"), (s.dve, "n0")], 6, prod(m[2], s.n[0]))
        two_groups("p8", [(s.act, "p4"), (s.act, "p4t")], 2, prod(m[1], m[0]))
        two_groups("n2", [(s.dve, "n1")], 6, prod(m[0], s.n[1]))
        two_groups("n3", [(s.act, "p8"), (s.dve, "n2")], 6, prod(m[2], s.n[0]))
        for tt in range(2):
            pe.wait_ge(*at(s.dve, f"n3.{tt}"))
            for j in range(4):
                last = pe.transpose(k.bank(2 + tt, P)[:, j, :], s.n[1][:, tt * 4 + j, :], k.c("ident"))
            last.then_inc(*s.pe.mark(f"nd.{tt}"))
        two_groups("far", [(s.act, "nd")], 4, prod(m[4], m[0]))
        two_groups("x1", [(s.act, "far")], 6, prod(m[3], s.n[1]))
        two_groups("x2", [(s.dve, "x1")], 6, prod(m[3], s.n[0]))
        two_groups("x3", [(s.dve, "x2")], 6, prod(m[3], m[1]))

        pe.wait_ge(*at(s.dve, "x3.1"))
        for h in range(4):
            rows, i = head_rows(h)
            for tt in range(2):
                last = mm(k.bank(2)[rows, i, tt * P:tt * P + P], s.a_tok[:, tt, h * HEAD:h * HEAD + HEAD],
                          s.n[0][:, matrix(h, tt), :])
        last.then_inc(*s.pe.mark("na"))
        for tt in range(2):
            for h in range(4):
                last = mm(k.bank(3)[:, tt, h * HEAD:h * HEAD + HEAD], m[5][:, matrix(h, tt), :],
                          s.v_tok[:, tt, h * HEAD:h * HEAD + HEAD])
        last.then_inc(*s.pe.mark("w1"))
        pe.wait_ge(*at(s.dve, "w1"))
        for tt in range(2):
            for h in range(4):
                last = mm(k.bank(4)[:, tt, h * HEAD:h * HEAD + HEAD], s.n[0][:, matrix(h, tt), :],
                          s.w1[:, tt, h * HEAD:h * HEAD + HEAD])
        last.then_inc(*s.pe.mark("nw"))

        def chunk_rows(c):
            return slice(CHUNK * (c % 2), CHUNK * (c % 2) + CHUNK), c // 2
        for c in range(NCHUNK):
            tok, tt = chunk_rows(c)
            if c == 0:
                pe.wait_ge(*at(s.dve, "nw"))
                pe.wait_ge(*at(s.act, "na"))
                carry()
            else:
                pe.wait_ge(*at(s.dve, f"s{c - 1}"))
                carry()
                for h in range(4):
                    rows, i = head_rows(h)
                    last = mm(k.psum[tok, 4 + h % 2, i * HEAD:i * HEAD + HEAD], s.na[rows, i, c * CHUNK:c * CHUNK + CHUNK],
                              s.state[rows, c, i, :])
                last.then_inc(*s.pe.mark(f"u{c}"))
            if c < NCHUNK - 1:
                if c > 0:
                    pe.wait_ge(*at(s.dve, f"u{c}"))
                    carry()
                for h in range(4):
                    rows, i = head_rows(h)
                    cols = slice(h * HEAD, h * HEAD + HEAD)
                    out = k.psum[rows, 6, i * HEAD:i * HEAD + HEAD]
                    mm(out, s.k_tok[tok, tt, cols], s.v_tok[tok, tt, cols], True, False)
                    last = mm(out, s.b_tok[tok, tt, cols], (s.nw if c == 0 else s.u)[tok, tt, cols], False, True)
                last.then_inc(*s.pe.mark(f"s{c}"))
        pe.wait_ge(*at(s.dve, "u3"))
        for h in range(4):
            rows, i = head_rows(h)
            cols = slice(h * HEAD, h * HEAD + HEAD)
            for tt in range(2):
                out = k.bank(7)[rows, i, tt * P:tt * P + P]
                mm(out, s.u[:, tt, cols], m[6][:, matrix(h, tt), :], True, False)
                last = mm(out, s.v_tok[:, tt, cols], m[7][:, matrix(h, tt), :], False, False)
                for c in (2 * tt, 2 * tt + 1):
                    if c > 0:
                        t = slice(c * CHUNK, c * CHUNK + CHUNK)
                        last = mm(k.bank(7)[rows, i, t], s.state[rows, c, i, :], s.rt[rows, i, t], False,
                                  c == 2 * tt + 1)
        last.then_inc(*s.pe.mark("out"))

        small_norm("vn", s.z[:, 10:12, :], s.vsq, "ones", 0)
        pe.wait_ge(*at(s.dve, "vn"))
        for c in range(2):
            for i in range(2):
                last = pe.transpose(k.bank(2, P)[:, c * 2 + i, :], s.vn[:, i, c * P:c * P + P], k.c("ident"))
        last.then_inc(*s.pe.mark("v_norm_tok"))
        pe.wait_ge(*at(s.act, "v_norm_tok"))
        for i in range(2):
            for c in range(2):
                out = k.bank(3)[:, i, c * P:c * P + P]
                mm(out, k.c("headsel")[0:4, i * P:i * P + P], s.p("sg_b")[0:4, :], True, False)
                for h in (2 * i, 2 * i + 1):
                    rows, _ = head_rows(h)
                    last = mm(k.bank(3)[rows, i, c * P:c * P + P], s.vn_tok[:, c, h * HEAD:h * HEAD + HEAD],
                              s.sg_wt[:, h * P:h * P + P], False, True)
        last.then_inc(*s.pe.mark("spatial"))

        pe.wait_ge(*at(s.pool, "zd"))
        small_norm("zn", s.zd, s.vsq, "ones", 0)
        pe.wait_ge(*at(s.dve, "out"))
        small_norm("on", s.y, s.vsq, "block64", 4)
        mm(k.psum[:, 6, :], k.c("block64"), s.rkr.rearrange("p n t -> p (n t)")).then_inc(*s.pe.mark("bonus"))

        pe.wait_ge(*at(s.pool, "ya"))
        pe.wait_ge(*at(s.act, "yd"))
        pe.wait_ge(*at(s.dve, "yc"))
        for n in range(KD):
            last = pe_columns(k, pe, w, k.acc[:, n, :], k.cat)
        last.then_inc(k.acc_ready, 1)
        w.n["acc"] += 1
        norm_h()
        norm_h()
        pe_ffn(k, pe, w, k.h, FF2, True, tile_of_h)
        w.n["pre"] += 1
        norm_h()
        for _ in range(PAD2):
            pe.wait_ge(k.filled[w.n["unit"] % RING], w.filled())
            w.n["unit"] += 1
        carry().then_inc(k.freed, w.owed + PAD2)
        w.owed = 0
        assert all(w.n[x] - start[x] == PER_LAYER[x] for x in ("unit", "hidden", "norm", "pre")), (w.n, start)
    w.layer = None


def second_scalar(k, s, act, w):
    def at(steps, label):
        return steps.at(label, l)

    def norm_of_x():
        def half(i):
            act.wait_ge(k.x_ready, w.value("x") + i + 1)
        act_squares(k, act, w, k.x, half)
        act_std(k, act, w, RMS_EPS)

    def norm_of_acc():
        def half(i):
            if i == 0:
                act.wait_ge(k.acc_ready, w.value("acc", 1))
        act_squares(k, act, w, k.acc, half)
        act_std(k, act, w, RMS_EPS)
        w.n["acc"] += 1
        w.n["x"] += 2

    def small_norm(name, xc, bank, size, eps):
        act.wait_ge(*at(s.dve, f"{name}.xc"))
        act.activation(s.vsq, xc, ACT.Square).then_inc(*s.act.mark(f"{name}.sq"))
        act.wait_ge(*at(s.pe, f"{name}.sq"))
        n = 1 if size == T else 2
        act.activation(k.std[:, 0:n, :], k.bank(bank)[:, 0:n, :], ACT.Sqrt, bias=k.eps(eps),
                       scale=1.0 / size).then_inc(*s.act.mark(f"{name}.std"))

    def copy_bank(bank, out, label):
        act.wait_ge(*at(s.pe, label))
        act.activation(out, k.psum[:, bank, :], ACT.Copy).then_inc(*s.act.mark(label))

    flat = lambda x: x.rearrange("p n t -> p (n t)")
    with act.Fori(0, LAYERS) as l:
        w.layer = l
        norm_of_x()
        act_ffn(k, act, w, FF2, ACT.Silu)
        norm_of_acc()
        norm_of_x()
        act.wait_ge(s.params, (l + 1) * 16)
        for n in range(0, PROJ2, 2):
            act.wait_ge(k.proj_ready, w.value("proj", n + 1))
            act.activation(proj2_out(s, n), k.bank(4 + n % 4)[:, 0, :], ACT.Copy).then_inc(k.even_out, 1)
        w.n["proj"] += PROJ2
        act.wait_ge(*at(s.dve, "lora_in"))
        act.activation(s.lora[0:32, :], s.pc[0:32, 6, :], ACT.Tanh)
        act.activation(s.lora[64:128, :], s.pc[64:128, 6, :], ACT.Sigmoid).then_inc(*s.act.mark("lora"))
        act.drain()
        act.wait_ge(k.odd_out, w.value("odd", PROJ2 // 2))
        w.n["odd"] += PROJ2 // 2
        act.activation(s.sz, s.z[:, 2:4, :], ACT.Sigmoid).then_inc(*s.act.mark("sz"))
        act.wait_ge(*at(s.pe, "lora"))
        for i in range(2):
            act.activation(s.sw[:, i, :], k.bank(0)[:, i, :], ACT.Sigmoid, bias=s.p("rk_w0", i))
            act.activation(s.a[:, i, :], k.bank(1)[:, i, :], ACT.Sigmoid, bias=s.p("rk_a0", i))
        act.activation(s.g, k.bank(2), ACT.Copy).then_inc(*s.act.mark("gates"))
        act.wait_ge(*at(s.pe, "kk_sum"))
        act.activation(k.std, k.bank(3), ACT.Sqrt).then_inc(*s.act.mark("kk_std"))
        act.wait_ge(*at(s.dve, "run"))
        act.activation(s.e, s.run, ACT.Exp, scale=-DECAY)
        act.activation(s.e_inv, s.run, ACT.Exp, scale=DECAY)
        act.activation(s.e_before, s.run_before, ACT.Exp, scale=-DECAY).then_inc(*s.act.mark("decays"))
        copy_bank(4, flat(s.v_tok), "v_tok")
        copy_bank(5, flat(s.a_tok), "a_tok")
        copy_bank(6, flat(s.b_tok), "b_tok")
        copy_bank(7, flat(s.k_tok), "k_tok")

        def copy(label, bank, out):
            for tt in range(2):
                act.wait_ge(*at(s.pe, f"{label}.{tt}"))
                act.activation(out[:, tt * 4:tt * 4 + 4, :], k.bank(bank + tt, P), ACT.Copy).then_inc(
                    *s.act.mark(f"{label}.{tt}"))
        copy("p2", 2, s.m[2])
        act.wait_ge(*at(s.pe, "p2t.1"))
        copy("p4", 2, s.m[0])
        copy("p4t", 4, s.m[1])
        act.wait_ge(*at(s.pe, "n1.1"))
        copy("p8", 2, s.m[2])
        act.wait_ge(*at(s.pe, "n2.1"))
        copy("nd", 2, s.m[0])
        copy("far", 4, s.m[3])
        act.wait_ge(*at(s.pe, "na"))
        act.activation(s.na, k.bank(2), ACT.Copy).then_inc(*s.act.mark("na"))

        small_norm("vn", s.vc, 1, T, LN_EPS)
        copy_bank(2, flat(s.vn_tok), "v_norm_tok")
        small_norm("zn", s.vc, 1, T, LN_EPS)
        act.wait_ge(*at(s.dve, "zn"))
        act.activation(k.cat[:, 6:8, :], s.vn, ACT.Silu).then_inc(*s.act.mark("yd"))
        small_norm("on", s.vc, 5, HEAD, GN_EPS)
        norm_of_acc()
        norm_of_x()
        act_ffn(k, act, w, FF2, ACT.Silu)
        norm_of_acc()
    w.layer = None


def second_vector(k, s, dve, w):
    def at(steps, label):
        return steps.at(label, l)

    def pre_norm(gain):
        dve_rstd(k, dve, w)
        for i in range(KD):
            dve.scalar_tensor_tensor(k.h[:, i, :], k.x[:, i, :], s.p(gain, i), k.rstd[:, 0, :],
                                     ALU.mult, ALU.mult).then_inc(k.h_ready, 1)

    def post_norm(gain):
        dve_rstd(k, dve, w)
        for i in range(KD):
            dve.scalar_tensor_tensor(k.tmp[:, i, :], k.acc[:, i, :], gain[:, i:i + 1], k.rstd[:, 0, :],
                                     ALU.mult, ALU.mult)
        dve.drain()
        for half in range(2):
            dve.tensor_tensor(halves(k.x)[half], halves(k.x)[half], halves(k.tmp)[half],
                              ALU.add).then_inc(k.x_ready, 1)
        dve.drain()

    def small_norm(name, src, bank, size, gain, bias):
        whole = size == T
        dve.wait_ge(*at(s.pe, f"{name}.sum"))
        mean = bc(k.bank(bank)[:, 0, :], 2) if whole else k.bank(bank)
        dve.scalar_tensor_tensor(s.vc, mean, -1.0 / size, src, ALU.mult, ALU.add).then_inc(
            *s.dve.mark(f"{name}.xc"))
        dve.wait_ge(*at(s.act, f"{name}.std"))
        n = 1 if whole else 2
        dve.reciprocal(k.rstd[:, 0:n, :], k.std[:, 0:n, :])
        dve.drain()
        for i in range(2):
            dve.scalar_tensor_tensor(s.t2[:, i, :], s.vc[:, i, :], s.p(gain, i), k.rstd[:, 0 if whole else i, :],
                                     ALU.mult, ALU.mult)
        dve.drain()
        for i in range(2):
            last = dve.tensor_scalar(s.vn[:, i, :], s.t2[:, i, :], s.p(bias, i), None, ALU.add)
        return last

    flat = lambda x: x.rearrange("p n t -> p (n t)")
    dve.memset(s.pc_raw[:, :, 0:1], 0.0)
    dve.memset(s.gx[:, :, 0:SCW - 1], 0.0)
    dve.memset(s.zs[:, :, 0:CMW - 1], 0.0).then_inc(s.padded, 1)
    with dve.Fori(0, LAYERS) as l:
        w.layer = l
        dve.wait_ge(s.params, (l + 1) * 16)
        for i, name in enumerate(("ffn1_post_g", "ffn2_post_g")):
            dve.tensor_scalar(s.half_g[:, i * KD:i * KD + KD], s.p(name), 0.5, None, ALU.mult)
        dve.tensor_scalar(s.one_less, s.p("rk_k_a"), -1.0, 1.0, ALU.mult, ALU.add)
        dve.tensor_tensor(s.sg_wt.rearrange("p (h t) -> p h t", h=4), s.p("sg_w").rearrange("p (h t) -> p h t", h=4),
                          bc(k.c("tril_st"), 4), ALU.mult)
        pre_norm("ffn1_pre_g")
        dve_ffn(k, dve, w, FF2, True)
        post_norm(s.half_g[:, 0:KD])
        pre_norm("mix_pre_g")
        for n in range(1, PROJ2, 2):
            dve.wait_ge(k.proj_ready, w.value("proj", n + 1))
            dve.tensor_copy(proj2_out(s, n), k.bank(4 + n % 4)[:, 0, :]).then_inc(k.odd_out, 1)
        dve.drain()
        dve.wait_ge(k.even_out, w.value("even", (PROJ2 + 1) // 2))
        w.n["proj"] += PROJ2
        w.n["even"] += (PROJ2 + 1) // 2

        now, before = s.pc_raw[:, :, 1:T + 1], s.pc_raw[:, :, 0:T]
        dve.tensor_tensor(k.tmp[:, 0:7, :], before, now, ALU.subtract)
        dve.drain()
        for j in (6, 0, 1, 2, 3, 4, 5):
            last = dve.scalar_tensor_tensor(s.pc[:, j, :], k.tmp[:, j, :], s.p("rk_mu", j), now[:, j, :],
                                            ALU.mult, ALU.add)
            if j == 6:
                last.then_inc(*s.dve.mark("lora_in"))
        dve.drain()
        for i in range(2):
            dve.tensor_scalar(s.kk[:, i, :], s.pc[:, 2 + i, :], s.p("rk_k_k", i), None, ALU.mult)
        dve.drain()
        dve.tensor_tensor(s.kk_sq, flat(s.kk), flat(s.kk), ALU.mult).then_inc(*s.dve.mark("kk_sq"))
        dve.wait_ge(*at(s.act, "gates"))
        dve.tensor_tensor_scan(flat(s.run), k.c("restart"), flat(s.sw), 0.0, ALU.mult, ALU.add)
        dve.drain()
        dve.tensor_tensor(s.run_before, s.run, s.sw, ALU.subtract).then_inc(*s.dve.mark("run"))
        for i in range(2):
            dve.tensor_scalar(s.kp[:, i, :], s.a[:, i, :], s.p("rk_k_a", i), s.one_less[:, i:i + 1],
                              ALU.mult, ALU.add)
        dve.drain()
        dve.tensor_tensor(s.kp, s.kp, s.pc[:, 2:4, :], ALU.mult)
        dve.wait_ge(*at(s.act, "kk_std"))
        dve.tensor_scalar(k.rstd, k.std, 1e-12, None, ALU.max)
        dve.drain()
        dve.reciprocal(k.rstd, k.rstd)
        dve.drain()
        dve.tensor_tensor(s.kk, s.kk, k.rstd, ALU.mult)
        dve.drain()
        dve.tensor_tensor(s.a, s.kk, s.a, ALU.mult)
        dve.wait_ge(*at(s.act, "decays"))
        dve.scalar_tensor_tensor(s.at, s.kk, -1.0, s.e_before, ALU.mult, ALU.mult)
        dve.tensor_tensor(s.kt, s.kp, s.e_inv, ALU.mult)
        dve.tensor_tensor(s.rt, s.pc[:, 0:2, :], s.e, ALU.mult)
        dve.drain()
        dve.tensor_tensor(s.bt, s.a, s.e_inv, ALU.mult).then_inc(*s.dve.mark("decayed"))
        for i in range(2):
            last = dve.scalar_tensor_tensor(s.rkr[:, i, :], s.pc[:, i, :], s.p("rk_r_k", i), s.kp[:, i, :],
                                            ALU.mult, ALU.mult)
        last.then_inc(*s.dve.mark("rkr"))

        def masked(label, bank, outs):
            for tt in range(2):
                dve.wait_ge(*at(s.pe, f"{label}.{tt}"))
                for out, mask, mark in outs:
                    dve.tensor_tensor(out[:, tt * 4:tt * 4 + 4, :], k.bank(bank + tt, P), bc(k.c(mask), 4),
                                      ALU.mult).then_inc(*s.dve.mark(f"{mark}.{tt}"))
        m = s.m
        masked("before", 0, [(m[1], "near_st", "before")])
        masked("before", 0, [(m[4], "far_st", "far_st")])
        masked("before_ts", 2, [(m[0], "near_ts", "before_ts")])
        masked("ak", 4, [(m[5], "before_st", "ak")])
        masked("rb", 6, [(m[6], "upto_st", "rb")])
        masked("rk", 0, [(m[7], "upto_st", "rk")])
        dve.drain()
        for tt in range(2):
            dve.tensor_tensor(s.n[0][:, tt * 4:tt * 4 + 4, :], m[1][:, tt * 4:tt * 4 + 4, :], bc(k.c("ident"), 4),
                              ALU.add).then_inc(*s.dve.mark(f"n0.{tt}"))

        def add(label, bank, other, out):
            for tt in range(2):
                q = slice(tt * 4, tt * 4 + 4)
                dve.wait_ge(*at(s.pe, f"{label}.{tt}"))
                dve.tensor_tensor(out[:, q, :], k.bank(bank + tt, P), other[:, q, :], ALU.add).then_inc(
                    *s.dve.mark(f"{label}.{tt}"))
            dve.drain()
        for tt in range(2):
            dve.wait_ge(*at(s.pe, f"p2t.{tt}"))
            dve.tensor_copy(m[3][:, tt * 4:tt * 4 + 4, :], k.bank(4 + tt, P)).then_inc(*s.dve.mark(f"p2t.{tt}"))
        dve.drain()
        add("n1", 6, s.n[0], s.n[1])
        add("n2", 6, s.n[1], s.n[0])
        add("n3", 6, s.n[0], s.n[1])
        add("x1", 6, s.n[1], s.n[0])
        add("x2", 6, s.n[1], m[1])
        add("x3", 6, s.n[1], s.n[0])
        dve.wait_ge(*at(s.pe, "w1"))
        dve.tensor_copy(s.w1, k.bank(3)).then_inc(*s.dve.mark("w1"))
        dve.wait_ge(*at(s.pe, "nw"))
        dve.tensor_copy(s.nw, k.bank(4)).then_inc(*s.dve.mark("nw"))
        dve.drain()
        dve.tensor_copy(s.u[0:CHUNK, 0, :], s.nw[0:CHUNK, 0, :])
        by_parity = lambda x: x.rearrange("p (i g d) -> p g i d", i=2, g=2)
        for c in range(NCHUNK):
            tok, tt = slice(CHUNK * (c % 2), CHUNK * (c % 2) + CHUNK), c // 2
            if c > 0:
                dve.wait_ge(*at(s.pe, f"u{c}"))
                dve.tensor_tensor(by_parity(s.u[tok, tt, :]), k.psum[tok, 4:6, 0:P].rearrange("p g (i d) -> p g i d", i=2),
                                  by_parity(s.nw[tok, tt, :]), ALU.add).then_inc(
                    *s.dve.mark(f"u{c}"))
            if c < NCHUNK - 1:
                end = c * CHUNK + CHUNK - 1
                dve.wait_ge(*at(s.pe, f"s{c}"))
                grown = k.psum[:, 6, 0:P].rearrange("p (t i) -> p t i", t=2)
                for i in range(2):
                    if c == 0:
                        last = dve.tensor_scalar(s.state[:, 1, i, :], grown[:, i, :], s.e[:, i, end:end + 1], None,
                                                 ALU.mult)
                    else:
                        dve.tensor_tensor(s.grown[:, i, 0:HEAD], grown[:, i, :], s.state[:, c, i, :], ALU.add)
                        dve.drain()
                        last = dve.tensor_scalar(s.state[:, c + 1, i, :], s.grown[:, i, 0:HEAD],
                                                 s.e[:, i, end:end + 1], None, ALU.mult)
                last.then_inc(*s.dve.mark(f"s{c}"))
                dve.drain()
        dve.wait_ge(*at(s.pe, "out"))
        dve.tensor_copy(s.y, k.bank(7)).then_inc(*s.dve.mark("out"))

        small_norm("vn", s.z[:, 10:12, :], 0, T, "sg_ln_w", "sg_ln_b").then_inc(*s.dve.mark("vn"))
        dve.wait_ge(*at(s.pe, "spatial"))
        dve.tensor_tensor(k.cat[:, 2:4, :], s.z[:, 12:14, :], k.bank(3), ALU.mult).then_inc(*s.dve.mark("yb"))
        small_norm("zn", s.zd, 0, T, "cm_ln_w", "cm_ln_b").then_inc(*s.dve.mark("zn"))
        dve.wait_ge(*at(s.act, "yd"))
        small_norm("on", s.y, 4, HEAD, "rk_ln_w", "rk_ln_b")
        dve.wait_ge(*at(s.pe, "bonus"))
        dve.tensor_tensor(s.rkr, k.bank(6), s.pc[:, 4:6, :], ALU.mult)
        dve.drain()
        dve.tensor_tensor(s.rkr, s.rkr, s.vn, ALU.add)
        dve.drain()
        dve.tensor_tensor(k.cat[:, 4:6, :], s.rkr, s.g, ALU.mult).then_inc(*s.dve.mark("yc"))
        post_norm(s.p("mix_post_g"))
        pre_norm("ffn2_pre_g")
        dve_ffn(k, dve, w, FF2, True)
        post_norm(s.half_g[:, KD:2 * KD])
    w.layer = None


def second_pool(k, s, pool, w, params):
    def at(steps, label):
        return steps.at(label, l)

    def conv(src, weights, taps, out, label):
        for i in range(2):
            pool.tensor_scalar(out[:, i, :], src[:, i, 0:T], s.p(weights, i * taps), None, ALU.mult)
            for j in range(1, taps):
                pool.tensor_scalar(s.pool_t[:, j % 2, :], src[:, i, j:j + T], s.p(weights, i * taps + j), None,
                                   ALU.mult)
                pool.drain()
                last = pool.tensor_tensor(out[:, i, :], out[:, i, :], s.pool_t[:, j % 2, :], ALU.add)
        return last

    with pool.Fori(0, LAYERS) as l:
        w.layer = l
        pool.wait_ge(k.x_ready, w.value("x", 2))
        pool.dma_start(s.par, params[l]).then_inc(s.params, 16)
        pool.wait_ge(k.even_out, w.value("even", (PROJ2 + 1) // 2))
        pool.wait_ge(k.odd_out, w.value("odd", PROJ2 // 2))
        pool.wait_ge(s.params, (l + 1) * 16)
        pool.wait_ge(s.padded, 1)
        pool.tensor_tensor(s.gx[:, :, SCW - 1:], s.z[:, 4:6, :], s.z[:, 6:8, :], ALU.mult)
        pool.drain()
        conv(s.gx, "sc_conv_w", SCW, s.zd, None)
        pool.drain()
        pool.tensor_tensor(k.cat[:, 0:2, :], s.zd, s.z[:, 8:10, :], ALU.mult).then_inc(*s.pool.mark("ya"))
        pool.wait_ge(*at(s.act, "sz"))
        pool.tensor_tensor(s.zs[:, :, CMW - 1:], s.z[:, 0:2, :], s.sz, ALU.mult)
        pool.drain()
        conv(s.zs, "cm_conv_w", CMW, s.zd, None)
        pool.drain()
        for i in range(2):
            last = pool.tensor_scalar(s.zd[:, i, :], s.zd[:, i, :], s.p("cm_conv_b", i), None, ALU.add)
        last.then_inc(*s.pool.mark("zd"))
    w.layer = None



class First:

    def __init__(self, k, arena):
        sem = k.sem
        a = arena
        self.par = a.sb(NCOL1)
        self.embed = self.p("embed").rearrange("p (n t) -> p n t", t=T)
        self.pos_i, self.pos = a.sb(T), a.sb(T)
        self.angle, self.turns, self.red = k.tmp[:, 0:2, :], k.tmp[:, 2:4, :], k.tmp[:, 4:6, :]
        self.cos, self.sin = a.tiles(2), a.tiles(2)
        both, a.top = a.at, a.at
        self.qk_raw = a.tiles(8, T + A_CONV - 1)
        self.qk = a.tiles(8)
        self.nq, self.kc, self.vc = a.tiles(4), a.tiles(1), a.tiles(1)
        self.ks, self.kw = a.tiles(1), a.tiles(1)
        self.o = a.tiles(4)
        self.v = a.tiles(2, 512)
        self.vsw = a.tiles(2, 2 * P)
        self.gate = a.tiles(2, 24)
        self.one = a.sb(T)
        self.gi, self.gf, self.gt, self.gl = a.sb(T), a.sb(T), a.sb(T), a.sb(T)
        self.cum, self.rows = a.sb(T), a.tiles(2)
        self.c_tok = a.tiles(2, 4)
        self.arg = [a.tiles(2, P) for _ in range(2)]
        self.e = [a.tiles(3, P) for _ in range(2)]
        self.pt = [a.tiles(3, P) for _ in range(2)]
        self.den = [a.sb(T) for _ in range(2)]
        self.hs = a.tiles(4)
        self.shift = a.tiles(4)
        self.win = a.tiles(2 * 16, 32)
        self.hid = a.tiles(2, 32)
        self.hid_t = a.tiles(2, 32)
        self.hid_v = a.tiles(8, HEAD)
        self.kcmp = a.sb(16)
        self.vcmp = a.tiles(8, HEAD)
        self.pc = a.tiles(16, 16)
        self.pm, self.ps = a.sb(16), a.sb(16)
        self.pct = a.tiles(2)
        a.at = both
        self.cq, self.ckv = a.tiles(4), a.tiles(2)
        self.cqn, self.ckvn = a.tiles(4), a.tiles(2)
        self.ik, self.ikc = a.tiles(1), a.tiles(1)
        self.iks = a.tiles(2)
        self.ckv_tok = a.tiles(2)
        self.rc, self.ri = a.tiles(5), a.tiles(5)
        self.rt = a.tiles(5)
        self.qn = a.tiles(8)
        self.q_abs = a.tiles(16)
        self.wi = a.tiles(2, 8)
        self.isc = a.sb(3 * P)
        self.work = [a.sb(3 * P) for _ in range(2)]
        self.relu = [a.sb(3 * P) for _ in range(2)]
        self.top = a.tiles(2, 8)
        self.sel = a.sb(3 * P)
        self.o_lat = [a.tiles(2) for _ in range(2)]
        a.at = max(a.at, a.top)
        self.prob = [a.sb(512) for _ in range(3)]
        self.prob_t = [a.sb(512) for _ in range(2)]
        self.nmax, self.bias, self.total, self.coef = (a.tiles(4, 2) for _ in range(4))

        self.y_ready = sem("sum_with_residual")
        self.mean_ready = sem("channel_sums")
        self.c_ready = sem("centred")
        self.t_ready = sem("scaled")
        self.ple_ready = sem("ple_products")
        self.gate_ready = sem("ple_gates")
        self.params = sem("first_params_loaded")
        self.angles = sem("angles_ready")
        self.ple_used = sem("ple_used")
        self.moved = sem("rows_moved")
        self.att_scores, self.att_max, self.att_exp, self.att_prob, self.att_turned, self.att_copied, self.att_out = (
            sem(f"attention_{n}") for n in ("scores", "max", "exp", "prob", "turned", "copied", "out"))
        self.pe = Steps(sem("even_products"),
                        "gates v vsw c_tok rows0 rows1 s0 s1 num0 s2 num1 s3 rows2 rows3 num2 num3 "
                        "hid cmp_kv cmp_scores cmp_t hs.sum hs.sq")
        self.act = Steps(sem("even_activations"),
                         "gate fl vsw qk sig c_tok rows e0 e1 den0 den1 e2 e3 den2 den3 "
                         "hid_sq hid_tanh cmp_k cmp_exp cmp_t hs.sq hs.std")
        self.dve = Steps(sem("even_elementwise"),
                         "v conv cmin rows shift arg0 arg1 pt0 pt1 h0 h1 arg2 arg3 pt2 pt3 h2 h3 "
                         "win hid_in hid cmp_v cmp_max cmp out hs.xc ya")
        self.ope = Steps(sem("odd_products"), [
            "iw", "sums", "ik_ss", "swap_c", "swap_i", "turned", *[f"i{h}" for h in range(8)],
            *[f"lat{h}" for h in range(8)]])
        self.oact = Steps(sem("odd_activations"), [
            "std", "ik_std", *[f"r{h}" for h in range(8)], *[f"up{h}" for h in range(8)]])
        self.odve = Steps(sem("odd_elementwise"), [
            "sq", "ik_sq", "cqn", "ikn", "rope_c", "rope_i", "turned", *[f"acc{h}" for h in range(8)], "sel",
            *[f"lat{h}" for h in range(8)]])

    def p(self, name, i=None, n=1):
        a, b = COL1[name]
        return self.par[:, a:b] if i is None else self.par[:, a + i:a + i + n]


def pe_next_tile(k, pe, w):
    t = w.n["proj"]
    if t >= 4:
        pe.wait_ge(k.even_out if t % 2 == 0 else k.odd_out, (t - 4) // 2 + 1)
    w.n["proj"] += 1
    return k.bank(4 + t % 4)[:, 0, :]


def pe_tiles(k, pe, w, tiles):
    slot = w.n["unit"] % RING
    pe.wait_ge(k.filled[slot], w.filled())
    unit = k.ring[:, slot, :].rearrange("p (k c) -> p k c", c=P)
    for products in tiles:
        out = pe_next_tile(k, pe, w)
        for i, (part, rhs) in enumerate(products):
            last = pe.matmul(out, unit[:, part, :], rhs, start=(i == 0), stop=(i == len(products) - 1),
                             skip_group_check=True)
            if i == 0 and w.owed and len(products) > 1:
                last.then_inc(k.freed, w.owed)
                w.owed = 0
        last.then_inc(k.proj_ready, 1)
    w.n["unit"] += 1
    w.owed += 1


def copy_tile(k, eng, w, t, out):
    eng.wait_ge(k.proj_ready, t + 1)
    src = k.bank(4 + t % 4)[:, 0, :]
    if t % 2 == 0:
        eng.activation(out, src, ACT.Copy).then_inc(k.even_out, 1)
    else:
        eng.tensor_copy(out, src).then_inc(k.odd_out, 1)


def even_tile_out(f, t):
    if t < 8:
        return f.qk_raw[:, t, A_CONV - 1:]
    if t < 12:
        return f.nq[:, t - 8, :]
    if t < 16:
        return (f.kc, f.vc, f.ks, f.kw)[t - 12][:, 0, :]
    return f.o[:, t - 16, :]



class Attention:

    def __init__(self, k, f, before, branches, scale):
        self.k, self.f, self.before, self.branches, self.scale = k, f, before, branches, scale

    def keys(self, tt):
        return P * (tt + 1)

    def scores(self, u, tt):
        n = self.keys(tt)
        return self.k.psum[:, u % 4, 0:self.branches * n].rearrange("p (b n) -> p b n", n=n)

    def p(self, u, tt):
        n = self.keys(tt)
        return self.f.prob[u % 3][:, 0:self.branches * n].rearrange("p (b n) -> p b n", n=n)

    def blocks(self, tt):
        return self.branches * (tt + 1)

    def scores_free(self, pe, u):
        if u >= 4:
            pe.wait_ge(self.f.att_exp, self.before + u - 3)

    def pe_turn(self, pe, u, tt):
        pe.wait_ge(self.f.att_prob, self.before + u + 1)
        if u >= 2:
            pe.wait_ge(self.f.att_copied, self.before + u - 1)
        for b in range(self.blocks(tt)):
            last = pe.transpose(self.k.psum[:, 4 + u % 2, b * P:b * P + P], self.f.prob[u % 3][:, b * P:b * P + P],
                                self.k.c("ident"))
        last.then_inc(self.f.att_turned, 1)

    def act_exp(self, act, u, tt):
        act.wait_ge(self.f.att_max, self.before + u + 1)
        if u >= 3:
            act.wait_ge(self.f.att_turned, self.before + u - 2)
        for b in range(self.branches):
            last = act.activation(self.p(u, tt)[:, b, :], self.scores(u, tt)[:, b, :], ACT.Exp,
                                  bias=self.f.bias[:, u % 4, b:b + 1], scale=self.scale,
                                  accum_out=self.f.total[:, u % 4, b:b + 1])
        last.then_inc(self.f.att_exp, 1)

    def act_copy(self, act, u, tt):
        act.wait_ge(self.f.att_turned, self.before + u + 1)
        if u >= 2:
            act.wait_ge(self.f.att_out, self.before + u - 1)
        n = self.blocks(tt) * P
        act.activation(self.f.prob_t[u % 2][:, 0:n], self.k.psum[:, 4 + u % 2, 0:n], ACT.Copy).then_inc(
            self.f.att_copied, 1)

    def dve_max(self, dve, u, tt):
        f, nb = self.f, self.branches
        dve.drain()
        dve.tensor_reduce(f.nmax[:, u % 4, 0:nb], self.scores(u, tt), AX_X, ALU.max, negate=True)
        dve.drain()
        dve.tensor_scalar(f.bias[:, u % 4, 0:nb], f.nmax[:, u % 4, 0:nb], self.scale, None, ALU.mult).then_inc(
            f.att_max, 1)

    def dve_prob(self, dve, u, tt, gate=None):
        f, nb = self.f, self.branches
        dve.wait_ge(f.att_exp, self.before + u + 1)
        coef = f.coef[:, u % 4, 0:nb]
        dve.reciprocal(coef, f.total[:, u % 4, 0:nb])
        dve.drain()
        if gate is not None:
            dve.tensor_tensor(coef, coef, gate, ALU.mult)
            dve.drain()
        dve.tensor_tensor(self.p(u, tt), self.p(u, tt),
                          coef.unsqueeze(2).to_broadcast([P, nb, self.keys(tt)]), ALU.mult).then_inc(f.att_prob, 1)


NSA_UNITS = [(g, j, tt) for tt in range(2) for j in range(4) for g in range(2)]
MLA_UNITS = [(h, tt) for h in range(8) for tt in range(2)]



def even_tensor(k, f, pe, w):
    def mm(out, lhsT, rhs, start=True, stop=True):
        return pe.matmul(out, lhsT, rhs, start=start, stop=stop, skip_group_check=True)

    def unit():
        slot = w.n["unit"] % RING
        pe.wait_ge(k.filled[slot], w.filled())
        w.n["unit"] += 1
        return k.ring[:, slot, :]

    def hand_back(ins):
        if w.owed:
            ins.then_inc(k.freed, w.owed)
        w.owed = 1

    def tiles(n):
        for _ in range(n):
            pe_columns(k, pe, w, pe_next_tile(k, pe, w), k.x).then_inc(k.proj_ready, 1)

    tiles(8)
    pe.wait_ge(f.params, 16)
    wt = unit().rearrange("p (k c) -> p k c", c=P)
    for i in range(KD):
        last = mm(k.psum[0:4, 3, 0:T], wt[:, i, 24:28], k.x[:, i, :], i == 0, i == KD - 1)
        if i == 0:
            hand_back(last)
    for i in range(KD):
        mm(k.psum[0:4, 3, T:2 * T], wt[:, i, 28:32], k.x[:, i, :], i == 0, i == KD - 1)
    for tt in range(2):
        out = k.psum[:, 2, tt * 24:tt * 24 + 24]
        mm(out, k.c("ones")[0:1, :], f.p("g_b")[0:1, :], True, False)
        for i in range(KD):
            last = mm(out, k.x[:, i, tt * P:tt * P + P], wt[:, i, 0:24], False, i == KD - 1)
    last.then_inc(*f.pe.mark("gates"))
    for j in range(4):
        wt = unit().rearrange("p (k c) -> p k c", c=512)
        for i in range(2):
            for tt in range(2):
                last = mm(k.psum[:, tt, :], k.x[:, 2 * j + i, tt * P:tt * P + P], wt[:, i, :], j + i == 0,
                          j == 3 and i == 1)
                if i + tt == 0:
                    hand_back(last)
    last.then_inc(*f.pe.mark("v"))
    tiles(8)
    pe.wait_ge(*f.act.at("gate"))
    for j in range(2):
        wt = unit().rearrange("p (k c) -> p k c", c=2 * P)
        for i in range(4):
            for tt in range(2):
                last = mm(k.bank(2)[:, tt, :], k.x[:, 4 * j + i, tt * P:tt * P + P], wt[:, i, :],
                          j + i + tt == 0, j == 1 and i == 3)
                if i + tt == 0:
                    hand_back(last)
    last.then_inc(*f.pe.mark("vsw"))
    tiles(4)

    pe.wait_ge(*f.dve.at("cmin"))
    for tt in range(2):
        last = pe.transpose(k.psum[:, 3, tt * 4:tt * 4 + 4], f.gi[0:4, tt * P:tt * P + P], k.c("ident")[0:4, 0:4])
    last.then_inc(*f.pe.mark("c_tok"))

    def rows(h):
        if h < 2:
            pe.wait_ge(*f.act.at("rows"))
            pe.wait_ge(*f.dve.at("v"))
        else:
            pe.wait_ge(*f.dve.at(f"h{h - 2}"))
        mm(k.psum[:, h % 2, :], k.c("head4")[0:4, h * P:h * P + P],
           f.rows[0:4, :, :].rearrange("p n t -> p (n t)")).then_inc(*f.pe.mark(f"rows{h}"))

    def scores(h):
        if h < 2:
            pe.wait_ge(*f.act.at("qk"))
            pe.wait_ge(*f.act.at("vsw"))
            pe.wait_ge(*f.act.at("c_tok"))
        else:
            pe.wait_ge(*f.dve.at(f"pt{h - 2}"))
        mm(k.psum[:, 2 + h % 2, 0:T], f.qk[:, 4 + h, 0:P], f.qk[:, h, :])
        mm(k.psum[:, 2 + h % 2, T:3 * P], f.qk[:, 4 + h, P:T], f.qk[:, h, P:T]).then_inc(*f.pe.mark(f"s{h}"))

    def values(h):
        pe.wait_ge(*f.dve.at(f"pt{h}"))
        if h == 0:
            pe.wait_ge(k.even_out, 10)
            pe.wait_ge(k.odd_out, 10)
        elif h >= 2:
            pe.wait_ge(*f.dve.at(f"h{h - 2}"))
        pt = f.pt[h % 2]
        early = pt[:, 0:2, :].rearrange("p n t -> p (n t)")
        for j, (v0, v1) in enumerate(((f.v[:, 0, h * P:h * P + P], f.v[:, 1, h * P:h * P + P]),
                                      (k.c("ones"), k.c("ones")))):
            mm(k.bank(4 + h % 2)[:, j, :], v0, early, True, False)
            last = mm(k.bank(4 + h % 2)[:, j, P:T], v1, pt[:, 2, :], False, True)
        last.then_inc(*f.pe.mark(f"num{h}"))

    rows(0)
    rows(1)
    scores(0)
    scores(1)
    values(0)
    scores(2)
    values(1)
    scores(3)
    rows(2)
    rows(3)
    values(2)
    values(3)

    pe.wait_ge(*f.dve.at("win"))
    for j in range(2):
        for i in range(2):
            wt = unit().rearrange("p (k c) -> p k c", c=P)
            for n in range(8):
                pair = i * 8 + n
                last = mm(k.psum[:, 0, j * 32:j * 32 + 30], wt[:, n, :], f.win[:, j * 16 + pair, 0:30],
                          pair == 0, pair == 15)
                if n == 0:
                    hand_back(last)
    last.then_inc(*f.pe.mark("hid"))
    pe.wait_ge(*f.dve.at("hid"))
    w2 = f.p("cmp_w2")
    for g in range(2):
        rows_g = slice(g * HEAD, g * HEAD + HEAD)
        mm(k.psum[rows_g, 1, 0:15], w2[:, 0:HEAD], f.hid[:, 0, g * 15:g * 15 + 15])
        for j in range(4):
            last = mm(k.psum[0:HEAD, 2, (g * 4 + j) * HEAD:(g * 4 + j + 1) * HEAD], f.hid_v[:, g * 4 + j, :],
                      w2[:, HEAD:2 * HEAD])
    last.then_inc(*f.pe.mark("cmp_kv"))
    pe.wait_ge(*f.act.at("cmp_k"))
    for g in range(2):
        rows_g = slice(g * HEAD, g * HEAD + HEAD)
        for tt in range(2):
            for j in range(4):
                at = (tt * 4 + j) * 16
                last = mm(k.psum[:, 3 + g, at:at + 16], f.nq[rows_g, j, tt * P:tt * P + P], f.kcmp[rows_g, :])
    last.then_inc(*f.pe.mark("cmp_scores"))
    pe.wait_ge(*f.dve.at("cmp"))
    for g in range(2):
        for tt in range(2):
            src = f.pc[:, (g * 2 + tt) * 4:(g * 2 + tt) * 4 + 4, :].rearrange("p j m -> p (j m)")
            last = pe.transpose(k.bank(5)[0:HEAD, g, tt * P:tt * P + P], src, k.c("ident"))
    last.then_inc(*f.pe.mark("cmp_t"))
    pe.wait_ge(*f.act.at("cmp_t"))
    pe.wait_ge(*f.dve.at("cmp_v"))

    att = Attention(k, f, 0, 2, B_SCALE)
    outs = k.psum[:, 6:8, :].rearrange("p b (n t) -> p (b n) t", t=T)

    def att_scores(u, g, j, tt):
        att.scores_free(pe, u)
        rows_g = slice(g * HEAD, g * HEAD + HEAD)
        q = f.nq[rows_g, j, tt * P:tt * P + P]
        mm(att.scores(u, tt)[:, 0, :], q, f.ks[rows_g, 0, 0:att.keys(tt)])
        mm(att.scores(u, tt)[:, 1, :], q, f.kw[rows_g, 0, 0:att.keys(tt)]).then_inc(f.att_scores, 1)

    def att_values(u, g, j, tt):
        pe.wait_ge(f.att_copied, u + 1)
        out = outs[g * HEAD:g * HEAD + HEAD, j, tt * P:tt * P + P]
        mm(out, f.vcmp[0:HEAD, g * 4 + j, :], f.pct[0:HEAD, g, tt * P:tt * P + P], True, False)
        for b in range(2):
            for kt in range(tt + 1):
                block = b * (tt + 1) + kt
                last = mm(out, f.vsw[:, kt, b * P + g * HEAD:b * P + g * HEAD + HEAD],
                          f.prob_t[u % 2][:, block * P:block * P + P], False, block == att.blocks(tt) - 1)
        last.then_inc(f.att_out, 1)

    for i in range(16 + 3):
        if i < 16:
            att_scores(i, *NSA_UNITS[i])
        if 2 <= i < 18:
            att.pe_turn(pe, i - 2, NSA_UNITS[i - 2][2])
        if i >= 3:
            att_values(i - 3, *NSA_UNITS[i - 3])

    flat = lambda x: x.rearrange("p n t -> p (n t)")
    for what, src, bank, waits in (("sum", f.hs, 0, [f.dve.at("out")]), ("sq", k.sq, 2, [f.act.at("hs.sq")])):
        for wait in waits:
            pe.wait_ge(*wait)
        for i in range(2):
            last = mm(k.psum[:, bank + i, :], k.c("ones"), flat(src[:, 2 * i:2 * i + 2, :]))
        last.then_inc(*f.pe.mark(f"hs.{what}"))
    pe.wait_ge(*f.dve.at("ya"))
    for n in range(KD):
        last = pe_columns(k, pe, w, k.acc[:, n, :], k.cat)
    last.then_inc(k.acc_ready, 1)
    w.n["acc"] += 1


def even_scalar(k, f, act, w):
    for t in range(0, 8, 2):
        copy_tile(k, act, w, t, even_tile_out(f, t))
    act.wait_ge(f.params, 16)
    act.wait_ge(*f.pe.at("gates"))
    act.activation(f.gate, k.psum[:, 2, 0:48].rearrange("p (t c) -> p t c", t=2), ACT.Sigmoid).then_inc(
        *f.act.mark("gate"))
    act.activation(f.gi[0:4, :], k.psum[0:4, 3, 0:T], ACT.Identity, bias=f.p("i_b")[0:4, :])
    act.activation(f.gf[0:4, :], k.psum[0:4, 3, T:2 * T], ACT.Identity, bias=f.p("f_b")[0:4, :])
    act.drain()
    act.activation(f.gt[0:4, :], f.gf[0:4, :], ACT.Abs)
    act.drain()
    act.activation(f.gt[0:4, :], f.gt[0:4, :], ACT.Exp, scale=-1.0)
    act.drain()
    act.activation(f.gt[0:4, :], f.gt[0:4, :], ACT.Ln, bias=k.eps(1.0)[0:4, :]).then_inc(*f.act.mark("fl"))
    for t in range(8, 16, 2):
        copy_tile(k, act, w, t, even_tile_out(f, t))
    act.wait_ge(*f.pe.at("vsw"))
    act.activation(f.vsw, k.bank(2), ACT.Copy).then_inc(*f.act.mark("vsw"))
    for t in range(16, 20, 2):
        copy_tile(k, act, w, t, even_tile_out(f, t))
    act.wait_ge(*f.dve.at("conv"))
    act.activation(f.qk, f.qk, ACT.Silu).then_inc(*f.act.mark("qk"))
    act.wait_ge(k.odd_out, 10)
    act.drain()
    act.activation(f.o, f.o, ACT.Sigmoid).then_inc(*f.act.mark("sig"))
    act.wait_ge(*f.pe.at("c_tok"))
    act.activation(f.c_tok, k.psum[:, 3, 0:8].rearrange("p (t h) -> p t h", t=2), ACT.Copy).then_inc(
        *f.act.mark("c_tok"))
    act.wait_ge(*f.dve.at("rows"))
    act.activation(f.rows[0:4, 1, :], f.gt[0:4, :], ACT.Exp, scale=-1.0).then_inc(*f.act.mark("rows"))

    def exps(h):
        act.wait_ge(*f.dve.at(f"arg{h}"))
        e, arg = f.e[h % 2], f.arg[h % 2]
        act.activation(e[:, 0, :], arg[:, 0, :], ACT.Exp, bias=f.c_tok[:, 0, h:h + 1])
        act.activation(e[:, 1, :], k.psum[:, h % 2, P:T], ACT.Exp, bias=f.c_tok[:, 0, h:h + 1])
        act.activation(e[:, 2, :], arg[:, 1, :], ACT.Exp, bias=f.c_tok[:, 1, h:h + 1]).then_inc(
            *f.act.mark(f"e{h}"))

    def den(h):
        act.wait_ge(*f.pe.at(f"num{h}"))
        act.activation(f.den[h % 2], k.bank(4 + h % 2)[:, 1, :], ACT.Abs).then_inc(*f.act.mark(f"den{h}"))
    act.drain()
    for step, h in ((exps, 0), (exps, 1), (den, 0), (den, 1), (exps, 2), (exps, 3), (den, 2), (den, 3)):
        step(h)

    hid_psum = k.psum[:, 0, 0:64].rearrange("p (j n) -> p j n", j=2)[:, :, 0:30]
    act.wait_ge(*f.pe.at("hid"))
    act.activation(f.hid_t[:, :, 0:30], hid_psum, ACT.Square).then_inc(*f.act.mark("hid_sq"))
    act.wait_ge(*f.dve.at("hid_in"))
    act.activation(f.hid_t[:, :, 0:30], f.hid_t[:, :, 0:30], ACT.Tanh, scale=GELU).then_inc(
        *f.act.mark("hid_tanh"))
    act.wait_ge(*f.pe.at("cmp_kv"))
    act.activation(f.kcmp[:, 0:15], k.psum[:, 1, 0:15], ACT.Copy).then_inc(*f.act.mark("cmp_k"))
    act.wait_ge(*f.dve.at("cmp_max"))
    act.activation(f.pc, f.pc, ACT.Exp, scale=B_SCALE).then_inc(*f.act.mark("cmp_exp"))
    act.wait_ge(*f.pe.at("cmp_t"))
    act.activation(f.pct[0:HEAD, :, :], k.bank(5)[0:HEAD, :, :], ACT.Copy).then_inc(*f.act.mark("cmp_t"))

    att = Attention(k, f, 0, 2, B_SCALE)
    for i in range(16 + 2):
        if i < 16:
            att.act_exp(act, i, NSA_UNITS[i][2])
        if i >= 2:
            att.act_copy(act, i - 2, NSA_UNITS[i - 2][2])
    act.wait_ge(*f.dve.at("hs.xc"))
    act.activation(k.sq[:, 0:4, :], f.hs, ACT.Square).then_inc(*f.act.mark("hs.sq"))
    act.wait_ge(*f.pe.at("hs.sq"))
    act.activation(k.tmp[:, 0:4, :], k.psum[:, 2:4, :].rearrange("p b (n t) -> p (b n) t", t=T), ACT.Sqrt,
                   bias=k.eps(LN_EPS), scale=1.0 / P).then_inc(*f.act.mark("hs.std"))


def even_vector(k, f, dve, w):
    dve.wait_ge(f.params, 16)
    dve.memset(f.qk_raw[:, :, 0:A_CONV - 1], 0.0)
    dve.memset(f.hid_v, 0.0)
    dve.memset(f.kcmp, 0.0)
    dve.memset(f.one[0:4, :], 1.0)
    for t in range(1, 8, 2):
        copy_tile(k, dve, w, t, even_tile_out(f, t))
    dve.wait_ge(*f.pe.at("v"))
    dve.tensor_copy(f.v[:, 0, :], k.psum[:, 0, :])
    dve.tensor_copy(f.v[:, 1, :], k.psum[:, 1, :]).then_inc(*f.dve.mark("v"))
    dve.drain()
    dve.wait_ge(k.even_out, 4)

    def tap(j):
        for i in range(8):
            weight = f.p("conv_w", i * A_CONV + j)
            src = f.qk_raw[:, i, j:j + T]
            if j == 0:
                last = dve.tensor_scalar(f.qk[:, i, :], src, weight, None, ALU.mult)
            else:
                last = dve.scalar_tensor_tensor(f.qk[:, i, :], src, weight, f.qk[:, i, :], ALU.mult, ALU.add)
        return last
    for j, t in enumerate(range(9, 16, 2)):
        last = tap(j)
        if j == 3:
            last.then_inc(*f.dve.mark("conv"))
        copy_tile(k, dve, w, t, even_tile_out(f, t))
        dve.drain()

    r4 = slice(0, 4)
    dve.wait_ge(*f.act.at("fl"))
    dve.scalar_tensor_tensor(f.gl[r4, :], f.gf[r4, :], 0.0, f.gt[r4, :], ALU.min, ALU.subtract)
    dve.drain()
    dve.tensor_tensor_scan(f.cum[r4, :], f.one[r4, :], f.gl[r4, :], 0.0, ALU.mult, ALU.add)
    dve.drain()
    dve.tensor_tensor(f.gi[r4, :], f.gi[r4, :], f.cum[r4, :], ALU.subtract).then_inc(*f.dve.mark("cmin"))
    dve.drain()
    dve.tensor_tensor_scan(f.gl[r4, :], f.one[r4, :], f.gi[r4, :], 0.0, ALU.mult, ALU.max)
    dve.drain()
    dve.tensor_scalar(f.rows[r4, 0, :], f.gl[r4, :], -1.0, None, ALU.mult)
    dve.tensor_tensor(f.gt[r4, :], f.cum[r4, :], f.gl[r4, :], ALU.add).then_inc(*f.dve.mark("rows"))
    for t in range(17, 20, 2):
        copy_tile(k, dve, w, t, even_tile_out(f, t))

    dve.wait_ge(k.even_out, 7)
    for j, raw in enumerate((f.kc, f.vc)):
        dve.tensor_copy(f.shift[0:HEAD, j * 2, :], raw[0:HEAD, 0, :])
        last = dve.tensor_copy(f.shift[HEAD:P, j * 2 + 1, 0:T - 1], raw[HEAD:P, 0, 1:T])
    last.then_inc(*f.dve.mark("shift"))

    def arg(h):
        dve.wait_ge(*f.pe.at(f"rows{h}"))
        dve.tensor_tensor(f.arg[h % 2], k.psum[:, h % 2, 0:T].rearrange("p (n t) -> p n t", n=2),
                          bc(k.c("causal_st"), 2), ALU.add).then_inc(*f.dve.mark(f"arg{h}"))

    def pt(h):
        dve.wait_ge(*f.pe.at(f"s{h}"))
        dve.wait_ge(*f.act.at(f"e{h}"))
        dve.scalar_tensor_tensor(f.pt[h % 2], k.psum[:, 2 + h % 2, 0:3 * P].rearrange("p (n t) -> p n t", n=3),
                                 A_SCALE, f.e[h % 2], ALU.mult, ALU.mult).then_inc(*f.dve.mark(f"pt{h}"))

    def out(h):
        dve.wait_ge(*f.act.at(f"den{h}"))
        den = f.den[h % 2]
        dve.tensor_tensor(den, den, k.bank(h % 2)[:, 1, :], ALU.max)
        dve.drain()
        dve.reciprocal(den, den)
        dve.drain()
        dve.tensor_tensor(f.hs[:, h, :], k.bank(4 + h % 2)[:, 0, :], den, ALU.mult).then_inc(
            *f.dve.mark(f"h{h}"))
    for step, h in ((arg, 0), (arg, 1), (pt, 0), (pt, 1), (out, 0), (out, 1), (arg, 2), (arg, 3), (pt, 2), (pt, 3),
                    (out, 2), (out, 3)):
        step(h)

    dve.wait_ge(f.moved, 64)
    for j in range(2):
        for g in range(2):
            for a in range(2):
                src = f.shift[:, j * 2 + g, 16 * a:16 * a + 240].rearrange("p (m l two) -> p two l m", two=2, l=8)
                where = f.p("cmp_pos")[:, j * 16 + 8 * a:j * 16 + 8 * a + 8].unsqueeze(2).to_broadcast([P, 8, 15])
                last = dve.tensor_tensor(f.win[:, j * 16 + 8 * a:j * 16 + 8 * a + 8, g * 15:g * 15 + 15],
                                         src[:, 0, :, :], where, ALU.add)
    last.then_inc(*f.dve.mark("win"))
    hid_psum = k.psum[:, 0, 0:64].rearrange("p (j n) -> p j n", j=2)[:, :, 0:30]
    hid, t = f.hid[:, :, 0:30], f.hid_t[:, :, 0:30]
    dve.wait_ge(*f.act.at("hid_sq"))
    dve.tensor_copy(hid, hid_psum)
    dve.tensor_scalar(t, t, 0.044715, 1.0, ALU.mult, ALU.add)
    dve.drain()
    dve.tensor_tensor(t, t, hid, ALU.mult).then_inc(*f.dve.mark("hid_in"))
    dve.wait_ge(*f.act.at("hid_tanh"))
    dve.scalar_tensor_tensor(t, t, 1.0, hid, ALU.add, ALU.mult)
    dve.drain()
    for g in range(2):
        for j in range(4):
            dve.tensor_scalar(f.hid_v[:, g * 4 + j, j * 16:j * 16 + 15], f.hid_t[:, 1, g * 15:g * 15 + 15], 0.5, None,
                              ALU.mult)
    dve.tensor_scalar(hid, t, 0.5, None, ALU.mult).then_inc(*f.dve.mark("hid"))
    dve.wait_ge(*f.pe.at("cmp_kv"))
    dve.tensor_copy(f.vcmp[0:HEAD, :, :], k.psum[0:HEAD, 2, :].rearrange("p (n d) -> p n d", n=8)).then_inc(
        *f.dve.mark("cmp_v"))
    dve.wait_ge(*f.pe.at("cmp_scores"))
    for g in range(2):
        mask = k.c("cmp_mask").rearrange("p (t m) -> p t m", t=2).unsqueeze(2).to_broadcast([P, 2, 4, 16])
        dve.tensor_tensor(f.pc[:, g * 8:g * 8 + 8, :].rearrange("p (t j) m -> p t j m", t=2),
                          k.psum[:, 3 + g, 0:P].rearrange("p (t j m) -> p t j m", t=2, j=4), mask, ALU.add)
    dve.drain()
    dve.tensor_reduce(f.pm, f.pc, AX_X, ALU.max)
    dve.drain()
    dve.tensor_scalar(f.pm, f.pm, NEG / 10, None, ALU.max)
    dve.drain()
    dve.tensor_tensor(f.pc, f.pc, f.pm.unsqueeze(2).to_broadcast([P, 16, 16]), ALU.subtract).then_inc(
        *f.dve.mark("cmp_max"))
    dve.wait_ge(*f.act.at("cmp_exp"))
    dve.tensor_reduce(f.ps, f.pc, AX_X, ALU.add)
    dve.drain()
    dve.tensor_scalar(f.ps, f.ps, 1e-30, None, ALU.max)
    dve.drain()
    dve.reciprocal(f.ps, f.ps)
    dve.drain()
    for g in range(2):
        ps = f.ps[:, g * 8:g * 8 + 8].rearrange("p (t j) -> p t j", t=2)
        gate = f.gate[:, :, g * 12:g * 12 + 12].rearrange("p t (j b) -> p b t j", b=3)[:, 0, :, :]
        dve.tensor_tensor(ps, ps, gate, ALU.mult)
    dve.drain()
    dve.tensor_tensor(f.pc, f.pc, f.ps.unsqueeze(2).to_broadcast([P, 16, 16]), ALU.mult).then_inc(
        *f.dve.mark("cmp"))

    att = Attention(k, f, 0, 2, B_SCALE)
    for i in range(16 + 1):
        if i < 16:
            tt = NSA_UNITS[i][2]
            n = att.keys(tt)
            dve.wait_ge(f.att_scores, i + 1)
            diag = att.scores(i, tt)[:, :, n - P:n]
            dve.tensor_tensor(diag, diag, bc(k.c("causal_qk"), 2), ALU.add)
            att.dve_max(dve, i, tt)
        if i >= 1:
            g, j, tt = NSA_UNITS[i - 1]
            head = (g * 4 + j) * 3
            att.dve_prob(dve, i - 1, tt, f.gate[:, tt, head + 1:head + 3])
    dve.wait_ge(f.att_out, 16)
    dve.tensor_copy(k.cat[:, 4:8, :], k.psum[:, 6:8, :].rearrange("p b (n t) -> p (b n) t", t=T)).then_inc(
        *f.dve.mark("out"))
    dve.wait_ge(*f.pe.at("hs.sum"))
    dve.scalar_tensor_tensor(f.hs, k.psum[:, 0:2, :].rearrange("p b (n t) -> p (b n) t", t=T), -1.0 / P, f.hs,
                             ALU.mult, ALU.add).then_inc(*f.dve.mark("hs.xc"))
    dve.wait_ge(*f.act.at("hs.std"))
    dve.reciprocal(k.tmp[:, 0:4, :], k.tmp[:, 0:4, :])
    dve.drain()
    dve.tensor_tensor(f.o, f.o, k.tmp[:, 0:4, :], ALU.mult)
    dve.drain()
    for h in range(4):
        last = dve.scalar_tensor_tensor(k.cat[:, h, :], f.hs[:, h, :], f.p("a_norm", h), f.o[:, h, :],
                                        ALU.mult, ALU.mult)
    last.then_inc(*f.dve.mark("ya"))
    dve.drain()


def even_pool(k, f, pool):
    pool.wait_ge(k.even_out, 7)
    pool.wait_ge(k.odd_out, 7)
    for j, raw in enumerate((f.kc, f.vc)):
        pool.dma_start(f.shift[HEAD:P, j * 2, 0:T - 1], raw[0:HEAD, 0, 1:T]).then_inc(f.moved, 16)
        pool.dma_start(f.shift[0:HEAD, j * 2 + 1, :], raw[HEAD:P, 0, :]).then_inc(f.moved, 16)



def odd_tile_out(f, t):
    if t < 8:
        return (*(f.cq[:, i, :] for i in range(4)), *(f.ckv[:, i, :] for i in range(2)), f.rc[:, 4, :],
                f.ik[:, 0, :])[t]
    if t < 16:
        return f.qn[:, t - 8, :]
    if t < 20:
        return f.rc[:, t - 16, :]
    if t < 24:
        return f.ri[:, t - 20, :]
    return f.q_abs[:, t - 24, :]


ODD_TILES = 40
EVEN_TILES = 20


def odd_tensor(k, f, pe, w):
    def mm(out, lhsT, rhs, start=True, stop=True):
        return pe.matmul(out, lhsT, rhs, start=start, stop=stop, skip_group_check=True)

    flat = lambda x: x.rearrange("p n t -> p (n t)")
    pe.wait_ge(k.x_ready, 2)
    for _ in range(8):
        pe_columns(k, pe, w, pe_next_tile(k, pe, w), k.x).then_inc(k.proj_ready, 1)
    slot = w.n["unit"] % RING
    pe.wait_ge(k.filled[slot], w.filled())
    wt = k.ring[:, slot, :].rearrange("p (k c) -> p k c", c=P)
    for tt in range(2):
        for i in range(KD):
            last = mm(k.psum[:, 0, tt * 8:tt * 8 + 8], k.x[:, i, tt * P:tt * P + P], wt[:, i, 0:8],
                      i == 0, i == KD - 1)
            if tt + i == 0:
                last.then_inc(k.freed, w.owed)
                w.owed = 0
    last.then_inc(*f.ope.mark("iw"))
    w.n["unit"] += 1
    w.owed += 1
    pe.wait_ge(*f.odve.at("sq"))
    for i in range(4):
        mm(k.bank(1)[:, 0, :], k.c("ones"), k.sq[:, i, :], i == 0, i == 3)
    for i in range(2):
        mm(k.bank(1)[:, 1, :], k.c("ones"), k.sq[:, 4 + i, :], i == 0, i == 1)
    mm(k.bank(2)[:, 0, :], k.c("block64"), f.ik[:, 0, :]).then_inc(*f.ope.mark("sums"))
    pe.wait_ge(*f.odve.at("ik_sq"))
    mm(k.bank(3)[:, 0, :], k.c("block64"), k.sq[:, 6, :]).then_inc(*f.ope.mark("ik_ss"))
    pe.wait_ge(*f.odve.at("cqn"))
    for _ in range(8):
        pe_tiles(k, pe, w, [[(half * 4 + i, f.cqn[:, i, :]) for i in range(4)] for half in range(2)])
    pe.wait_ge(k.even_out, (EVEN_TILES + 24) // 2)
    pe.wait_ge(k.odd_out, (EVEN_TILES + 24) // 2)
    for i in range(2):
        pe_tiles(k, pe, w, [[(h * 2 + c, f.qn[:, 4 * i + h, :])] for h in range(4) for c in range(2)])
    pe.wait_ge(*f.odve.at("ikn"))
    for what, src, matrix_name in (("swap_c", f.rc, "swap64"), ("swap_i", f.ri, "swap32")):
        if what == "swap_i":
            pe.wait_ge(*f.odve.at("rope_c"))
        for b, (i, n) in enumerate(((0, 2), (2, 2), (4, 1))):
            last = mm(k.psum[:, b, 0:n * T], k.c(matrix_name), flat(src[:, i:i + n, :]))
        last.then_inc(*f.ope.mark(what))
    for tt in range(2):
        for c in range(2):
            last = pe.transpose(k.bank(3, P)[:, tt * 2 + c, :], f.ckvn[:, c, tt * P:tt * P + P], k.c("ident"))
    last.then_inc(*f.ope.mark("turned"))
    pe.wait_ge(*f.odve.at("rope_i"))
    pe.wait_ge(*f.odve.at("turned"))
    pe.wait_ge(k.even_out, (EVEN_TILES + ODD_TILES) // 2)
    pe.wait_ge(k.odd_out, (EVEN_TILES + ODD_TILES) // 2)
    for h in range(8):
        rows, i = head_rows(h)
        mm(k.psum[:, h, 0:P], f.ri[rows, i, 0:P], f.ri[rows, 4, 0:P])
        mm(k.psum[:, h, P:3 * P], f.ri[rows, i, P:T], f.ri[rows, 4, :]).then_inc(*f.ope.mark(f"i{h}"))

    att = Attention(k, f, 16, 1, C_SCALE)
    pe.wait_ge(*f.oact.at("r7"))

    def att_scores(u, h, tt):
        att.scores_free(pe, u)
        rows, i = head_rows(h)
        out, n, tok = att.scores(u, tt)[:, 0, :], att.keys(tt), slice(tt * P, tt * P + P)
        for c in range(2):
            mm(out, f.q_abs[:, h * 2 + c, tok], f.ckvn[:, c, 0:n], c == 0, False)
        mm(out, f.rc[rows, i, tok], f.rc[rows, 4, 0:n], False, True).then_inc(f.att_scores, 1)

    def att_values(u, h, tt):
        pe.wait_ge(f.att_copied, 16 + u + 1)
        if tt == 0 and h > 0:
            pe.wait_ge(*f.odve.at(f"lat{h - 1}"))
        for c in range(2):
            out = k.bank(6)[:, c, tt * P:tt * P + P]
            for kt in range(tt + 1):
                last = mm(out, f.ckv_tok[:, kt, c * P:c * P + P], f.prob_t[u % 2][:, kt * P:kt * P + P],
                          kt == 0, kt == tt)
        last.then_inc(f.att_out, 1)

    def up(h):
        if h % 4 == 0:
            slot = w.n["unit"] % RING
            pe.wait_ge(k.filled[slot], w.filled())
            w.n["unit"] += 1
            f.up_unit = k.ring[:, slot, :].rearrange("p (k c) -> p k c", c=P)
        pe.wait_ge(*f.odve.at(f"lat{h}"))
        if h > 0:
            pe.wait_ge(*f.oact.at(f"up{h - 1}"))
        for c in range(2):
            last = mm(k.bank(7)[:, 0, :], f.up_unit[:, h % 4 * 2 + c, :], f.o_lat[h % 2][:, c, :], c == 0, c == 1)
            if c == 0 and h % 4 == 0:
                last.then_inc(k.freed, w.owed)
                w.owed = 1
        last.then_inc(*f.ope.mark(f"lat{h}"))

    for i in range(16 + 6):
        if i < 16:
            att_scores(i, *MLA_UNITS[i])
        if 2 <= i < 18:
            att.pe_turn(pe, i - 2, MLA_UNITS[i - 2][1])
        if 3 <= i < 19:
            att_values(i - 3, *MLA_UNITS[i - 3])
        if i >= 5 and i % 2 == 1 and i < 21:
            up((i - 5) // 2)
    pe.wait_ge(*f.oact.at("up7"))
    for n in range(KD):
        last = pe_columns(k, pe, w, k.acc[:, n, :], k.cat)
    last.then_inc(k.acc_ready, 1)
    w.n["acc"] += 1


def odd_scalar(k, f, act, w):
    for t in range(0, 8, 2):
        copy_tile(k, act, w, EVEN_TILES + t, odd_tile_out(f, t))
    act.wait_ge(*f.ope.at("sums"))
    act.activation(k.std[:, 0, :], k.bank(1)[:, 0, :], ACT.Sqrt, bias=k.eps(LN_EPS), scale=1.0 / 512)
    act.activation(k.std[:, 1, :], k.bank(1)[:, 1, :], ACT.Sqrt, bias=k.eps(LN_EPS), scale=1.0 / 256).then_inc(
        *f.oact.mark("std"))
    act.wait_ge(*f.ope.at("ik_ss"))
    act.activation(f.iks[:, 0, :], k.bank(3)[:, 0, :], ACT.Sqrt, bias=k.eps(LN_EPS), scale=1.0 / HEAD).then_inc(
        *f.oact.mark("ik_std"))
    for t in range(8, ODD_TILES, 2):
        copy_tile(k, act, w, EVEN_TILES + t, odd_tile_out(f, t))
    for h in range(8):
        act.wait_ge(*f.ope.at(f"i{h}"))
        if h >= 2:
            act.wait_ge(*f.odve.at(f"acc{h - 2}"))
        act.activation(f.relu[h % 2], k.psum[:, h, 0:3 * P], ACT.Relu).then_inc(*f.oact.mark(f"r{h}"))
    att = Attention(k, f, 16, 1, C_SCALE)
    for i in range(16 + 7):
        if i < 16:
            att.act_exp(act, i, MLA_UNITS[i][1])
        if 2 <= i < 18:
            att.act_copy(act, i - 2, MLA_UNITS[i - 2][1])
        if i >= 6 and i % 2 == 0 and (i - 6) // 2 < 8:
            h = (i - 6) // 2
            act.wait_ge(*f.ope.at(f"lat{h}"))
            act.activation(k.cat[:, h, :], k.bank(7)[:, 0, :], ACT.Copy).then_inc(*f.oact.mark(f"up{h}"))


def odd_vector(k, f, dve, w):
    for t in range(1, 8, 2):
        copy_tile(k, dve, w, EVEN_TILES + t, odd_tile_out(f, t))
    dve.drain()
    dve.wait_ge(k.even_out, (EVEN_TILES + 8) // 2)
    dve.tensor_tensor(k.sq[:, 0:4, :], f.cq, f.cq, ALU.mult)
    dve.tensor_tensor(k.sq[:, 4:6, :], f.ckv, f.ckv, ALU.mult)
    dve.wait_ge(*f.ope.at("iw"))
    dve.tensor_scalar(f.wi, k.psum[:, 0, 0:16].rearrange("p (t h) -> p t h", t=2), WI_SCALE, None,
                      ALU.mult).then_inc(*f.odve.mark("sq"))
    dve.wait_ge(*f.ope.at("sums"))
    dve.scalar_tensor_tensor(f.ikc[:, 0, :], k.bank(2)[:, 0, :], -1.0 / HEAD, f.ik[:, 0, :], ALU.mult, ALU.add)
    dve.drain()
    dve.tensor_tensor(k.sq[:, 6, :], f.ikc[:, 0, :], f.ikc[:, 0, :], ALU.mult).then_inc(*f.odve.mark("ik_sq"))
    dve.wait_ge(*f.oact.at("std"))
    dve.reciprocal(k.rstd, k.std)
    dve.drain()
    for i in range(4):
        dve.scalar_tensor_tensor(f.cqn[:, i, :], f.cq[:, i, :], f.p("q_norm", i), k.rstd[:, 0, :],
                                 ALU.mult, ALU.mult)
    for i in range(2):
        last = dve.scalar_tensor_tensor(f.ckvn[:, i, :], f.ckv[:, i, :], f.p("kv_norm", i), k.rstd[:, 1, :],
                                        ALU.mult, ALU.mult)
    last.then_inc(*f.odve.mark("cqn"))
    dve.wait_ge(*f.oact.at("ik_std"))
    dve.reciprocal(f.iks[:, 1, :], f.iks[:, 0, :])
    dve.drain()
    dve.scalar_tensor_tensor(f.ikc[:, 0, :], f.ikc[:, 0, :], f.p("ik_g"), f.iks[:, 1, :], ALU.mult, ALU.mult)
    dve.drain()
    dve.tensor_scalar(f.ri[:, 4, :], f.ikc[:, 0, :], f.p("ik_b"), None, ALU.add).then_inc(*f.odve.mark("ikn"))
    for t in range(9, ODD_TILES, 2):
        copy_tile(k, dve, w, EVEN_TILES + t, odd_tile_out(f, t))
    dve.drain()
    dve.wait_ge(k.even_out, (EVEN_TILES + ODD_TILES) // 2)
    for j, (name, x) in enumerate((("c", f.rc), ("i", f.ri))):
        dve.wait_ge(*f.ope.at(f"swap_{name}"))
        dve.tensor_tensor(f.rt, x, bc(f.cos[:, j, :], 5), ALU.mult)
        dve.tensor_tensor(k.tmp[:, 0:5, :], k.psum[:, 0:3, :].rearrange("p b (n t) -> p (b n) t", t=T)[:, 0:5, :],
                          bc(f.sin[:, j, :], 5), ALU.mult)
        dve.drain()
        dve.tensor_tensor(x, f.rt, k.tmp[:, 0:5, :], ALU.add).then_inc(*f.odve.mark(f"rope_{name}"))
        dve.drain()
    dve.wait_ge(*f.ope.at("turned"))
    dve.tensor_copy(f.ckv_tok, k.bank(3)).then_inc(*f.odve.mark("turned"))

    for h in range(8):
        dve.wait_ge(*f.oact.at(f"r{h}"))
        for tt, cols in enumerate((slice(0, P), slice(P, 3 * P))):
            weight = f.wi[:, tt, h:h + 1]
            if h == 0:
                last = dve.tensor_scalar(f.isc[:, cols], f.relu[0][:, cols], weight, None, ALU.mult)
            else:
                last = dve.scalar_tensor_tensor(f.isc[:, cols], f.relu[h % 2][:, cols], weight, f.isc[:, cols],
                                                ALU.mult, ALU.add)
        last.then_inc(*f.odve.mark(f"acc{h}"))
        dve.drain()
    diag = lambda x: x.rearrange("p (n t) -> p n t", n=3)[:, 0:3:2, :]
    dve.tensor_tensor(diag(f.isc), diag(f.isc), bc(k.c("causal_qk"), 2), ALU.add)
    dve.drain()
    src = f.isc
    for r in range(TOPK // 8):
        dst = f.work[r % 2]
        for tt, cols in enumerate((slice(0, P), slice(P, 3 * P))):
            dve.max(f.top[:, tt, :], src[:, cols])
        dve.drain()
        for tt, cols in enumerate((slice(0, P), slice(P, 3 * P))):
            dve.match_replace(dst[:, cols], f.top[:, tt, :], src[:, cols], TAKEN)
        dve.drain()
        src = dst
    dve.tensor_scalar(f.sel, src, TAKEN / 2, NEG, ALU.is_gt, ALU.mult)
    dve.drain()
    dve.tensor_tensor(diag(f.sel), diag(f.sel), bc(k.c("causal_qk"), 2), ALU.add).then_inc(*f.odve.mark("sel"))
    dve.drain()

    att = Attention(k, f, 16, 1, C_SCALE)
    for i in range(16 + 5):
        if i < 16:
            tt = MLA_UNITS[i][1]
            dve.wait_ge(f.att_scores, 16 + i + 1)
            s = att.scores(i, tt)[:, 0, :]
            dve.tensor_tensor(s, s, f.sel[:, 0:P] if tt == 0 else f.sel[:, P:3 * P], ALU.add)
            att.dve_max(dve, i, tt)
        if 1 <= i < 17:
            att.dve_prob(dve, i - 1, MLA_UNITS[i - 1][1])
        if i >= 5 and i % 2 == 1:
            h = (i - 5) // 2
            dve.wait_ge(f.att_out, 16 + 2 * h + 2)
            if h >= 2:
                dve.wait_ge(*f.ope.at(f"lat{h - 2}"))
            dve.tensor_copy(f.o_lat[h % 2], k.bank(6)).then_inc(*f.odve.mark(f"lat{h}"))



def tables_vector(k, f, dve):
    dve.wait_ge(f.params, 32)
    dve.tensor_copy(f.pos, f.pos_i.bitcast(I32))
    dve.drain()
    for j in range(2):
        dve.tensor_scalar(f.angle[:, j, :], f.pos, k.c("inv_freq")[:, j:j + 1], None, ALU.mult)
    dve.drain()
    dve.tensor_scalar(f.turns, f.angle, float(1 / (2 * np.pi)), ROUND, ALU.mult, ALU.add)
    dve.drain()
    dve.tensor_scalar(f.turns, f.turns, ROUND, None, ALU.subtract)
    dve.drain()
    for part in TWO_PI:
        dve.scalar_tensor_tensor(f.angle, f.turns, -part, f.angle, ALU.mult, ALU.add)
        dve.drain()
    dve.tensor_scalar(f.turns, f.angle, float(np.pi / 2), float(-2 * np.pi), ALU.is_gt, ALU.mult)
    dve.drain()
    dve.scalar_tensor_tensor(f.red, f.angle, float(np.pi / 2), f.turns, ALU.add, ALU.add)
    dve.drain()
    dve.tensor_scalar(f.red, f.red, -PI, PI, ALU.max, ALU.min)
    dve.tensor_scalar(f.angle, f.angle, -PI, PI, ALU.max, ALU.min).then_inc(f.angles, 1)


def tables_scalar(k, f, act):
    act.wait_ge(f.angles, 1)
    act.activation(f.cos, f.red, ACT.Sin)
    act.activation(f.sin, f.angle, ACT.Sin)



def tail_tensor(k, f, pe, w, layer):
    def norm():
        for half in range(2):
            pe.wait_ge(f.y_ready, w.value("norm", scale=2) + half + 1)
            for i in range(half * KD // 2, (half + 1) * KD // 2):
                last = pe.matmul(k.bank(7)[:, 0, :], k.c("ones"), k.x[:, i, :], start=(i == 0), stop=(i == KD - 1))
        last.then_inc(f.mean_ready, 1)
        pe_square_sum(k, pe, w)

    def tile_of_h(i):
        pe.wait_ge(k.h_ready, w.value("pre", scale=KD) + i + 1)
    norm()
    pe_ffn(k, pe, w, k.x, FF1, False, tile_of_h)
    w.n["pre"] += 1
    norm()
    for n in range(KD):
        if n % 4 == 0:
            slot = w.n["unit"] % RING
            pe.wait_ge(k.filled[slot], w.filled())
            unit = k.ring[:, slot, :].rearrange("p (k c) -> p k c", c=P)
            w.n["unit"] += 1
        if n >= 4:
            pe.wait_ge(f.ple_used, layer * KD + n - 3)
        for c in range(2):
            last = pe.matmul(k.bank(4 + n % 4)[:, 1, :], unit[:, n % 4 * 2 + c, :], f.embed[:, layer * 2 + c, :],
                             start=(c == 0), stop=(c == 1), skip_group_check=True)
            if n % 4 == 0 and c == 0:
                last.then_inc(k.freed, w.owed)
                w.owed = 0
        slot = w.n["unit"] % RING
        pe.wait_ge(k.filled[slot], w.filled())
        own = k.ring[:, slot, :].rearrange("p (k c) -> p k c", c=P)
        for i in range(KD):
            if n == 0:
                tile_of_h(i)
            last = pe.matmul(k.bank(4 + n % 4)[:, 0, :], own[:, i, :], k.x[:, i, :], start=(i == 0),
                             stop=(i == KD - 1), skip_group_check=True)
        last.then_inc(f.ple_ready, 1)
        w.n["unit"] += 1
        w.owed += 1 + (n % 4 == 3)
    w.n["pre"] += 1


def tail_scalar(k, f, act, w, layer):
    def norm(bias):
        def half(i):
            act.wait_ge(f.c_ready, w.value("norm", scale=2) + i + 1)
        act_squares(k, act, w, k.x, half)
        act_std(k, act, w, LN_EPS)
        for i in range(KD):
            act.wait_ge(f.t_ready, w.value("pre", scale=KD) + i + 1)
            act.activation(k.x[:, i, :], k.tmp[:, i, :], ACT.Identity, bias=f.p(bias, layer * KD + i)).then_inc(
                k.h_ready, 1)
        w.n["pre"] += 1
    norm("ln1_b")
    act_ffn(k, act, w, FF1, ACT.Relu)
    norm("ln2_b")
    for n in range(KD):
        act.wait_ge(f.ple_ready, layer * KD + n + 1)
        if n >= 2:
            act.wait_ge(f.ple_used, layer * KD + n - 1)
        act.activation(k.hid_act[:, n % 2, :], k.bank(4 + n % 4)[:, 0, :], ACT.Sigmoid).then_inc(f.gate_ready, 1)
    w.n["acc"] += 2
    w.n["x"] += 2


def tail_vector(k, f, dve, w, layer):
    def norm(gain):
        dve.wait_ge(k.acc_ready, w.value("acc", 1))
        w.n["acc"] += 1
        if gain == "ln2_g":
            dve.wait_ge(k.h_ready, w.value("pre", scale=KD))
        for half in range(2):
            dve.scalar_tensor_tensor(halves(k.x)[half], halves(k.x)[half], ALPHA, halves(k.acc)[half],
                                     ALU.mult, ALU.add).then_inc(f.y_ready, 1)
        dve.drain()
        dve.wait_ge(f.mean_ready, w.value("norm", 1))
        for half in range(2):
            dve.scalar_tensor_tensor(halves(k.x)[half], bc(k.bank(7)[:, 0, :], KD // 2), -1.0 / D,
                                     halves(k.x)[half], ALU.mult, ALU.add).then_inc(f.c_ready, 1)
        dve_rstd(k, dve, w)
        for i in range(KD):
            dve.scalar_tensor_tensor(k.tmp[:, i, :], k.x[:, i, :], f.p(gain, layer * KD + i), k.rstd[:, 0, :],
                                     ALU.mult, ALU.mult).then_inc(f.t_ready, 1)
        w.n["pre"] += 1
    norm("ln1_g")
    dve_ffn(k, dve, w, FF1, False)
    norm("ln2_g")
    for n in range(KD):
        dve.wait_ge(f.gate_ready, layer * KD + n + 1)
        dve.tensor_tensor(k.h[:, n, :], k.hid_act[:, n % 2, :], k.bank(4 + n % 4)[:, 1, :], ALU.mult).then_inc(
            f.ple_used, 1)
    dve.drain()
    dve.wait_ge(k.h_ready, w.value("pre", scale=KD))
    for half in range(2):
        dve.tensor_tensor(halves(k.x)[half], halves(k.x)[half], halves(k.h)[half], ALU.add).then_inc(k.x_ready, 1)
    dve.drain()
    w.n["x"] += 2



def build(nc, x, consts, weights, params1, positions, params2, out):
    with ExitStack() as ctx:
        k = Core(nc, ctx)
        space = k.sb("space", ARENA)
        f, s = First(k, Arena(space)), Second(k, Arena(space))
        block = ctx.enter_context(nc.Block())
        turns = weights.shape[0] // RING
        assert weights.shape[0] % RING == 0

        def between(w):
            w.n["proj"] = EVEN_TILES + ODD_TILES
            w.n["even"] = w.n["odd"] = w.n["proj"] // 2
            w.n["x"] = 2

        @block.sync
        def _(sp):
            sp.dma_start(k.x, x).then_inc(k.load, 16)
            sp.dma_start(k.const, consts).then_inc(k.load, 16)
            for slot in range(RING):
                sp.dma_start(k.ring[:, slot, :], weights[slot]).then_inc(k.filled[slot], 16)
                if slot == 2:
                    sp.dma_start(f.par, params1).then_inc(f.params, 16)
                    sp.dma_start(f.pos_i.bitcast(I32), positions.broadcast_to([P, T])).then_inc(f.params, 16)
            with sp.Fori(1, turns) as turn:
                for slot in range(RING):
                    sp.wait_ge(k.freed, (turn - 1) * RING + (slot + 1))
                    sp.dma_start(k.ring[:, slot, :], weights[turn * RING + slot]).then_inc(k.filled[slot], 16)
            sp.wait_ge(k.x_ready, 2 * LAYERS + LAYERS * PER_LAYER["x"])
            sp.dma_start(out, k.x).then_inc(k.saved, 16)
            sp.wait_ge(k.saved, 16)

        @block.tensor
        def _(pe):
            w = Walk()
            pe.wait_ge(k.load, 32)
            pe.wait_ge(f.params, 32)
            even_tensor(k, f, pe, w)
            tail_tensor(k, f, pe, w, 0)
            odd_tensor(k, f, pe, w)
            tail_tensor(k, f, pe, w, 1)
            between(w)
            pe.wait_ge(k.x_ready, 2 * LAYERS)
            second_tensor(k, s, pe, w)

        @block.scalar
        def _(act):
            w = Walk()
            act.wait_ge(k.load, 32)
            act.wait_ge(f.params, 32)
            tables_scalar(k, f, act)
            even_scalar(k, f, act, w)
            tail_scalar(k, f, act, w, 0)
            odd_scalar(k, f, act, w)
            tail_scalar(k, f, act, w, 1)
            between(w)
            second_scalar(k, s, act, w)

        @block.vector
        def _(dve):
            w = Walk()
            dve.wait_ge(k.load, 32)
            tables_vector(k, f, dve)
            even_vector(k, f, dve, w)
            tail_vector(k, f, dve, w, 0)
            odd_vector(k, f, dve, w)
            tail_vector(k, f, dve, w, 1)
            between(w)
            second_vector(k, s, dve, w)

        @block.gpsimd
        def _(pool):
            w = Walk()
            even_pool(k, f, pool)
            between(w)
            second_pool(k, s, pool, w, params2)



def constants():
    c = np.zeros((P, NCOLC), np.float32)
    i = np.arange(P)
    s, t = i[:, None], i[None, :]
    near, chunk = s // 16 == t // 16, s // CHUNK == t // CHUNK

    def put(name, a):
        c[:, COLC[name][0]:COLC[name][1]] = a
    put("ident", s == t)
    put("ones", 1)
    put("block64", s // HEAD == t // HEAD)
    put("near_st", (s < t) & near)
    put("near_ts", (s > t) & near)
    put("far_st", (s < t) & chunk & ~near)
    put("before_st", (s < t) & chunk)
    put("upto_st", (s <= t) & chunk)
    put("tril_st", s <= t)
    put("restart", np.arange(2 * T)[None, :] % CHUNK != 0)
    sel = np.zeros((P, 2 * P))
    for ch in range(2 * P):
        sel[ch // HEAD, ch] = 1
    put("headsel", sel)
    put("causal_st", np.where(s <= t, 0, NEG))
    put("causal_qk", np.where(t <= s, 0, NEG))
    q, m = np.arange(2)[None, :, None] * P + i[:, None, None], np.arange(16)[None, None, :]
    put("cmp_mask", np.where((16 * m + 31 <= q) & (m < 15), 0, NEG).reshape(P, 32))
    put("head4", np.arange(4 * P)[None, :] // P == i[:, None])
    for name, half in (("swap64", 32), ("swap32", 16)):
        m = np.zeros((P, P))
        for o in range(P):
            r = o % HEAD
            if r < half:
                m[o + half, o] = -1
            elif r < 2 * half:
                m[o - half, o] = 1
        put(name, m)
    inv = lambda d: (np.float32(10000.0) ** (-np.arange(0, d, 2, dtype=np.float32) / np.float32(d))).astype(np.float32)
    r = i % HEAD
    put("inv_freq", np.stack([inv(64)[r % 32], np.where(r < 32, inv(32)[r % 16], 0)], axis=1))
    a = COLC["eps"][0]
    for value, j in EPS.items():
        c[:, a + j] = value
    return c


def channels(a):
    a = np.asarray(a)
    if a.ndim == 1:
        return a.reshape(-1, P).T
    return a.reshape(a.shape[0], -1, P).transpose(2, 1, 0).reshape(P, -1)


def units_in(wt):
    n = wt.shape[1] // P
    return wt.reshape(KD, P, n, P).transpose(2, 1, 0, 3).reshape(n, P, UNIT)


def ffn_units(ins, down):
    ins, down = [units_in(a) for a in ins], down.reshape(-1, P, UNIT)
    out = []
    for f in range(len(down)):
        out += [a[f] for a in ins]
        if f:
            out.append(down[f - 1])
    return out + [down[-1]]


def second_units(v, l):
    w_in = v["w_in"][l]
    a, b, c, d = np.split(w_in, [768, 1280, 2176], axis=1)
    gate_b, gate_c, xa = np.split(a, 3, axis=1)
    u, vv = np.split(b, 2, axis=1)
    order = np.concatenate([c, d, gate_c, xa, gate_b, vv, u], axis=1)
    units = ffn_units([v["ffn1_w_gate"][l], v["ffn1_w_up"][l]], v["ffn1_w_down"][l])
    units += list(units_in(order)) + list(units_in(v["w_out"][l]))
    units += ffn_units([v["ffn2_w_gate"][l], v["ffn2_w_up"][l]], v["ffn2_w_down"][l])
    units += [np.zeros((P, UNIT), np.float32)] * PAD2
    assert len(units) == UNITS2
    return units


def second_params(v, l):
    out = np.zeros((P, NCOL2), np.float32)
    for name, _ in VEC2:
        a, b = COL2[name]
        if name == "lora_up":
            out[:, a:b] = np.concatenate([v["rk_w_up"][l], v["rk_a_up"][l], v["rk_g_up"][l]], axis=0)
        elif name == "sg_w":
            out[:, a:b] = v["sg_w"][l].transpose(2, 0, 1).reshape(P, -1)
        elif name == "sg_b":
            out[0:4, a:b] = v["sg_b"][l]
        else:
            src = v[name][l]
            out[:, a:b] = channels(src.reshape(-1) if name == "rk_r_k" else src)
    return out


def square_units(wt, inner):
    kt, n = wt.shape[0] // P, wt.shape[1] // inner
    per = UNIT // inner
    a = wt.reshape(kt, P, n, inner).transpose(2, 0, 1, 3)
    a = a.reshape(-1, P, inner)
    return a.reshape(-1, per, P, inner).transpose(0, 2, 1, 3).reshape(-1, P, UNIT)


def first_units(v):
    sizes = (512, 512, 512, 512, 4, 4, 512, 128, 128, 128, 128, 128, 128, 24)
    aq, ak, av, ao, ai, af, bq, kc, vc, ks, vs, kw, vw, bg = np.split(v["e_w_in"][0], np.cumsum(sizes)[:-1], axis=1)
    perm = np.concatenate([np.arange(HEAD) + (g * 4 + j) * HEAD for j in range(4) for g in range(2)])
    gates = np.zeros((D, P), np.float32)
    gates[:, 0:24], gates[:, 24:28], gates[:, 28:32] = bg, ai, af
    units = [*units_in(aq), *units_in(ak), *units_in(gates), *square_units(av, 512)]
    units += [*units_in(bq[:, perm]), *units_in(np.concatenate([kc, vc, ks, kw], axis=1))]
    units += [*square_units(np.concatenate([vs, vw], axis=1), 256), *units_in(ao)]
    for j in range(2):
        units += list(square_units(v["e_b_cmp_w1"][0, j], P))
    w_out = v["e_w_out"][0]
    units += list(units_in(np.concatenate([w_out[0:512], w_out[512:][perm]], axis=0)))
    units += first_tail_units(v, 0)

    cq, ckv, kr, ik, iw = np.split(v["o_w_in"][0], [512, 768, 832, 896], axis=1)
    units += list(units_in(np.concatenate([cq, ckv, kr, kr, ik, ik], axis=1)))
    weights = np.zeros((D, P), np.float32)
    weights[:, 0:8] = iw
    units += list(units_in(weights))
    qb = v["o_w_qb"][0].reshape(512, 8, P + HEAD)
    units += list(square_units(qb[:, :, 0:P].reshape(512, -1), P))
    units += list(square_units(qb[:, :, P:].reshape(512, -1), P))
    units += list(square_units(v["o_w_iq"][0], P))
    uk = v["o_w_uk"][0].transpose(1, 2, 0)
    units += list(uk.reshape(2, 4, P, 256).transpose(0, 2, 1, 3).reshape(2, P, UNIT))
    uv = v["o_w_uv"][0].reshape(2, P, 2, 4, P)
    units += list(uv.transpose(2, 1, 3, 0, 4).reshape(2, P, UNIT))
    units += list(units_in(v["o_w_out"][0]))
    units += first_tail_units(v, 1)
    return units


def first_tail_units(v, l):
    units = ffn_units([v["mlp_w1"][l]], v["mlp_w2"][l])
    gate, ple = list(units_in(v["ple_gate_w"][l])), list(square_units(v["ple_w"][l], P))
    return units + [ple[0], *gate[0:4], ple[1], *gate[4:8]]


def first_params(v):
    out = np.zeros((P, NCOL1), np.float32)

    def put(name, a, rows=slice(0, P)):
        out[rows, COL1[name][0]:COL1[name][1]] = a
    put("conv_w", channels(v["e_a_conv"][0]))
    put("a_norm", channels(v["e_a_norm"][0]))
    put("i_b", v["e_a_i_b"][0][:, None], slice(0, 4))
    put("f_b", v["e_a_f_b"][0][:, None], slice(0, 4))
    put("g_b", v["e_b_g_b"][0], slice(0, 1))
    put("cmp_pos", v["e_b_cmp_pos"][0].reshape(2, 16, P).transpose(2, 0, 1).reshape(P, 32))
    put("cmp_w2", v["e_b_cmp_w2"][0].transpose(1, 0, 2).reshape(P, P))
    put("q_norm", channels(v["o_q_norm"][0]))
    put("kv_norm", channels(v["o_kv_norm"][0]))
    put("ik_g", np.tile(v["o_ik_g"][0], 2)[:, None])
    put("ik_b", np.tile(v["o_ik_b"][0], 2)[:, None])
    for name in ("ln1_g", "ln1_b", "ln2_g", "ln2_b"):
        put(name, np.concatenate([channels(v[name][l]) for l in range(LAYERS)], axis=1))
    put("embed", v["p"][:, 0].reshape(LAYERS, T, 2, P).transpose(3, 0, 2, 1).reshape(P, -1))
    return out


def kernel(**inputs):
    import concourse.bacc as bacc
    from concourse.bass_utils import run_bass_kernel_spmd as run

    v = {n: np.asarray(a) for n, a in inputs.items()}
    v2 = {n[:-2]: a for n, a in v.items() if n.endswith("_2")}
    units = first_units(v) + [u for l in range(LAYERS) for u in second_units(v2, l)]
    arrays = {
        "x": np.ascontiguousarray(v["x"][0].T.reshape(KD, P, T).transpose(1, 0, 2)),
        "consts": constants(),
        "weights": np.stack(units),
        "params1": first_params(v),
        "positions": np.ascontiguousarray(v["positions"]),
        "params2": np.stack([second_params(v2, l) for l in range(LAYERS)]),
    }
    nc = bacc.Bacc("TRN2", target_bir_lowering=False, num_devices=1)
    args = [nc.dram_tensor(f"in_{n}", a.shape, mybir.dt.from_np(a.dtype), kind="ExternalInput").ap() for n, a in arrays.items()]
    out = nc.dram_tensor("out", (P, KD, T), F32, kind="ExternalOutput").ap()
    build(nc, *args, out)
    got = run(nc, [{f"in_{n}": a for n, a in arrays.items()}], core_ids=[0]).results[0]["out"]
    return np.ascontiguousarray(got.transpose(2, 1, 0).reshape(1, T, D))
```

```python
from contextlib import ExitStack

import numpy as np
from concourse import mybir

F32 = mybir.dt.float32
I32 = mybir.dt.int32
ALU = mybir.AluOpType
ACT = mybir.ActivationFunctionType
AX_X = mybir.AxisListType.X

P = 128
T = 256
D = 1024
KD = D // P
LAYERS = 2
PARTS = 4
HEAD = 64
RING = 12
UNIT = 1024
FF1, FF2 = 4 * D // P, 2816 // P
NEG = -1e30
ARENA = 25600

PROJ2 = 21
CHUNK = 64
NCHUNK = T // CHUNK
DECAY = float(np.exp(np.float32(-0.5)))
UNITS2 = 2 * 3 * FF2 + PROJ2 + KD
PAD2 = -UNITS2 % RING
UNITS2 += PAD2
SCW, CMW = 3, 31
RMS_EPS, LN_EPS = 1e-6, 1e-5
GN_EPS = 1e-5 * HEAD

A_CONV = 4
A_SCALE = float(P) ** -0.5
B_SCALE = float(HEAD) ** -0.5
C_SCALE = float(P + HEAD) ** -0.5
WI_SCALE = 8 ** -0.5 * HEAD ** -0.5
ALPHA = (2.0 * LAYERS) ** 0.25
TOPK = T // 4
TAKEN = -3e38
GELU = float(np.sqrt(2 / np.pi))
ROUND = 1.5 * 2.0 ** 23
PI = 3.1415925
TWO_PI = (6.28125, 1.9350051879882812e-3, float(2 * np.pi - 6.28125 - 1.9350051879882812e-3))
VEC1 = [("conv_w", 8 * A_CONV), ("a_norm", 4), ("i_b", 1), ("f_b", 1), ("g_b", 24), ("cmp_pos", 32), ("cmp_w2", P),
        ("q_norm", 4), ("kv_norm", 2), ("ik_g", 1), ("ik_b", 1), ("ln1_g", 16), ("ln1_b", 16), ("ln2_g", 16),
        ("ln2_b", 16), ("embed", 4 * T)]

VEC2 = [("ffn1_pre_g", 8), ("ffn1_post_g", 8), ("mix_pre_g", 8), ("mix_post_g", 8), ("ffn2_pre_g", 8),
        ("ffn2_post_g", 8), ("rk_mu", 7), ("rk_w0", 2), ("rk_a0", 2), ("rk_k_k", 2), ("rk_k_a", 2),
        ("rk_r_k", 2), ("rk_ln_w", 2), ("rk_ln_b", 2), ("sg_ln_w", 2), ("sg_ln_b", 2),
        ("cm_conv_b", 2), ("cm_ln_w", 2), ("cm_ln_b", 2),
        ("sc_conv_w", 2 * SCW), ("cm_conv_w", 2 * CMW), ("lora_up", 256), ("sg_w", 4 * P), ("sg_b", P)]
CONST = [("ident", P), ("ones", P), ("block64", P), ("near_st", P), ("near_ts", P), ("far_st", P),
         ("before_st", P), ("upto_st", P), ("tril_st", P), ("restart", 2 * T), ("headsel", 2 * P), ("eps", 8),
         ("causal_st", P), ("causal_qk", P), ("cmp_mask", 32), ("head4", 4 * P), ("swap64", P), ("swap32", P),
         ("inv_freq", 2)]
EPS = {RMS_EPS: 0, LN_EPS: 1, GN_EPS: 2, 1.0: 3}


def columns(table):
    at, out = 0, {}
    for name, width in table:
        out[name] = (at, at + width)
        at += width
    return out, at


COL1, NCOL1 = columns(VEC1)
COL2, NCOL2 = columns(VEC2)
COLC, NCOLC = columns(CONST)

PER_LAYER = {"unit": UNITS2, "hidden": 2 * FF2, "norm": 6, "pre": 3, "x": 3 * PARTS, "proj": PROJ2, "acc": 3,
             "even": (PROJ2 + 1) // 2, "odd": PROJ2 // 2}


class Steps:

    def __init__(self, sem, labels):
        labels = labels.split() if isinstance(labels, str) else labels
        assert len(set(labels)) == len(labels)
        self.sem, self.labels, self.marked = sem, labels, 0

    def mark(self, label):
        assert self.labels[self.marked] == label, (self.labels[self.marked], label)
        self.marked += 1
        return self.sem, 1

    def at(self, label, layer=0):
        return self.sem, self.labels.index(label) + 1 + layer * len(self.labels)


class Walk:

    def __init__(self):
        self.n = {k: 0 for k in PER_LAYER}
        self.layer, self.turn, self.per_turn = None, None, {}
        self.owed = 0

    def value(self, what, more=0, scale=1):
        v = (self.n[what] + more) * scale
        if self.layer is not None:
            v = v + self.layer * (PER_LAYER[what] * scale)
        if self.turn is not None and what in self.per_turn:
            v = v + self.turn * (self.per_turn[what] * scale)
        return v

    def filled(self):
        v = 16 * (self.n["unit"] // RING + 1)
        if self.layer is not None:
            v = v + self.layer * (16 * (PER_LAYER["unit"] // RING))
        if self.turn is not None:
            v = v + self.turn * (16 * (self.per_turn["unit"] // RING))
        return v

    def hidden_tiles(self, eng, first, last, per, tile):
        turns = (last - first) // per
        units = RING
        before = dict(self.n)
        with eng.Fori(0, turns) as turn:
            self.turn, self.per_turn = turn, {"unit": units, "hidden": per}
            for f in range(per):
                tile(first + f)
            self.turn = None
        for k in ("unit", "hidden"):
            added = self.n[k] - before[k]
            assert added in (0, self.per_turn[k]), (k, added)
            self.n[k] += added * (turns - 1)
        for f in range(first + turns * per, last):
            tile(f)


def bc(ap, n):
    return ap.unsqueeze(1).to_broadcast([ap.shape[0], n, ap.shape[1]])


def part_tiles(j):
    return range(j * KD // PARTS, (j + 1) * KD // PARTS)


def part(ap, j):
    return ap[:, j * KD // PARTS:(j + 1) * KD // PARTS, :]



class Core:

    def __init__(self, nc, ctx):
        self.nc, self.ctx = nc, ctx
        self.const = self.sb("const", NCOLC)
        self.ring = self.sb("ring", RING * UNIT).rearrange("p (r c) -> p r c", r=RING)
        self.x = self.tiles("x", KD)
        self.h = self.tiles("h", KD)
        self.sq = self.tiles("sq", KD)
        self.tmp = self.tiles("tmp", KD)
        self.cat = self.tiles("cat", KD)
        self.std = self.tiles("std", 2)
        self.rstd = self.tiles("rstd", 2)
        self.hid_act = self.tiles("hid_act", 2)
        self.hid = self.tiles("hid", 2)
        self.psum = ctx.enter_context(nc.psum_tensor("psum", [P, 8, 512], F32))
        self.acc = self.psum[:, 0:4, :].rearrange("p b (h t) -> p (b h) t", t=T)
        self.x_loaded = self.sem("x_loaded")
        self.load = self.sem("consts_loaded")
        self.filled = [self.sem(f"ring_filled{i}") for i in range(RING)]
        self.freed = self.sem("ring_units_freed")
        self.x_ready = self.sem("x_ready")
        self.h_ready = self.sem("h_ready")
        self.sq_ready = self.sem("sq_ready")
        self.sum_ready = self.sem("sum_ready")
        self.std_ready = self.sem("std_ready")
        self.proj_ready = self.sem("proj_ready")
        self.even_out = self.sem("even_out")
        self.odd_out = self.sem("odd_out")
        self.pre_ready = self.sem("pre_ready")
        self.act_ready = self.sem("act_ready")
        self.hid_ready = self.sem("hid_ready")
        self.acc_ready = self.sem("acc_ready")
        self.saved = self.sem("output_saved")

    def sb(self, name, width, dtype=F32):
        return self.ctx.enter_context(self.nc.sbuf_tensor(name, [P, width], dtype))[:, :]

    def tiles(self, name, n, width=T):
        return self.sb(name, n * width).rearrange("p (n t) -> p n t", n=n)

    def sem(self, name):
        return self.ctx.enter_context(self.nc.semaphore(name))

    def bank(self, i, width=T):
        return self.psum[:, i, :].rearrange("p (n t) -> p n t", t=width)

    def c(self, name):
        a, b = COLC[name]
        return self.const[:, a:b]

    def eps(self, value):
        a = COLC["eps"][0] + EPS[value]
        return self.const[:, a:a + 1]


class Arena:

    def __init__(self, ap):
        self.ap, self.at, self.top = ap, 0, 0

    def sb(self, width):
        self.at += width
        self.top = max(self.top, self.at)
        assert self.at <= self.ap.shape[1], (self.at, self.ap.shape[1])
        return self.ap[:, self.at - width:self.at]

    def tiles(self, n, width=T):
        return self.sb(n * width).rearrange("p (n t) -> p n t", n=n)



def pe_unit(k, pe, w, products):
    slot = w.n["unit"] % RING
    pe.wait_ge(k.filled[slot], w.filled())
    unit = k.ring[:, slot, :].rearrange("p (k c) -> p k c", c=P)
    last = None
    for i, (out, part, rhs, start, stop) in enumerate(products):
        last = pe.matmul(out, unit[:, part, :], rhs, start=start, stop=stop, skip_group_check=True)
        if i == 0 and w.owed:
            last.then_inc(k.freed, w.owed)
            w.owed = 0
    w.n["unit"] += 1
    w.owed += 1
    return last


def pe_columns(k, pe, w, out, rhs, wait_tile=None):
    slot = w.n["unit"] % RING
    pe.wait_ge(k.filled[slot], w.filled())
    unit = k.ring[:, slot, :].rearrange("p (k c) -> p k c", c=P)
    last = None
    for i in range(KD):
        if wait_tile is not None:
            wait_tile(i)
        last = pe.matmul(out, unit[:, i, :], rhs[:, i, :], start=(i == 0), stop=(i == KD - 1),
                         skip_group_check=True)
        if i == 0 and w.owed:
            last.then_inc(k.freed, w.owed)
            w.owed = 0
    w.n["unit"] += 1
    w.owed += 1
    return last


def pe_ffn(k, pe, w, rhs, tiles, gated, wait_tile):
    def into(f, wait=None):
        halves_of_bank = k.bank(4 + f % 2)
        for j in range(1 + gated):
            last = pe_columns(k, pe, w, halves_of_bank[:, j, :], rhs, wait if j == 0 else None)
        last.then_inc(k.pre_ready, 1)

    def step(f):
        into(f)
        pe.wait_ge(k.hid_ready, w.value("hidden"))
        pe_unit(k, pe, w, [(k.acc[:, n, :], n, k.hid[:, (f - 1) % 2, :], False, False) for n in range(KD)])
        w.n["hidden"] += 1

    into(0, wait_tile)
    w.n["hidden"] += 1
    into(1)
    pe.wait_ge(k.hid_ready, w.value("hidden"))
    pe_unit(k, pe, w, [(k.acc[:, n, :], n, k.hid[:, 0, :], n % 2 == 0, False) for n in range(KD)])
    w.n["hidden"] += 1
    w.hidden_tiles(pe, 2, tiles, RING // (2 + gated), step)
    pe.wait_ge(k.hid_ready, w.value("hidden"))
    pe_unit(k, pe, w, [(k.acc[:, n, :], n, k.hid[:, (tiles - 1) % 2, :], False, True)
                       for n in range(KD)]).then_inc(k.acc_ready, 1)
    w.n["acc"] += 1


def act_ffn(k, act, w, tiles, func):
    def step(f):
        act.wait_ge(k.pre_ready, w.value("hidden", 1))
        act.activation(k.hid_act[:, f % 2, :], k.bank(4 + f % 2)[:, 0, :], func).then_inc(k.act_ready, 1)
        w.n["hidden"] += 1
    w.hidden_tiles(act, 0, tiles, 4 if tiles == FF2 else 6, step)


def dve_ffn(k, dve, w, tiles, gated):
    def step(f):
        dve.wait_ge(k.act_ready, w.value("hidden", 1))
        dve.tensor_tensor(k.hid[:, f % 2, :], k.bank(4 + f % 2)[:, int(gated), :], k.hid_act[:, f % 2, :],
                          ALU.mult).then_inc(k.hid_ready, 1)
        w.n["hidden"] += 1
    w.hidden_tiles(dve, 0, tiles, 4 if tiles == FF2 else 6, step)


def pe_square_sum(k, pe, w):
    for j in range(PARTS):
        pe.wait_ge(k.sq_ready, w.value("norm", scale=PARTS) + j + 1)
        for i in part_tiles(j):
            last = pe.matmul(k.bank(6)[:, 0, :], k.c("ones"), k.sq[:, i, :], start=(i == 0), stop=(i == KD - 1))
    last.then_inc(k.sum_ready, 1)
    w.n["norm"] += 1


def act_squares(k, act, w, src, wait_part):
    for j in range(PARTS):
        wait_part(j)
        act.activation(part(k.sq, j), part(src, j), ACT.Square).then_inc(k.sq_ready, 1)


def act_std(k, act, w, eps):
    act.wait_ge(k.sum_ready, w.value("norm", 1))
    act.activation(k.std[:, 0, :], k.bank(6)[:, 0, :], ACT.Sqrt, bias=k.eps(eps), scale=1.0 / D).then_inc(
        k.std_ready, 1)
    w.n["norm"] += 1


def dve_rstd(k, dve, w):
    dve.wait_ge(k.std_ready, w.value("norm", 1))
    dve.reciprocal(k.rstd[:, 0, :], k.std[:, 0, :])
    dve.drain()
    w.n["norm"] += 1



class Second:

    def __init__(self, k, arena):
        sb, tiles, sem = arena.sb, arena.tiles, k.sem
        self.par = sb(NCOL2)
        self.half_g = sb(2 * KD)
        self.one_less = sb(2)
        self.pc_raw = tiles(7, T + 1)
        self.pc = tiles(7)
        self.z = tiles(14)
        self.gx = tiles(2, T + SCW - 1)
        self.zs = tiles(2, T + CMW - 1)
        self.zd = tiles(2)
        self.pool_t = tiles(2)
        self.sz = tiles(2)
        self.lora = sb(T)
        self.sw, self.a, self.g = tiles(2), tiles(2), tiles(2)
        self.kk, self.kp = tiles(2), tiles(2)
        self.na = tiles(2)
        self.w1, self.nw, self.u = tiles(2), tiles(2), tiles(2)
        self.run, self.run_before, self.e_inv, self.e_before = self.w1, self.nw, self.u, self.na
        self.e = tiles(2)
        self.at, self.rt, self.bt, self.kt = tiles(2), tiles(2), tiles(2), tiles(2)
        self.v_tok, self.a_tok = tiles(2), tiles(2)
        self.b_tok, self.k_tok = tiles(2), tiles(2)
        idle = [buf[:, i:i + KD // 2, :].rearrange("p n t -> p (n t)").rearrange("p (q t) -> p q t", t=P)
                for buf in (k.h, k.sq, k.tmp) for i in (0, KD // 2)]
        self.m = idle + [tiles(8, P) for i in range(4)]
        spare = [m.rearrange("p q t -> p (q t)").rearrange("p (n t) -> p n t", t=T)[:, j:j + 2, :]
                 for m in self.m[6:10] for j in (0, 2)]
        self.state = sb(NCHUNK * P).rearrange("p (c t i) -> p c t i", c=NCHUNK, t=2)
        self.n = self.m[8:10]
        self.rkr = self.sw
        vsq, vc, vn, t2, _, _, self.y, kk_sq = spare
        self.vsq, self.vc, self.t2, self.vn = ({"vn": own, "zn": own, "on": late} for own, late in (
            (k.hid, vsq), (k.hid_act, vc), (k.cat[:, 4:6, :], t2), (k.cat[:, 6:8, :], vn)))
        self.vn_tok = self.kk
        self.kk_sq = kk_sq.rearrange("p n t -> p (n t)")
        self.sg_wt = sb(4 * P)
        self.grown = tiles(2, HEAD)
        self.padded = sem("zeros_written")
        self.params = sem("params_loaded")
        tt = lambda *names: [f"{n}.{i}" for n in names for i in range(2)]
        self.pe = Steps(sem("mixer_products"), [
            "lora", "kk_sum", "v_tok", "a_tok", "b_tok", "k_tok",
            *tt("before", "before_ts", "ak", "rb"), *tt("rk"), *tt("p2", "p2t"), "vn.sum", *tt("p4", "p4t", "n1"),
            *tt("p8"), "vn.sq", *tt("n2"), *tt("n3"), *tt("nd"), *tt("far"), "v_norm_tok", *tt("x1"), "spatial",
            *tt("x2"), *tt("x3"), "na", "w1", "nw",
            "s0", "zn.sum", "u1", "s1", "zn.sq", "u2", "s2", "u3", "out", "on.sum", "bonus", "on.sq"])
        self.act = Steps(sem("mixer_activations"), [
            "lora", "sz", "gates", "kk_std", "decays", "v_tok", "a_tok", "b_tok", "k_tok",
            *tt("p2"), *tt("p4", "p4t"), "vn.sq", *tt("p8"), "vn.std", *tt("nd"), *tt("far"), "v_norm_tok", "na",
            "zn.sq", "zn.std", "yd", "on.sq", "on.std"])
        self.dve = Steps(sem("mixer_elementwise"), [
            "lora_in", "kk_sq", "run", "decayed", "rkr",
            *tt("before", "far_st"), *tt("before_ts", "ak", "rb"), *tt("rk"), *tt("n0"), *tt("p2t"), "vn.xc", *tt("n1"),
            *tt("n2"), "vn", *tt("n3"), *tt("x1"), *tt("x2"), "yb", *tt("x3"), "zd", "w1", "nw",
            "s0", "zn.xc", "u1", "s1", "u2", "s2", "u3", "zn", "out", "on.xc", "yc"])
        self.pool = Steps(sem("mixer_convolutions"), "zd ya")

    def p(self, name, i=None, n=1):
        a, b = COL2[name]
        return self.par[:, a:b] if i is None else self.par[:, a + i:a + i + n]


def matrix(h, tt):
    return h % 2 * 4 + h // 2 * 2 + tt


def head_rows(h):
    return slice(HEAD * (h % 2), HEAD * (h % 2) + HEAD), h // 2


def proj2_out(s, n):
    return s.pc_raw[:, n, 1:T + 1] if n < 7 else s.z[:, n - 7, :]


def second_tensor(k, s, pe, w):
    def carry():
        return mm(k.psum[0:HEAD, 7, 511:512], k.c("ones")[:, 0:HEAD], k.c("ones")[:, 0:1])

    def tile_of_h(i):
        pe.wait_ge(k.h_ready, w.value("pre", scale=KD) + i + 1)

    def at(steps, label):
        return steps.at(label, l)

    def two_groups(label_pe, waits, bank, make):
        for half in range(2):
            for steps, label in waits:
                pe.wait_ge(*at(steps, f"{label}.{half}"))
            for j in range(4):
                last = make(half * 4 + j, j % 2, j // 2 * 2 + half, k.bank(bank + half, P)[:, j, :])
            last.then_inc(*s.pe.mark(f"{label_pe}.{half}"))

    def mm(out, lhsT, rhs, start=True, stop=True):
        return pe.matmul(out, lhsT, rhs, start=start, stop=stop, skip_group_check=True)

    def channel_sums(name, what, buf, matrix, bank):
        if what == "sq":
            pe.wait_ge(*at(s.act, f"{name}.sq"))
        if matrix == "ones":
            for i in range(2):
                last = mm(k.bank(bank)[:, 0, :], k.c("ones"), buf[:, i, :], i == 0, i == 1)
        else:
            last = mm(k.psum[:, bank, :], k.c("block64"), buf.rearrange("p n t -> p (n t)"))
        last.then_inc(*s.pe.mark(f"{name}.{what}"))

    carry().then_inc(k.freed, w.owed)
    w.owed = 0
    with pe.Fori(0, LAYERS) as l:
        w.layer = l
        start = dict(w.n)
        pe_square_sum(k, pe, w)
        pe_ffn(k, pe, w, k.h, FF2, True, tile_of_h)
        w.n["pre"] += 1
        pe_square_sum(k, pe, w)
        def low_rank():
            pe.wait_ge(*at(s.act, "lora"))
            pe.wait_ge(*at(s.dve, "lora_in"))
            up = s.p("lora_up")
            for i in range(2):
                mm(k.bank(0)[:, i, :], up[0:32, i * P:i * P + P], s.lora[0:32, :])
                mm(k.bank(1)[:, i, :], up[32:64, i * P:i * P + P], s.pc[32:64, 6, :])
                last = mm(k.bank(2)[:, i, :], up[64:128, i * P:i * P + P], s.lora[64:128, :])
            last.then_inc(*s.pe.mark("lora"))
            pe.wait_ge(*at(s.dve, "kk_sq"))
            mm(k.psum[:, 3, :], k.c("block64"), s.kk_sq).then_inc(*s.pe.mark("kk_sum"))

        pe_square_sum(k, pe, w)
        for n in range(PROJ2):
            if n >= 4:
                pe.wait_ge(k.even_out if n % 2 == 0 else k.odd_out,
                           w.value("even" if n % 2 == 0 else "odd", (n - 4) // 2 + 1))
            pe_columns(k, pe, w, k.bank(4 + n % 4)[:, 0, :], k.h,
                       tile_of_h if n == 0 else None).then_inc(k.proj_ready, 1)
            if n == 9:
                low_rank()
        w.n["pre"] += 1
        w.n["even"] += (PROJ2 + 1) // 2
        w.n["odd"] += PROJ2 // 2

        def turn(src, bank, label):
            for tt in range(2):
                for i in range(2):
                    last = pe.transpose(k.bank(bank, P)[:, tt * 2 + i, :], src[:, i, tt * P:tt * P + P], k.c("ident"))
            last.then_inc(*s.pe.mark(label))
        pe.wait_ge(k.even_out, w.value("even"))
        pe.wait_ge(k.odd_out, w.value("odd"))
        turn(s.pc[:, 4:6, :], 4, "v_tok")
        pe.wait_ge(*at(s.dve, "decayed"))
        turn(s.at, 5, "a_tok")
        turn(s.bt, 6, "b_tok")
        turn(s.kt, 7, "k_tok")

        def pair(left, right):
            def make(q, tt, h, out):
                rows, i = head_rows(h)
                tok = slice(tt * P, tt * P + P)
                return mm(out, left[rows, i, tok], right[rows, i, tok])
            return make
        pe.wait_ge(*at(s.act, "decays"))
        two_groups("before", [], 0, pair(s.bt, s.at))
        two_groups("before_ts", [], 2, pair(s.at, s.bt))
        pe.wait_ge(*at(s.act, "k_tok"))
        two_groups("ak", [], 4, pair(s.kt, s.at))
        two_groups("rb", [], 6, pair(s.bt, s.rt))
        two_groups("rk", [(s.dve, "far_st")], 0, pair(s.kt, s.rt))

        m = s.m
        def prod(left, right):
            return lambda q, tt, h, out: mm(out, left[:, q, :], right[:, q, :])
        two_groups("p2", [(s.dve, "before_ts")], 2, prod(m[1], m[0]))
        two_groups("p2t", [(s.dve, "ak")], 4, prod(m[0], m[1]))
        pe.wait_ge(*at(s.dve, "rk.1"))
        channel_sums("vn", "sum", s.z[:, 10:12, :], "ones", 0)
        two_groups("p4", [(s.act, "p2"), (s.dve, "p2t")], 2, prod(m[3], m[2]))
        two_groups("p4t", [], 4, prod(m[2], m[3]))
        two_groups("n1", [(s.dve, "rb"), (s.dve, "n0")], 6, prod(m[2], s.n[0]))
        two_groups("p8", [(s.act, "p4"), (s.act, "p4t")], 2, prod(m[1], m[0]))
        channel_sums("vn", "sq", s.vsq["vn"], "ones", 1)
        two_groups("n2", [(s.dve, "n1")], 6, prod(m[0], s.n[1]))
        two_groups("n3", [(s.act, "p8"), (s.dve, "n2")], 6, prod(m[2], s.n[0]))
        for tt in range(2):
            pe.wait_ge(*at(s.dve, f"n3.{tt}"))
            for j in range(4):
                last = pe.transpose(k.bank(2 + tt, P)[:, j, :], s.n[1][:, tt * 4 + j, :], k.c("ident"))
            last.then_inc(*s.pe.mark(f"nd.{tt}"))
        two_groups("far", [(s.act, "nd")], 4, prod(m[4], m[0]))
        pe.wait_ge(*at(s.dve, "vn"))
        for c in range(2):
            for i in range(2):
                last = pe.transpose(k.bank(0, P)[:, c * 2 + i, :], s.vn["vn"][:, i, c * P:c * P + P], k.c("ident"))
        last.then_inc(*s.pe.mark("v_norm_tok"))
        two_groups("x1", [(s.act, "far")], 6, prod(m[3], s.n[1]))
        pe.wait_ge(*at(s.act, "v_norm_tok"))
        for i in range(2):
            for c in range(2):
                out = k.bank(1)[:, i, c * P:c * P + P]
                mm(out, k.c("headsel")[0:4, i * P:i * P + P], s.p("sg_b")[0:4, :], True, False)
                for h in (2 * i, 2 * i + 1):
                    rows, _ = head_rows(h)
                    last = mm(k.bank(1)[rows, i, c * P:c * P + P], s.vn_tok[:, c, h * HEAD:h * HEAD + HEAD],
                              s.sg_wt[:, h * P:h * P + P], False, True)
        last.then_inc(*s.pe.mark("spatial"))
        two_groups("x2", [(s.dve, "x1")], 6, prod(m[3], s.n[0]))
        two_groups("x3", [(s.dve, "x2")], 6, prod(m[3], m[1]))

        pe.wait_ge(*at(s.dve, "x3.1"))
        for h in range(4):
            rows, i = head_rows(h)
            for tt in range(2):
                last = mm(k.bank(2)[rows, i, tt * P:tt * P + P], s.a_tok[:, tt, h * HEAD:h * HEAD + HEAD],
                          s.n[0][:, matrix(h, tt), :])
        last.then_inc(*s.pe.mark("na"))
        for tt in range(2):
            for h in range(4):
                last = mm(k.bank(3)[:, tt, h * HEAD:h * HEAD + HEAD], m[5][:, matrix(h, tt), :],
                          s.v_tok[:, tt, h * HEAD:h * HEAD + HEAD])
        last.then_inc(*s.pe.mark("w1"))
        pe.wait_ge(*at(s.dve, "w1"))
        for tt in range(2):
            for h in range(4):
                last = mm(k.bank(4)[:, tt, h * HEAD:h * HEAD + HEAD], s.n[0][:, matrix(h, tt), :],
                          s.w1[:, tt, h * HEAD:h * HEAD + HEAD])
        last.then_inc(*s.pe.mark("nw"))

        def chunk_rows(c):
            return slice(CHUNK * (c % 2), CHUNK * (c % 2) + CHUNK), c // 2
        for c in range(NCHUNK):
            tok, tt = chunk_rows(c)
            if c == 0:
                pe.wait_ge(*at(s.dve, "nw"))
                pe.wait_ge(*at(s.act, "na"))
                carry()
            else:
                pe.wait_ge(*at(s.dve, f"s{c - 1}"))
                carry()
                for h in range(4):
                    rows, i = head_rows(h)
                    last = mm(k.psum[tok, 4 + h % 2, i * HEAD:i * HEAD + HEAD], s.na[rows, i, c * CHUNK:c * CHUNK + CHUNK],
                              s.state[rows, c, i, :])
                last.then_inc(*s.pe.mark(f"u{c}"))
            if c < NCHUNK - 1:
                if c > 0:
                    pe.wait_ge(*at(s.dve, f"u{c}"))
                    carry()
                for h in range(4):
                    rows, i = head_rows(h)
                    cols = slice(h * HEAD, h * HEAD + HEAD)
                    out = k.psum[rows, 6, i * HEAD:i * HEAD + HEAD]
                    mm(out, s.k_tok[tok, tt, cols], s.v_tok[tok, tt, cols], True, False)
                    last = mm(out, s.b_tok[tok, tt, cols], (s.nw if c == 0 else s.u)[tok, tt, cols], False, True)
                last.then_inc(*s.pe.mark(f"s{c}"))
            if c == 0:
                pe.wait_ge(*at(s.pool, "zd"))
                pe.wait_ge(*at(s.dve, "zd"))
                channel_sums("zn", "sum", s.zd, "ones", 0)
            if c == 1:
                channel_sums("zn", "sq", s.vsq["zn"], "ones", 1)
        pe.wait_ge(*at(s.dve, "u3"))
        for h in range(4):
            rows, i = head_rows(h)
            cols = slice(h * HEAD, h * HEAD + HEAD)
            for tt in range(2):
                out = k.bank(7)[rows, i, tt * P:tt * P + P]
                mm(out, s.u[:, tt, cols], m[6][:, matrix(h, tt), :], True, False)
                last = mm(out, s.v_tok[:, tt, cols], m[7][:, matrix(h, tt), :], False, False)
                for c in (2 * tt, 2 * tt + 1):
                    if c > 0:
                        t = slice(c * CHUNK, c * CHUNK + CHUNK)
                        last = mm(k.bank(7)[rows, i, t], s.state[rows, c, i, :], s.rt[rows, i, t], False,
                                  c == 2 * tt + 1)
        last.then_inc(*s.pe.mark("out"))

        held = []

        def open_output(first, last):
            for n in range(first, last):
                slot = w.n["unit"] % RING
                pe.wait_ge(k.filled[slot], w.filled())
                w.n["unit"] += 1
                held.append(k.ring[:, slot, :].rearrange("p (k c) -> p k c", c=P))
                for i in (0, 1, 2, 3, 6, 7):
                    ins = mm(k.acc[:, n, :], held[n][:, i, :], k.cat[:, i, :], i == 0 and n % 2 == 0, False)
                    if n == 0 and i == 0:
                        ins.then_inc(k.freed, w.owed)
                        w.owed = 0
        pe.wait_ge(*at(s.pool, "ya"))
        pe.wait_ge(*at(s.act, "yd"))
        open_output(0, 1)
        pe.wait_ge(*at(s.dve, "out"))
        channel_sums("on", "sum", s.y, "block64", 4)
        mm(k.psum[:, 6, :], k.c("block64"), s.rkr.rearrange("p n t -> p (n t)")).then_inc(*s.pe.mark("bonus"))
        open_output(1, 2)
        channel_sums("on", "sq", s.vsq["on"], "block64", 5)
        open_output(2, KD)
        pe.wait_ge(*at(s.dve, "yc"))
        for n in range(KD):
            for i in (4, 5):
                last = mm(k.acc[:, n, :], held[n][:, i, :], k.cat[:, i, :], False, i == 5)
                if n > 0 and i == 4:
                    last.then_inc(k.freed, 1)
        w.owed = 1
        last.then_inc(k.acc_ready, 1)
        w.n["acc"] += 1
        pe_square_sum(k, pe, w)
        pe_square_sum(k, pe, w)
        pe_ffn(k, pe, w, k.h, FF2, True, tile_of_h)
        w.n["pre"] += 1
        pe_square_sum(k, pe, w)
        for _ in range(PAD2):
            pe.wait_ge(k.filled[w.n["unit"] % RING], w.filled())
            w.n["unit"] += 1
        carry().then_inc(k.freed, w.owed + PAD2)
        w.owed = 0
        assert all(w.n[x] - start[x] == PER_LAYER[x] for x in ("unit", "hidden", "norm", "pre")), (w.n, start)
    w.layer = None


def second_scalar(k, s, act, w):
    def at(steps, label):
        return steps.at(label, l)

    def norm_of_x():
        def ready(j):
            act.wait_ge(k.x_ready, w.value("x") + j + 1)
        act_squares(k, act, w, k.x, ready)
        act_std(k, act, w, RMS_EPS)

    def norm_of_acc():
        def ready(j):
            if j == 0:
                act.wait_ge(k.acc_ready, w.value("acc", 1))
        act_squares(k, act, w, k.acc, ready)
        act_std(k, act, w, RMS_EPS)
        w.n["acc"] += 1
        w.n["x"] += PARTS

    def square(name):
        act.wait_ge(*at(s.dve, f"{name}.xc"))
        act.activation(s.vsq[name], s.vc[name], ACT.Square).then_inc(*s.act.mark(f"{name}.sq"))

    def deviation(name, bank, size, eps):
        act.wait_ge(*at(s.pe, f"{name}.sq"))
        n = 1 if size == T else 2
        act.activation(k.std[:, 0:n, :], k.bank(bank)[:, 0:n, :], ACT.Sqrt, bias=k.eps(eps),
                       scale=1.0 / size).then_inc(*s.act.mark(f"{name}.std"))

    def small_norm(name, bank, size, eps):
        square(name)
        deviation(name, bank, size, eps)

    def copy_bank(bank, out, label):
        act.wait_ge(*at(s.pe, label))
        act.activation(out, k.psum[:, bank, :], ACT.Copy).then_inc(*s.act.mark(label))

    flat = lambda x: x.rearrange("p n t -> p (n t)")
    with act.Fori(0, LAYERS) as l:
        w.layer = l
        norm_of_x()
        act_ffn(k, act, w, FF2, ACT.Silu)
        norm_of_acc()
        norm_of_x()
        act.wait_ge(s.params, (l + 1) * 16)

        def tiles_out(first, last):
            for n in range(first, last, 2):
                act.wait_ge(k.proj_ready, w.value("proj", n + 1))
                act.activation(proj2_out(s, n), k.bank(4 + n % 4)[:, 0, :], ACT.Copy).then_inc(k.even_out, 1)
        tiles_out(0, 10)
        act.wait_ge(*at(s.dve, "lora_in"))
        act.activation(s.lora[0:32, :], s.pc[0:32, 6, :], ACT.Tanh)
        act.activation(s.lora[64:128, :], s.pc[64:128, 6, :], ACT.Sigmoid).then_inc(*s.act.mark("lora"))
        tiles_out(10, 12)
        act.drain()
        act.wait_ge(k.odd_out, w.value("odd", 5))
        act.activation(s.sz, s.z[:, 2:4, :], ACT.Sigmoid).then_inc(*s.act.mark("sz"))
        act.wait_ge(*at(s.pe, "lora"))
        for i in range(2):
            act.activation(s.sw[:, i, :], k.bank(0)[:, i, :], ACT.Sigmoid, bias=s.p("rk_w0", i))
            act.activation(s.a[:, i, :], k.bank(1)[:, i, :], ACT.Sigmoid, bias=s.p("rk_a0", i))
        act.activation(s.g, k.bank(2), ACT.Copy).then_inc(*s.act.mark("gates"))
        act.wait_ge(*at(s.pe, "kk_sum"))
        act.activation(k.std, k.bank(3), ACT.Sqrt).then_inc(*s.act.mark("kk_std"))
        tiles_out(12, 16)
        act.wait_ge(*at(s.dve, "run"))
        act.activation(s.e, s.run, ACT.Exp, scale=-DECAY)
        act.activation(s.e_inv, s.run, ACT.Exp, scale=DECAY)
        act.activation(s.e_before, s.run_before, ACT.Exp, scale=-DECAY).then_inc(*s.act.mark("decays"))
        tiles_out(16, PROJ2)
        act.wait_ge(k.odd_out, w.value("odd", PROJ2 // 2))
        w.n["proj"] += PROJ2
        w.n["odd"] += PROJ2 // 2
        copy_bank(4, flat(s.v_tok), "v_tok")
        copy_bank(5, flat(s.a_tok), "a_tok")
        copy_bank(6, flat(s.b_tok), "b_tok")
        copy_bank(7, flat(s.k_tok), "k_tok")

        def copy(label, bank, out):
            for tt in range(2):
                act.wait_ge(*at(s.pe, f"{label}.{tt}"))
                act.activation(out[:, tt * 4:tt * 4 + 4, :], k.bank(bank + tt, P), ACT.Copy).then_inc(
                    *s.act.mark(f"{label}.{tt}"))
        copy("p2", 2, s.m[2])
        act.wait_ge(*at(s.pe, "p2t.1"))
        copy("p4", 2, s.m[0])
        copy("p4t", 4, s.m[1])
        square("vn")
        act.wait_ge(*at(s.pe, "n1.1"))
        copy("p8", 2, s.m[2])
        deviation("vn", 1, T, LN_EPS)
        act.wait_ge(*at(s.pe, "n2.1"))
        copy("nd", 2, s.m[0])
        copy("far", 4, s.m[3])
        copy_bank(0, flat(s.vn_tok), "v_norm_tok")
        act.wait_ge(*at(s.pe, "na"))
        act.activation(s.na, k.bank(2), ACT.Copy).then_inc(*s.act.mark("na"))

        small_norm("zn", 1, T, LN_EPS)
        act.wait_ge(*at(s.dve, "zn"))
        act.activation(k.cat[:, 6:8, :], s.vn["zn"], ACT.Silu).then_inc(*s.act.mark("yd"))
        small_norm("on", 5, HEAD, GN_EPS)
        norm_of_acc()
        norm_of_x()
        act_ffn(k, act, w, FF2, ACT.Silu)
        norm_of_acc()
    w.layer = None


def second_vector(k, s, dve, w):
    def at(steps, label):
        return steps.at(label, l)

    def pre_norm(gain):
        dve_rstd(k, dve, w)
        for i in range(KD):
            dve.scalar_tensor_tensor(k.h[:, i, :], k.x[:, i, :], s.p(gain, i), k.rstd[:, 0, :],
                                     ALU.mult, ALU.mult).then_inc(k.h_ready, 1)

    def post_norm(gain):
        dve_rstd(k, dve, w)
        for j in range(PARTS):
            for i in part_tiles(j):
                dve.scalar_tensor_tensor(k.tmp[:, i, :], k.acc[:, i, :], gain[:, i:i + 1], k.rstd[:, 0, :],
                                         ALU.mult, ALU.mult)
            dve.drain()
            dve.tensor_tensor(part(k.x, j), part(k.x, j), part(k.tmp, j), ALU.add).then_inc(k.x_ready, 1)
        dve.drain()

    def centre(name, src, bank, size):
        dve.wait_ge(*at(s.pe, f"{name}.sum"))
        mean = bc(k.bank(bank)[:, 0, :], 2) if size == T else k.bank(bank)
        dve.scalar_tensor_tensor(s.vc[name], mean, -1.0 / size, src, ALU.mult, ALU.add).then_inc(
            *s.dve.mark(f"{name}.xc"))

    def scaled(name, size, gain, bias):
        whole = size == T
        dve.wait_ge(*at(s.act, f"{name}.std"))
        n = 1 if whole else 2
        dve.reciprocal(k.rstd[:, 0:n, :], k.std[:, 0:n, :])
        dve.drain()
        for i in range(2):
            dve.scalar_tensor_tensor(s.t2[name][:, i, :], s.vc[name][:, i, :], s.p(gain, i), k.rstd[:, 0 if whole else i, :],
                                     ALU.mult, ALU.mult)
        dve.drain()
        for i in range(2):
            last = dve.tensor_scalar(s.vn[name][:, i, :], s.t2[name][:, i, :], s.p(bias, i), None, ALU.add)
        return last

    flat = lambda x: x.rearrange("p n t -> p (n t)")
    dve.memset(s.pc_raw[:, :, 0:1], 0.0)
    dve.memset(s.gx[:, :, 0:SCW - 1], 0.0)
    dve.memset(s.zs[:, :, 0:CMW - 1], 0.0).then_inc(s.padded, 1)
    with dve.Fori(0, LAYERS) as l:
        w.layer = l
        dve.wait_ge(s.params, (l + 1) * 16)
        for i, name in enumerate(("ffn1_post_g", "ffn2_post_g")):
            dve.tensor_scalar(s.half_g[:, i * KD:i * KD + KD], s.p(name), 0.5, None, ALU.mult)
        dve.tensor_scalar(s.one_less, s.p("rk_k_a"), -1.0, 1.0, ALU.mult, ALU.add)
        dve.tensor_tensor(s.sg_wt.rearrange("p (h t) -> p h t", h=4), s.p("sg_w").rearrange("p (h t) -> p h t", h=4),
                          bc(k.c("tril_st"), 4), ALU.mult)
        pre_norm("ffn1_pre_g")
        dve_ffn(k, dve, w, FF2, True)
        post_norm(s.half_g[:, 0:KD])
        pre_norm("mix_pre_g")

        def tiles_out(first, last):
            for n in range(first, last, 2):
                dve.wait_ge(k.proj_ready, w.value("proj", n + 1))
                dve.tensor_copy(proj2_out(s, n), k.bank(4 + n % 4)[:, 0, :]).then_inc(k.odd_out, 1)
        tiles_out(1, 7)
        dve.drain()
        dve.wait_ge(k.even_out, w.value("even", 4))

        now, before = s.pc_raw[:, :, 1:T + 1], s.pc_raw[:, :, 0:T]
        dve.tensor_tensor(k.tmp[:, 0:7, :], before, now, ALU.subtract)
        dve.drain()
        for j in (6, 0, 1, 2, 3, 4, 5):
            last = dve.scalar_tensor_tensor(s.pc[:, j, :], k.tmp[:, j, :], s.p("rk_mu", j), now[:, j, :],
                                            ALU.mult, ALU.add)
            if j == 6:
                last.then_inc(*s.dve.mark("lora_in"))
        dve.drain()
        for i in range(2):
            dve.tensor_scalar(s.kk[:, i, :], s.pc[:, 2 + i, :], s.p("rk_k_k", i), None, ALU.mult)
        dve.drain()
        dve.tensor_tensor(s.kk_sq, flat(s.kk), flat(s.kk), ALU.mult).then_inc(*s.dve.mark("kk_sq"))
        tiles_out(7, 11)
        dve.wait_ge(*at(s.act, "gates"))
        dve.tensor_tensor_scan(flat(s.run), k.c("restart"), flat(s.sw), 0.0, ALU.mult, ALU.add)
        dve.drain()
        dve.tensor_tensor(s.run_before, s.run, s.sw, ALU.subtract).then_inc(*s.dve.mark("run"))
        for i in range(2):
            dve.tensor_scalar(s.kp[:, i, :], s.a[:, i, :], s.p("rk_k_a", i), s.one_less[:, i:i + 1],
                              ALU.mult, ALU.add)
        dve.drain()
        dve.tensor_tensor(s.kp, s.kp, s.pc[:, 2:4, :], ALU.mult)
        dve.wait_ge(*at(s.act, "kk_std"))
        dve.tensor_scalar(k.rstd, k.std, 1e-12, None, ALU.max)
        dve.drain()
        dve.reciprocal(k.rstd, k.rstd)
        dve.drain()
        dve.tensor_tensor(s.kk, s.kk, k.rstd, ALU.mult)
        dve.drain()
        dve.tensor_tensor(s.a, s.kk, s.a, ALU.mult)
        tiles_out(11, 15)
        dve.wait_ge(*at(s.act, "decays"))
        dve.scalar_tensor_tensor(s.at, s.kk, -1.0, s.e_before, ALU.mult, ALU.mult)
        dve.tensor_tensor(s.kt, s.kp, s.e_inv, ALU.mult)
        dve.tensor_tensor(s.rt, s.pc[:, 0:2, :], s.e, ALU.mult)
        dve.drain()
        dve.tensor_tensor(s.bt, s.a, s.e_inv, ALU.mult).then_inc(*s.dve.mark("decayed"))
        for i in range(2):
            last = dve.scalar_tensor_tensor(s.rkr[:, i, :], s.pc[:, i, :], s.p("rk_r_k", i), s.kp[:, i, :],
                                            ALU.mult, ALU.mult)
        last.then_inc(*s.dve.mark("rkr"))
        tiles_out(15, PROJ2)
        dve.drain()
        dve.wait_ge(k.even_out, w.value("even", (PROJ2 + 1) // 2))
        w.n["proj"] += PROJ2
        w.n["even"] += (PROJ2 + 1) // 2

        def masked(label, bank, outs):
            for tt in range(2):
                dve.wait_ge(*at(s.pe, f"{label}.{tt}"))
                for out, mask, mark in outs:
                    dve.tensor_tensor(out[:, tt * 4:tt * 4 + 4, :], k.bank(bank + tt, P), bc(k.c(mask), 4),
                                      ALU.mult).then_inc(*s.dve.mark(f"{mark}.{tt}"))
        m = s.m
        dve.wait_ge(*at(s.act, "sz"))
        dve.tensor_tensor(s.zs[:, 1, CMW - 1:], s.z[:, 1, :], s.sz[:, 1, :], ALU.mult)

        def taps(first, last):
            for j in range(first, last):
                weight, src, out = s.p("cm_conv_w", CMW + j), s.zs[:, 1, j:j + T], s.zd[:, 1, :]
                dve.drain()
                if j == 0:
                    ins = dve.tensor_scalar(out, src, weight, s.p("cm_conv_b", 1), ALU.mult, ALU.add)
                else:
                    ins = dve.scalar_tensor_tensor(out, src, weight, out, ALU.mult, ALU.add)
            return ins
        masked("before", 0, [(m[1], "near_st", "before")])
        masked("before", 0, [(m[4], "far_st", "far_st")])
        masked("before_ts", 2, [(m[0], "near_ts", "before_ts")])
        masked("ak", 4, [(m[5], "before_st", "ak")])
        masked("rb", 6, [(m[6], "upto_st", "rb")])
        masked("rk", 0, [(m[7], "upto_st", "rk")])
        dve.drain()
        for tt in range(2):
            dve.tensor_tensor(s.n[0][:, tt * 4:tt * 4 + 4, :], m[1][:, tt * 4:tt * 4 + 4, :], bc(k.c("ident"), 4),
                              ALU.add).then_inc(*s.dve.mark(f"n0.{tt}"))

        def add(label, bank, other, out):
            for tt in range(2):
                q = slice(tt * 4, tt * 4 + 4)
                dve.wait_ge(*at(s.pe, f"{label}.{tt}"))
                dve.tensor_tensor(out[:, q, :], k.bank(bank + tt, P), other[:, q, :], ALU.add).then_inc(
                    *s.dve.mark(f"{label}.{tt}"))
            dve.drain()
        taps(0, 3)
        for tt in range(2):
            dve.wait_ge(*at(s.pe, f"p2t.{tt}"))
            dve.tensor_copy(m[3][:, tt * 4:tt * 4 + 4, :], k.bank(4 + tt, P)).then_inc(*s.dve.mark(f"p2t.{tt}"))
        dve.drain()
        centre("vn", s.z[:, 10:12, :], 0, T)
        taps(3, 7)
        add("n1", 6, s.n[0], s.n[1])
        taps(7, 11)
        add("n2", 6, s.n[1], s.n[0])
        scaled("vn", T, "sg_ln_w", "sg_ln_b").then_inc(*s.dve.mark("vn"))
        taps(11, 15)
        add("n3", 6, s.n[0], s.n[1])
        taps(15, 19)
        add("x1", 6, s.n[1], s.n[0])
        taps(19, 23)
        add("x2", 6, s.n[1], m[1])
        dve.wait_ge(*at(s.pe, "spatial"))
        dve.tensor_tensor(k.cat[:, 2:4, :], s.z[:, 12:14, :], k.bank(1), ALU.mult).then_inc(*s.dve.mark("yb"))
        taps(23, 27)
        add("x3", 6, s.n[1], s.n[0])
        taps(27, CMW).then_inc(*s.dve.mark("zd"))
        dve.wait_ge(*at(s.pe, "w1"))
        dve.tensor_copy(s.w1, k.bank(3)).then_inc(*s.dve.mark("w1"))
        dve.wait_ge(*at(s.pe, "nw"))
        dve.tensor_copy(s.nw, k.bank(4)).then_inc(*s.dve.mark("nw"))
        dve.drain()
        dve.tensor_copy(s.u[0:CHUNK, 0, :], s.nw[0:CHUNK, 0, :])
        by_parity = lambda x: x.rearrange("p (i g d) -> p g i d", i=2, g=2)
        for c in range(NCHUNK):
            tok, tt = slice(CHUNK * (c % 2), CHUNK * (c % 2) + CHUNK), c // 2
            if c > 0:
                dve.wait_ge(*at(s.pe, f"u{c}"))
                dve.tensor_tensor(by_parity(s.u[tok, tt, :]), k.psum[tok, 4:6, 0:P].rearrange("p g (i d) -> p g i d", i=2),
                                  by_parity(s.nw[tok, tt, :]), ALU.add).then_inc(
                    *s.dve.mark(f"u{c}"))
            if c < NCHUNK - 1:
                end = c * CHUNK + CHUNK - 1
                dve.wait_ge(*at(s.pe, f"s{c}"))
                grown = k.psum[:, 6, 0:P].rearrange("p (t i) -> p t i", t=2)
                for i in range(2):
                    if c == 0:
                        last = dve.tensor_scalar(s.state[:, 1, i, :], grown[:, i, :], s.e[:, i, end:end + 1], None,
                                                 ALU.mult)
                    else:
                        dve.tensor_tensor(s.grown[:, i, 0:HEAD], grown[:, i, :], s.state[:, c, i, :], ALU.add)
                        dve.drain()
                        last = dve.tensor_scalar(s.state[:, c + 1, i, :], s.grown[:, i, 0:HEAD],
                                                 s.e[:, i, end:end + 1], None, ALU.mult)
                last.then_inc(*s.dve.mark(f"s{c}"))
                dve.drain()
            if c == 0:
                centre("zn", s.zd, 0, T)
        scaled("zn", T, "cm_ln_w", "cm_ln_b").then_inc(*s.dve.mark("zn"))
        dve.wait_ge(*at(s.pe, "out"))
        dve.tensor_copy(s.y, k.bank(7)).then_inc(*s.dve.mark("out"))

        dve.wait_ge(*at(s.act, "yd"))
        centre("on", s.y, 4, HEAD)
        dve.wait_ge(*at(s.pe, "bonus"))
        dve.tensor_tensor(s.rkr, k.bank(6), s.pc[:, 4:6, :], ALU.mult)
        scaled("on", HEAD, "rk_ln_w", "rk_ln_b")
        dve.drain()
        dve.tensor_tensor(s.rkr, s.rkr, s.vn["on"], ALU.add)
        dve.drain()
        dve.tensor_tensor(k.cat[:, 4:6, :], s.rkr, s.g, ALU.mult).then_inc(*s.dve.mark("yc"))
        post_norm(s.p("mix_post_g"))
        pre_norm("ffn2_pre_g")
        dve_ffn(k, dve, w, FF2, True)
        post_norm(s.half_g[:, KD:2 * KD])
    w.layer = None


def second_pool(k, s, pool, w, params):
    def at(steps, label):
        return steps.at(label, l)

    def conv(src, weights, taps, out, tiles):
        for i in range(tiles):
            pool.tensor_scalar(out[:, i, :], src[:, i, 0:T], s.p(weights, i * taps), None, ALU.mult)
            for j in range(1, taps):
                pool.tensor_scalar(s.pool_t[:, j % 2, :], src[:, i, j:j + T], s.p(weights, i * taps + j), None,
                                   ALU.mult)
                pool.drain()
                last = pool.tensor_tensor(out[:, i, :], out[:, i, :], s.pool_t[:, j % 2, :], ALU.add)
        return last

    with pool.Fori(0, LAYERS) as l:
        w.layer = l
        pool.wait_ge(k.x_ready, w.value("x", PARTS))
        pool.dma_start(s.par, params[l]).then_inc(s.params, 16)
        pool.wait_ge(s.params, (l + 1) * 16)
        pool.wait_ge(s.padded, 1)
        pool.wait_ge(*at(s.act, "sz"))
        pool.tensor_tensor(s.zs[:, 0, CMW - 1:], s.z[:, 0, :], s.sz[:, 0, :], ALU.mult)
        pool.drain()
        conv(s.zs, "cm_conv_w", CMW, s.zd, 1)
        pool.drain()
        pool.tensor_scalar(s.zd[:, 0, :], s.zd[:, 0, :], s.p("cm_conv_b", 0), None, ALU.add).then_inc(
            *s.pool.mark("zd"))
        pool.wait_ge(k.even_out, w.value("even", (PROJ2 + 1) // 2))
        pool.wait_ge(k.odd_out, w.value("odd", PROJ2 // 2))
        pool.tensor_tensor(s.gx[:, :, SCW - 1:], s.z[:, 4:6, :], s.z[:, 6:8, :], ALU.mult)
        pool.drain()
        conv(s.gx, "sc_conv_w", SCW, k.cat, 2)
        pool.drain()
        pool.tensor_tensor(k.cat[:, 0:2, :], k.cat[:, 0:2, :], s.z[:, 8:10, :], ALU.mult).then_inc(
            *s.pool.mark("ya"))
    w.layer = None



class First:

    def __init__(self, k, arena):
        sem = k.sem
        a = arena
        self.par = a.sb(NCOL1)
        self.embed = self.p("embed").rearrange("p (n t) -> p n t", t=T)
        self.pos_i, self.pos = a.sb(T), a.sb(T)
        self.angle, self.turns, self.red = k.tmp[:, 0:2, :], k.tmp[:, 2:4, :], k.tmp[:, 4:6, :]
        self.cos, self.sin = a.tiles(2), a.tiles(2)
        both, a.top = a.at, a.at
        self.qk_raw = a.tiles(8, T + A_CONV - 1)
        self.qk = a.tiles(8)
        self.nq, self.kc, self.vc = a.tiles(4), a.tiles(1), a.tiles(1)
        self.ks, self.kw = a.tiles(1), a.tiles(1)
        self.o = a.tiles(4)
        self.v = a.tiles(2, 512)
        self.vsw = a.tiles(2, 2 * P)
        self.gate = a.tiles(2, 24)
        self.one = a.sb(T)
        self.gi, self.gf, self.gt, self.gl = a.sb(T), a.sb(T), a.sb(T), a.sb(T)
        self.cum, self.rows = a.sb(T), a.tiles(2)
        self.c_tok = a.tiles(2, 4)
        self.arg = [a.tiles(2, P) for _ in range(2)]
        self.e = [a.tiles(3, P) for _ in range(2)]
        self.pt = [a.tiles(3, P) for _ in range(2)]
        self.den = [a.sb(T) for _ in range(2)]
        self.hs = a.tiles(4)
        self.shift = a.tiles(4)
        self.win = a.tiles(2 * 16, 32)
        self.hid = a.tiles(2, 32)
        self.hid_t = a.tiles(2, 32)
        self.hid_v = a.tiles(8, HEAD)
        self.kcmp = a.sb(16)
        self.vcmp = a.tiles(8, HEAD)
        self.pc = a.tiles(16, 16)
        self.pm, self.ps = a.sb(16), a.sb(16)
        self.pct = a.tiles(2)
        a.at = both
        self.cq, self.ckv = a.tiles(4), a.tiles(2)
        self.cqn, self.ckvn = a.tiles(4), a.tiles(2)
        self.ik, self.ikc = a.tiles(1), a.tiles(1)
        self.iks = a.tiles(2)
        self.ckv_tok = a.tiles(2)
        self.rc, self.ri = a.tiles(5), a.tiles(5)
        self.rt = a.tiles(5)
        self.qn = a.tiles(8)
        self.q_abs = a.tiles(16)
        self.wi = a.tiles(2, 8)
        self.isc = a.sb(3 * P)
        self.work = [a.sb(3 * P) for _ in range(2)]
        self.relu = [a.sb(3 * P) for _ in range(2)]
        self.top = a.tiles(2, 8)
        self.sel = a.sb(3 * P)
        self.o_lat = [a.tiles(2) for _ in range(2)]
        a.at = max(a.at, a.top)
        self.prob = [a.sb(512) for _ in range(3)]
        self.prob_t = [a.sb(512) for _ in range(2)]
        self.nmax, self.bias, self.total, self.coef = (a.tiles(4, 2) for _ in range(4))

        self.y_ready = sem("sum_with_residual")
        self.mean_ready = sem("channel_sums")
        self.c_ready = sem("centred")
        self.t_ready = sem("scaled")
        self.ple_ready = sem("ple_products")
        self.gate_ready = sem("ple_gates")
        self.params = sem("first_params_loaded")
        self.angles = sem("angles_ready")
        self.ple_used = sem("ple_used")
        self.moved = sem("rows_moved")
        self.att_scores, self.att_max, self.att_exp, self.att_prob, self.att_turned, self.att_copied, self.att_out = (
            sem(f"attention_{n}") for n in ("scores", "max", "exp", "prob", "turned", "copied", "out"))
        self.pe = Steps(sem("even_products"),
                        "gates v vsw c_tok rows0 rows1 s0 s1 num0 s2 num1 s3 rows2 rows3 num2 num3 "
                        "hs.sum hid hs.sq cmp_kv cmp_scores cmp_t")
        self.act = Steps(sem("even_activations"),
                         "gate fl vsw qk sig c_tok rows e0 e1 den0 den1 e2 e3 den2 den3 "
                         "hs.sq hid_sq hid_tanh cmp_k cmp_exp cmp_t hs.std")
        self.dve = Steps(sem("even_elementwise"),
                         "v conv cmin rows shift arg0 arg1 pt0 pt1 h0 h1 arg2 arg3 pt2 pt3 h2 h3 "
                         "hs.xc win hid_in hid cmp_v cmp_max cmp out")
        self.ope = Steps(sem("odd_products"), [
            "iw", "sums", "ik_ss", "swap_i", *[f"i{h}" for h in range(8)], "swap_c", "turned",
            *[f"lat{h}" for h in range(8)]])
        self.oact = Steps(sem("odd_activations"), [
            "std", "ik_std", *[f"r{h}" for h in range(8)], *[f"up{h}" for h in range(8)]])
        self.odve = Steps(sem("odd_elementwise"), [
            "sq", "ik_sq", "cqn", "ikn", "rope_i", *[f"acc{h}" for h in range(8)], "rope_c", "turned", "sel",
            *[f"lat{h}" for h in range(8)]])

    def p(self, name, i=None, n=1):
        a, b = COL1[name]
        return self.par[:, a:b] if i is None else self.par[:, a + i:a + i + n]


def pe_next_tile(k, pe, w):
    t = w.n["proj"]
    if t >= 4:
        pe.wait_ge(k.even_out if t % 2 == 0 else k.odd_out, (t - 4) // 2 + 1)
    w.n["proj"] += 1
    return k.bank(4 + t % 4)[:, 0, :]


def pe_tiles(k, pe, w, tiles):
    slot = w.n["unit"] % RING
    pe.wait_ge(k.filled[slot], w.filled())
    unit = k.ring[:, slot, :].rearrange("p (k c) -> p k c", c=P)
    for products in tiles:
        out = pe_next_tile(k, pe, w)
        for i, (part, rhs) in enumerate(products):
            last = pe.matmul(out, unit[:, part, :], rhs, start=(i == 0), stop=(i == len(products) - 1),
                             skip_group_check=True)
            if i == 0 and w.owed and len(products) > 1:
                last.then_inc(k.freed, w.owed)
                w.owed = 0
        last.then_inc(k.proj_ready, 1)
    w.n["unit"] += 1
    w.owed += 1


def copy_tile(k, eng, w, t, out):
    eng.wait_ge(k.proj_ready, t + 1)
    src = k.bank(4 + t % 4)[:, 0, :]
    if t % 2 == 0:
        eng.activation(out, src, ACT.Copy).then_inc(k.even_out, 1)
    else:
        eng.tensor_copy(out, src).then_inc(k.odd_out, 1)


def even_tile_out(f, t):
    if t < 8:
        return f.qk_raw[:, t, A_CONV - 1:]
    if t < 12:
        return f.nq[:, t - 8, :]
    if t < 16:
        return (f.kc, f.vc, f.ks, f.kw)[t - 12][:, 0, :]
    return f.o[:, t - 16, :]



class Attention:

    def __init__(self, k, f, before, branches, scale):
        self.k, self.f, self.before, self.branches, self.scale = k, f, before, branches, scale

    def keys(self, tt):
        return P * (tt + 1)

    def scores(self, u, tt):
        n = self.keys(tt)
        return self.k.psum[:, u % 4, 0:self.branches * n].rearrange("p (b n) -> p b n", n=n)

    def p(self, u, tt):
        n = self.keys(tt)
        return self.f.prob[u % 3][:, 0:self.branches * n].rearrange("p (b n) -> p b n", n=n)

    def blocks(self, tt):
        return self.branches * (tt + 1)

    def scores_free(self, pe, u):
        if u >= 4:
            pe.wait_ge(self.f.att_exp, self.before + u - 3)

    def pe_turn(self, pe, u, tt):
        pe.wait_ge(self.f.att_prob, self.before + u + 1)
        if u >= 2:
            pe.wait_ge(self.f.att_copied, self.before + u - 1)
        for b in range(self.blocks(tt)):
            last = pe.transpose(self.k.psum[:, 4 + u % 2, b * P:b * P + P], self.f.prob[u % 3][:, b * P:b * P + P],
                                self.k.c("ident"))
        last.then_inc(self.f.att_turned, 1)

    def act_exp(self, act, u, tt):
        act.wait_ge(self.f.att_max, self.before + u + 1)
        if u >= 3:
            act.wait_ge(self.f.att_turned, self.before + u - 2)
        for b in range(self.branches):
            last = act.activation(self.p(u, tt)[:, b, :], self.scores(u, tt)[:, b, :], ACT.Exp,
                                  bias=self.f.bias[:, u % 4, b:b + 1], scale=self.scale,
                                  accum_out=self.f.total[:, u % 4, b:b + 1])
        last.then_inc(self.f.att_exp, 1)

    def act_copy(self, act, u, tt):
        act.wait_ge(self.f.att_turned, self.before + u + 1)
        if u >= 2:
            act.wait_ge(self.f.att_out, self.before + u - 1)
        n = self.blocks(tt) * P
        act.activation(self.f.prob_t[u % 2][:, 0:n], self.k.psum[:, 4 + u % 2, 0:n], ACT.Copy).then_inc(
            self.f.att_copied, 1)

    def dve_max(self, dve, u, tt):
        f, nb = self.f, self.branches
        dve.drain()
        dve.tensor_reduce(f.nmax[:, u % 4, 0:nb], self.scores(u, tt), AX_X, ALU.max, negate=True)
        dve.drain()
        dve.tensor_scalar(f.bias[:, u % 4, 0:nb], f.nmax[:, u % 4, 0:nb], self.scale, None, ALU.mult).then_inc(
            f.att_max, 1)

    def dve_prob(self, dve, u, tt, gate=None):
        f, nb = self.f, self.branches
        dve.wait_ge(f.att_exp, self.before + u + 1)
        coef = f.coef[:, u % 4, 0:nb]
        dve.reciprocal(coef, f.total[:, u % 4, 0:nb])
        dve.drain()
        if gate is not None:
            dve.tensor_tensor(coef, coef, gate, ALU.mult)
            dve.drain()
        dve.tensor_tensor(self.p(u, tt), self.p(u, tt),
                          coef.unsqueeze(2).to_broadcast([P, nb, self.keys(tt)]), ALU.mult).then_inc(f.att_prob, 1)


NSA_UNITS = [(g, j, tt) for tt in range(2) for j in range(4) for g in range(2)]
MLA_UNITS = [(h, tt) for h in range(8) for tt in range(2)]



def even_tensor(k, f, pe, w):
    def mm(out, lhsT, rhs, start=True, stop=True):
        return pe.matmul(out, lhsT, rhs, start=start, stop=stop, skip_group_check=True)

    def unit():
        slot = w.n["unit"] % RING
        pe.wait_ge(k.filled[slot], w.filled())
        w.n["unit"] += 1
        return k.ring[:, slot, :]

    def hand_back(ins):
        if w.owed:
            ins.then_inc(k.freed, w.owed)
        w.owed = 1

    def tiles(n):
        for _ in range(n):
            pe_columns(k, pe, w, pe_next_tile(k, pe, w), k.x).then_inc(k.proj_ready, 1)

    tiles(8)
    pe.wait_ge(k.load, 16)
    pe.wait_ge(f.params, 32)
    wt = unit().rearrange("p (k c) -> p k c", c=P)
    for i in range(KD):
        last = mm(k.psum[0:4, 3, 0:T], wt[:, i, 24:28], k.x[:, i, :], i == 0, i == KD - 1)
        if i == 0:
            hand_back(last)
    for i in range(KD):
        mm(k.psum[0:4, 3, T:2 * T], wt[:, i, 28:32], k.x[:, i, :], i == 0, i == KD - 1)
    for tt in range(2):
        out = k.psum[:, 2, tt * 24:tt * 24 + 24]
        mm(out, k.c("ones")[0:1, :], f.p("g_b")[0:1, :], True, False)
        for i in range(KD):
            last = mm(out, k.x[:, i, tt * P:tt * P + P], wt[:, i, 0:24], False, i == KD - 1)
    last.then_inc(*f.pe.mark("gates"))
    for j in range(4):
        wt = unit().rearrange("p (k c) -> p k c", c=512)
        for i in range(2):
            for tt in range(2):
                last = mm(k.psum[:, tt, :], k.x[:, 2 * j + i, tt * P:tt * P + P], wt[:, i, :], j + i == 0,
                          j == 3 and i == 1)
                if i + tt == 0:
                    hand_back(last)
    last.then_inc(*f.pe.mark("v"))
    tiles(8)
    pe.wait_ge(*f.act.at("gate"))
    for j in range(2):
        wt = unit().rearrange("p (k c) -> p k c", c=2 * P)
        for i in range(4):
            for tt in range(2):
                last = mm(k.bank(2)[:, tt, :], k.x[:, 4 * j + i, tt * P:tt * P + P], wt[:, i, :],
                          j + i + tt == 0, j == 1 and i == 3)
                if i + tt == 0:
                    hand_back(last)
    last.then_inc(*f.pe.mark("vsw"))
    tiles(4)

    pe.wait_ge(*f.dve.at("cmin"))
    for tt in range(2):
        last = pe.transpose(k.psum[:, 3, tt * 4:tt * 4 + 4], f.gi[0:4, tt * P:tt * P + P], k.c("ident")[0:4, 0:4])
    last.then_inc(*f.pe.mark("c_tok"))

    def rows(h):
        if h < 2:
            pe.wait_ge(*f.act.at("rows"))
            pe.wait_ge(*f.dve.at("v"))
        else:
            pe.wait_ge(*f.dve.at(f"h{h - 2}"))
        mm(k.psum[:, h % 2, :], k.c("head4")[0:4, h * P:h * P + P],
           f.rows[0:4, :, :].rearrange("p n t -> p (n t)")).then_inc(*f.pe.mark(f"rows{h}"))

    def scores(h):
        if h < 2:
            pe.wait_ge(*f.act.at("qk"))
            pe.wait_ge(*f.act.at("vsw"))
            pe.wait_ge(*f.act.at("c_tok"))
        else:
            pe.wait_ge(*f.dve.at(f"pt{h - 2}"))
        mm(k.psum[:, 2 + h % 2, 0:T], f.qk[:, 4 + h, 0:P], f.qk[:, h, :])
        mm(k.psum[:, 2 + h % 2, T:3 * P], f.qk[:, 4 + h, P:T], f.qk[:, h, P:T]).then_inc(*f.pe.mark(f"s{h}"))

    def values(h):
        pe.wait_ge(*f.dve.at(f"pt{h}"))
        if h == 0:
            pe.wait_ge(k.even_out, 10)
            pe.wait_ge(k.odd_out, 10)
        elif h >= 2:
            pe.wait_ge(*f.dve.at(f"h{h - 2}"))
        pt = f.pt[h % 2]
        early = pt[:, 0:2, :].rearrange("p n t -> p (n t)")
        for j, (v0, v1) in enumerate(((f.v[:, 0, h * P:h * P + P], f.v[:, 1, h * P:h * P + P]),
                                      (k.c("ones"), k.c("ones")))):
            mm(k.bank(4 + h % 2)[:, j, :], v0, early, True, False)
            last = mm(k.bank(4 + h % 2)[:, j, P:T], v1, pt[:, 2, :], False, True)
        last.then_inc(*f.pe.mark(f"num{h}"))

    rows(0)
    rows(1)
    scores(0)
    scores(1)
    values(0)
    scores(2)
    values(1)
    scores(3)
    rows(2)
    rows(3)
    values(2)
    values(3)

    def head_sums(what, src):
        for i in range(2):
            last = mm(k.psum[:, 6 + i, :], k.c("ones"), src[:, 2 * i:2 * i + 2, :].rearrange("p n t -> p (n t)"))
        last.then_inc(*f.pe.mark(f"hs.{what}"))
    pe.wait_ge(*f.dve.at("h3"))
    head_sums("sum", f.hs)

    pe.wait_ge(*f.dve.at("win"))
    for j in range(2):
        for i in range(2):
            wt = unit().rearrange("p (k c) -> p k c", c=P)
            for n in range(8):
                pair = i * 8 + n
                last = mm(k.psum[:, 0, j * 32:j * 32 + 30], wt[:, n, :], f.win[:, j * 16 + pair, 0:30],
                          pair == 0, pair == 15)
                if n == 0:
                    hand_back(last)
    last.then_inc(*f.pe.mark("hid"))
    pe.wait_ge(*f.act.at("hs.sq"))
    head_sums("sq", k.sq)
    pe.wait_ge(*f.dve.at("hid"))
    w2 = f.p("cmp_w2")
    for g in range(2):
        rows_g = slice(g * HEAD, g * HEAD + HEAD)
        mm(k.psum[rows_g, 1, 0:15], w2[:, 0:HEAD], f.hid[:, 0, g * 15:g * 15 + 15])
        for j in range(4):
            last = mm(k.psum[0:HEAD, 2, (g * 4 + j) * HEAD:(g * 4 + j + 1) * HEAD], f.hid_v[:, g * 4 + j, :],
                      w2[:, HEAD:2 * HEAD])
    last.then_inc(*f.pe.mark("cmp_kv"))
    pe.wait_ge(*f.act.at("cmp_k"))
    for g in range(2):
        rows_g = slice(g * HEAD, g * HEAD + HEAD)
        for tt in range(2):
            for j in range(4):
                at = (tt * 4 + j) * 16
                last = mm(k.psum[:, 3 + g, at:at + 16], f.nq[rows_g, j, tt * P:tt * P + P], f.kcmp[rows_g, :])
    last.then_inc(*f.pe.mark("cmp_scores"))
    pe.wait_ge(*f.dve.at("cmp"))
    for g in range(2):
        for tt in range(2):
            src = f.pc[:, (g * 2 + tt) * 4:(g * 2 + tt) * 4 + 4, :].rearrange("p j m -> p (j m)")
            last = pe.transpose(k.bank(5)[0:HEAD, g, tt * P:tt * P + P], src, k.c("ident"))
    last.then_inc(*f.pe.mark("cmp_t"))
    pe.wait_ge(*f.act.at("cmp_t"))
    pe.wait_ge(*f.dve.at("cmp_v"))

    att = Attention(k, f, 0, 2, B_SCALE)
    outs = k.psum[:, 6:8, :].rearrange("p b (n t) -> p (b n) t", t=T)

    def att_scores(u, g, j, tt):
        att.scores_free(pe, u)
        rows_g = slice(g * HEAD, g * HEAD + HEAD)
        q = f.nq[rows_g, j, tt * P:tt * P + P]
        mm(att.scores(u, tt)[:, 0, :], q, f.ks[rows_g, 0, 0:att.keys(tt)])
        mm(att.scores(u, tt)[:, 1, :], q, f.kw[rows_g, 0, 0:att.keys(tt)]).then_inc(f.att_scores, 1)

    def att_values(u, g, j, tt):
        pe.wait_ge(f.att_copied, u + 1)
        out = outs[g * HEAD:g * HEAD + HEAD, j, tt * P:tt * P + P]
        mm(out, f.vcmp[0:HEAD, g * 4 + j, :], f.pct[0:HEAD, g, tt * P:tt * P + P], True, False)
        for b in range(2):
            for kt in range(tt + 1):
                block = b * (tt + 1) + kt
                last = mm(out, f.vsw[:, kt, b * P + g * HEAD:b * P + g * HEAD + HEAD],
                          f.prob_t[u % 2][:, block * P:block * P + P], False, block == att.blocks(tt) - 1)
        last.then_inc(f.att_out, 1)

    for i in range(16 + 3):
        if i < 16:
            att_scores(i, *NSA_UNITS[i])
        if 2 <= i < 18:
            att.pe_turn(pe, i - 2, NSA_UNITS[i - 2][2])
        if i >= 3:
            att_values(i - 3, *NSA_UNITS[i - 3])

    pe.wait_ge(*f.dve.at("out"))
    for n in range(KD):
        last = pe_columns(k, pe, w, k.acc[:, n, :], k.cat)
    last.then_inc(k.acc_ready, 1)
    w.n["acc"] += 1


def even_scalar(k, f, act, w):
    for t in range(0, 8, 2):
        copy_tile(k, act, w, t, even_tile_out(f, t))
    act.wait_ge(k.load, 16)
    act.wait_ge(f.params, 32)
    act.wait_ge(*f.pe.at("gates"))
    act.activation(f.gate, k.psum[:, 2, 0:48].rearrange("p (t c) -> p t c", t=2), ACT.Sigmoid).then_inc(
        *f.act.mark("gate"))
    act.activation(f.gi[0:4, :], k.psum[0:4, 3, 0:T], ACT.Identity, bias=f.p("i_b")[0:4, :])
    act.activation(f.gf[0:4, :], k.psum[0:4, 3, T:2 * T], ACT.Identity, bias=f.p("f_b")[0:4, :])
    act.drain()
    act.activation(f.gt[0:4, :], f.gf[0:4, :], ACT.Abs)
    act.drain()
    act.activation(f.gt[0:4, :], f.gt[0:4, :], ACT.Exp, scale=-1.0)
    act.drain()
    act.activation(f.gt[0:4, :], f.gt[0:4, :], ACT.Ln, bias=k.eps(1.0)[0:4, :]).then_inc(*f.act.mark("fl"))
    for t in range(8, 16, 2):
        copy_tile(k, act, w, t, even_tile_out(f, t))
    act.wait_ge(*f.pe.at("vsw"))
    act.activation(f.vsw, k.bank(2), ACT.Copy).then_inc(*f.act.mark("vsw"))
    for t in range(16, 20, 2):
        copy_tile(k, act, w, t, even_tile_out(f, t))
    act.wait_ge(*f.dve.at("conv"))
    act.activation(f.qk, f.qk, ACT.Silu).then_inc(*f.act.mark("qk"))
    act.wait_ge(k.odd_out, 10)
    act.drain()
    act.activation(f.o, f.o, ACT.Sigmoid).then_inc(*f.act.mark("sig"))
    act.wait_ge(*f.pe.at("c_tok"))
    act.activation(f.c_tok, k.psum[:, 3, 0:8].rearrange("p (t h) -> p t h", t=2), ACT.Copy).then_inc(
        *f.act.mark("c_tok"))
    act.wait_ge(*f.dve.at("rows"))
    act.activation(f.rows[0:4, 1, :], f.gt[0:4, :], ACT.Exp, scale=-1.0).then_inc(*f.act.mark("rows"))

    def exps(h):
        act.wait_ge(*f.dve.at(f"arg{h}"))
        e, arg = f.e[h % 2], f.arg[h % 2]
        act.activation(e[:, 0, :], arg[:, 0, :], ACT.Exp, bias=f.c_tok[:, 0, h:h + 1])
        act.activation(e[:, 1, :], k.psum[:, h % 2, P:T], ACT.Exp, bias=f.c_tok[:, 0, h:h + 1])
        act.activation(e[:, 2, :], arg[:, 1, :], ACT.Exp, bias=f.c_tok[:, 1, h:h + 1]).then_inc(
            *f.act.mark(f"e{h}"))

    def den(h):
        act.wait_ge(*f.pe.at(f"num{h}"))
        act.activation(f.den[h % 2], k.bank(4 + h % 2)[:, 1, :], ACT.Abs).then_inc(*f.act.mark(f"den{h}"))
    act.drain()
    for step, h in ((exps, 0), (exps, 1), (den, 0), (den, 1), (exps, 2), (exps, 3), (den, 2), (den, 3)):
        step(h)

    act.wait_ge(*f.dve.at("hs.xc"))
    act.activation(k.sq[:, 0:4, :], f.hs, ACT.Square).then_inc(*f.act.mark("hs.sq"))

    hid_psum = k.psum[:, 0, 0:64].rearrange("p (j n) -> p j n", j=2)[:, :, 0:30]
    act.wait_ge(*f.pe.at("hid"))
    act.activation(f.hid_t[:, :, 0:30], hid_psum, ACT.Square).then_inc(*f.act.mark("hid_sq"))
    act.wait_ge(*f.dve.at("hid_in"))
    act.activation(f.hid_t[:, :, 0:30], f.hid_t[:, :, 0:30], ACT.Tanh, scale=GELU).then_inc(
        *f.act.mark("hid_tanh"))
    act.wait_ge(*f.pe.at("cmp_kv"))
    act.activation(f.kcmp[:, 0:15], k.psum[:, 1, 0:15], ACT.Copy).then_inc(*f.act.mark("cmp_k"))
    act.wait_ge(*f.dve.at("cmp_max"))
    act.activation(f.pc, f.pc, ACT.Exp, scale=B_SCALE).then_inc(*f.act.mark("cmp_exp"))
    act.wait_ge(*f.pe.at("cmp_t"))
    act.activation(f.pct[0:HEAD, :, :], k.bank(5)[0:HEAD, :, :], ACT.Copy).then_inc(*f.act.mark("cmp_t"))
    act.wait_ge(*f.pe.at("hs.sq"))
    act.activation(k.tmp[:, 0:4, :], k.psum[:, 6:8, :].rearrange("p b (n t) -> p (b n) t", t=T), ACT.Sqrt,
                   bias=k.eps(LN_EPS), scale=1.0 / P).then_inc(*f.act.mark("hs.std"))

    att = Attention(k, f, 0, 2, B_SCALE)
    for i in range(16 + 2):
        if i < 16:
            att.act_exp(act, i, NSA_UNITS[i][2])
        if i >= 2:
            att.act_copy(act, i - 2, NSA_UNITS[i - 2][2])


def even_vector(k, f, dve, w):
    dve.memset(f.qk_raw[:, :, 0:A_CONV - 1], 0.0)
    dve.memset(f.hid_v, 0.0)
    dve.memset(f.kcmp, 0.0)
    dve.memset(f.one[0:4, :], 1.0)
    for t in range(1, 8, 2):
        copy_tile(k, dve, w, t, even_tile_out(f, t))
    dve.wait_ge(*f.pe.at("v"))
    dve.tensor_copy(f.v[:, 0, :], k.psum[:, 0, :])
    dve.tensor_copy(f.v[:, 1, :], k.psum[:, 1, :]).then_inc(*f.dve.mark("v"))
    dve.drain()
    dve.wait_ge(k.even_out, 4)

    dve.wait_ge(k.load, 16)
    dve.wait_ge(f.params, 32)

    def tap(j):
        for i in range(8):
            weight = f.p("conv_w", i * A_CONV + j)
            src = f.qk_raw[:, i, j:j + T]
            if j == 0:
                last = dve.tensor_scalar(f.qk[:, i, :], src, weight, None, ALU.mult)
            else:
                last = dve.scalar_tensor_tensor(f.qk[:, i, :], src, weight, f.qk[:, i, :], ALU.mult, ALU.add)
        return last
    for j, t in enumerate(range(9, 16, 2)):
        last = tap(j)
        if j == 3:
            last.then_inc(*f.dve.mark("conv"))
        copy_tile(k, dve, w, t, even_tile_out(f, t))
        dve.drain()

    r4 = slice(0, 4)
    dve.wait_ge(*f.act.at("fl"))
    dve.scalar_tensor_tensor(f.gl[r4, :], f.gf[r4, :], 0.0, f.gt[r4, :], ALU.min, ALU.subtract)
    dve.drain()
    dve.tensor_tensor_scan(f.cum[r4, :], f.one[r4, :], f.gl[r4, :], 0.0, ALU.mult, ALU.add)
    dve.drain()
    dve.tensor_tensor(f.gi[r4, :], f.gi[r4, :], f.cum[r4, :], ALU.subtract).then_inc(*f.dve.mark("cmin"))
    dve.drain()
    dve.tensor_tensor_scan(f.gl[r4, :], f.one[r4, :], f.gi[r4, :], 0.0, ALU.mult, ALU.max)
    dve.drain()
    dve.tensor_scalar(f.rows[r4, 0, :], f.gl[r4, :], -1.0, None, ALU.mult)
    dve.tensor_tensor(f.gt[r4, :], f.cum[r4, :], f.gl[r4, :], ALU.add).then_inc(*f.dve.mark("rows"))
    for t in range(17, 20, 2):
        copy_tile(k, dve, w, t, even_tile_out(f, t))

    dve.wait_ge(k.even_out, 7)
    for j, raw in enumerate((f.kc, f.vc)):
        dve.tensor_copy(f.shift[0:HEAD, j * 2, :], raw[0:HEAD, 0, :])
        last = dve.tensor_copy(f.shift[HEAD:P, j * 2 + 1, 0:T - 1], raw[HEAD:P, 0, 1:T])
    last.then_inc(*f.dve.mark("shift"))

    def arg(h):
        dve.wait_ge(*f.pe.at(f"rows{h}"))
        dve.tensor_tensor(f.arg[h % 2], k.psum[:, h % 2, 0:T].rearrange("p (n t) -> p n t", n=2),
                          bc(k.c("causal_st"), 2), ALU.add).then_inc(*f.dve.mark(f"arg{h}"))

    def pt(h):
        dve.wait_ge(*f.pe.at(f"s{h}"))
        dve.wait_ge(*f.act.at(f"e{h}"))
        dve.scalar_tensor_tensor(f.pt[h % 2], k.psum[:, 2 + h % 2, 0:3 * P].rearrange("p (n t) -> p n t", n=3),
                                 A_SCALE, f.e[h % 2], ALU.mult, ALU.mult).then_inc(*f.dve.mark(f"pt{h}"))

    def out(h):
        dve.wait_ge(*f.act.at(f"den{h}"))
        den = f.den[h % 2]
        dve.tensor_tensor(den, den, k.bank(h % 2)[:, 1, :], ALU.max)
        dve.drain()
        dve.reciprocal(den, den)
        dve.drain()
        dve.tensor_tensor(f.hs[:, h, :], k.bank(4 + h % 2)[:, 0, :], den, ALU.mult).then_inc(
            *f.dve.mark(f"h{h}"))
    for step, h in ((arg, 0), (arg, 1), (pt, 0), (pt, 1), (out, 0), (out, 1), (arg, 2), (arg, 3), (pt, 2), (pt, 3),
                    (out, 2), (out, 3)):
        step(h)

    dve.wait_ge(*f.pe.at("hs.sum"))
    dve.drain()
    dve.scalar_tensor_tensor(f.hs, k.psum[:, 6:8, :].rearrange("p b (n t) -> p (b n) t", t=T), -1.0 / P, f.hs,
                             ALU.mult, ALU.add).then_inc(*f.dve.mark("hs.xc"))

    dve.wait_ge(f.moved, 64)
    for j in range(2):
        for g in range(2):
            for a in range(2):
                src = f.shift[:, j * 2 + g, 16 * a:16 * a + 240].rearrange("p (m l two) -> p two l m", two=2, l=8)
                where = f.p("cmp_pos")[:, j * 16 + 8 * a:j * 16 + 8 * a + 8].unsqueeze(2).to_broadcast([P, 8, 15])
                last = dve.tensor_tensor(f.win[:, j * 16 + 8 * a:j * 16 + 8 * a + 8, g * 15:g * 15 + 15],
                                         src[:, 0, :, :], where, ALU.add)
    last.then_inc(*f.dve.mark("win"))
    hid_psum = k.psum[:, 0, 0:64].rearrange("p (j n) -> p j n", j=2)[:, :, 0:30]
    hid, t = f.hid[:, :, 0:30], f.hid_t[:, :, 0:30]
    dve.wait_ge(*f.act.at("hid_sq"))
    dve.tensor_copy(hid, hid_psum)
    dve.tensor_scalar(t, t, 0.044715, 1.0, ALU.mult, ALU.add)
    dve.drain()
    dve.tensor_tensor(t, t, hid, ALU.mult).then_inc(*f.dve.mark("hid_in"))
    dve.wait_ge(*f.act.at("hid_tanh"))
    dve.scalar_tensor_tensor(t, t, 1.0, hid, ALU.add, ALU.mult)
    dve.drain()
    for g in range(2):
        for j in range(4):
            dve.tensor_scalar(f.hid_v[:, g * 4 + j, j * 16:j * 16 + 15], f.hid_t[:, 1, g * 15:g * 15 + 15], 0.5, None,
                              ALU.mult)
    dve.tensor_scalar(hid, t, 0.5, None, ALU.mult).then_inc(*f.dve.mark("hid"))
    dve.wait_ge(*f.pe.at("cmp_kv"))
    dve.tensor_copy(f.vcmp[0:HEAD, :, :], k.psum[0:HEAD, 2, :].rearrange("p (n d) -> p n d", n=8)).then_inc(
        *f.dve.mark("cmp_v"))
    dve.wait_ge(*f.pe.at("cmp_scores"))
    for g in range(2):
        mask = k.c("cmp_mask").rearrange("p (t m) -> p t m", t=2).unsqueeze(2).to_broadcast([P, 2, 4, 16])
        dve.tensor_tensor(f.pc[:, g * 8:g * 8 + 8, :].rearrange("p (t j) m -> p t j m", t=2),
                          k.psum[:, 3 + g, 0:P].rearrange("p (t j m) -> p t j m", t=2, j=4), mask, ALU.add)
    dve.drain()
    dve.tensor_reduce(f.pm, f.pc, AX_X, ALU.max)
    dve.drain()
    dve.tensor_scalar(f.pm, f.pm, NEG / 10, None, ALU.max)
    dve.drain()
    dve.tensor_tensor(f.pc, f.pc, f.pm.unsqueeze(2).to_broadcast([P, 16, 16]), ALU.subtract).then_inc(
        *f.dve.mark("cmp_max"))
    dve.wait_ge(*f.act.at("cmp_exp"))
    dve.tensor_reduce(f.ps, f.pc, AX_X, ALU.add)
    dve.drain()
    dve.tensor_scalar(f.ps, f.ps, 1e-30, None, ALU.max)
    dve.drain()
    dve.reciprocal(f.ps, f.ps)
    dve.drain()
    for g in range(2):
        ps = f.ps[:, g * 8:g * 8 + 8].rearrange("p (t j) -> p t j", t=2)
        gate = f.gate[:, :, g * 12:g * 12 + 12].rearrange("p t (j b) -> p b t j", b=3)[:, 0, :, :]
        dve.tensor_tensor(ps, ps, gate, ALU.mult)
    dve.drain()
    dve.tensor_tensor(f.pc, f.pc, f.ps.unsqueeze(2).to_broadcast([P, 16, 16]), ALU.mult).then_inc(
        *f.dve.mark("cmp"))

    def head_out(h, step):
        dve.drain()
        if step == 0:
            dve.reciprocal(k.tmp[:, h, :], k.tmp[:, h, :])
        elif step == 1:
            dve.tensor_tensor(f.o[:, h, :], f.o[:, h, :], k.tmp[:, h, :], ALU.mult)
        else:
            dve.scalar_tensor_tensor(k.cat[:, h, :], f.hs[:, h, :], f.p("a_norm", h), f.o[:, h, :],
                                     ALU.mult, ALU.mult)

    att = Attention(k, f, 0, 2, B_SCALE)
    for i in range(16 + 1):
        if i == 2:
            dve.wait_ge(*f.act.at("hs.std"))
            dve.wait_ge(*f.act.at("sig"))
        if 2 <= i < 14:
            head_out((i - 2) // 3, (i - 2) % 3)
        if i < 16:
            tt = NSA_UNITS[i][2]
            n = att.keys(tt)
            dve.wait_ge(f.att_scores, i + 1)
            diag = att.scores(i, tt)[:, :, n - P:n]
            dve.tensor_tensor(diag, diag, bc(k.c("causal_qk"), 2), ALU.add)
            att.dve_max(dve, i, tt)
        if i >= 1:
            g, j, tt = NSA_UNITS[i - 1]
            head = (g * 4 + j) * 3
            att.dve_prob(dve, i - 1, tt, f.gate[:, tt, head + 1:head + 3])
    dve.wait_ge(f.att_out, 16)
    dve.tensor_copy(k.cat[:, 4:8, :], k.psum[:, 6:8, :].rearrange("p b (n t) -> p (b n) t", t=T)).then_inc(
        *f.dve.mark("out"))
    dve.drain()


def even_pool(k, f, pool):
    pool.wait_ge(k.even_out, 7)
    pool.wait_ge(k.odd_out, 7)
    for j, raw in enumerate((f.kc, f.vc)):
        pool.dma_start(f.shift[HEAD:P, j * 2, 0:T - 1], raw[0:HEAD, 0, 1:T]).then_inc(f.moved, 16)
        pool.dma_start(f.shift[0:HEAD, j * 2 + 1, :], raw[HEAD:P, 0, :]).then_inc(f.moved, 16)



def odd_tile_out(f, t):
    if t < 8:
        return (*(f.cq[:, i, :] for i in range(4)), *(f.ckv[:, i, :] for i in range(2)), f.rc[:, 4, :],
                f.ik[:, 0, :])[t]
    if t < 12:
        return f.ri[:, t - 8, :]
    if t < 16:
        return f.rc[:, t - 12, :]
    if t < 24:
        return f.qn[:, t - 16, :]
    return f.q_abs[:, t - 24, :]


ODD_TILES = 40
EVEN_TILES = 20


def odd_tensor(k, f, pe, w):
    def mm(out, lhsT, rhs, start=True, stop=True):
        return pe.matmul(out, lhsT, rhs, start=start, stop=stop, skip_group_check=True)

    flat = lambda x: x.rearrange("p n t -> p (n t)")
    pe.wait_ge(k.x_ready, PARTS)
    for _ in range(8):
        pe_columns(k, pe, w, pe_next_tile(k, pe, w), k.x).then_inc(k.proj_ready, 1)
    slot = w.n["unit"] % RING
    pe.wait_ge(k.filled[slot], w.filled())
    wt = k.ring[:, slot, :].rearrange("p (k c) -> p k c", c=P)
    for tt in range(2):
        for i in range(KD):
            last = mm(k.psum[:, 0, tt * 8:tt * 8 + 8], k.x[:, i, tt * P:tt * P + P], wt[:, i, 0:8],
                      i == 0, i == KD - 1)
            if tt + i == 0:
                last.then_inc(k.freed, w.owed)
                w.owed = 0
    last.then_inc(*f.ope.mark("iw"))
    w.n["unit"] += 1
    w.owed += 1
    pe.wait_ge(*f.odve.at("sq"))
    for i in range(4):
        mm(k.bank(1)[:, 0, :], k.c("ones"), k.sq[:, i, :], i == 0, i == 3)
    for i in range(2):
        mm(k.bank(1)[:, 1, :], k.c("ones"), k.sq[:, 4 + i, :], i == 0, i == 1)
    mm(k.bank(2)[:, 0, :], k.c("block64"), f.ik[:, 0, :]).then_inc(*f.ope.mark("sums"))
    pe.wait_ge(*f.odve.at("ik_sq"))
    mm(k.bank(3)[:, 0, :], k.c("block64"), k.sq[:, 6, :]).then_inc(*f.ope.mark("ik_ss"))

    def out_of_psum(tiles):
        pe.wait_ge(k.even_out, (EVEN_TILES + tiles) // 2)
        pe.wait_ge(k.odd_out, (EVEN_TILES + tiles) // 2)

    def queries(units):
        for _ in range(units):
            pe_tiles(k, pe, w, [[(half * 4 + i, f.cqn[:, i, :]) for i in range(4)] for half in range(2)])

    def swap(what, src, matrix_name):
        for b, (i, n) in enumerate(((0, 2), (2, 2), (4, 1))):
            last = mm(k.psum[:, b, 0:n * T], k.c(matrix_name), flat(src[:, i:i + n, :]))
        last.then_inc(*f.ope.mark(what))

    def index(h):
        if h >= 4:
            pe.wait_ge(*f.oact.at(f"r{h - 4}"))
        rows, i = head_rows(h)
        mm(k.psum[:, h % 4, 0:P], f.ri[rows, i, 0:P], f.ri[rows, 4, 0:P])
        mm(k.psum[:, h % 4, P:3 * P], f.ri[rows, i, P:T], f.ri[rows, 4, :]).then_inc(*f.ope.mark(f"i{h}"))

    pe.wait_ge(*f.odve.at("cqn"))
    queries(4)
    out_of_psum(12)
    pe.wait_ge(*f.odve.at("ikn"))
    swap("swap_i", f.ri, "swap32")
    queries(2)
    pe.wait_ge(*f.odve.at("rope_i"))
    for h in range(4):
        index(h)
    queries(1)
    for h in range(4, 8):
        index(h)
    queries(1)
    out_of_psum(16)
    pe.wait_ge(*f.oact.at("r7"))
    swap("swap_c", f.rc, "swap64")
    for tt in range(2):
        for c in range(2):
            last = pe.transpose(k.bank(3, P)[:, tt * 2 + c, :], f.ckvn[:, c, tt * P:tt * P + P], k.c("ident"))
    last.then_inc(*f.ope.mark("turned"))
    out_of_psum(24)
    for i in range(2):
        pe_tiles(k, pe, w, [[(h * 2 + c, f.qn[:, 4 * i + h, :])] for h in range(4) for c in range(2)])
    out_of_psum(ODD_TILES)
    pe.wait_ge(*f.odve.at("turned"))

    att = Attention(k, f, 16, 1, C_SCALE)

    def att_scores(u, h, tt):
        att.scores_free(pe, u)
        rows, i = head_rows(h)
        out, n, tok = att.scores(u, tt)[:, 0, :], att.keys(tt), slice(tt * P, tt * P + P)
        for c in range(2):
            mm(out, f.q_abs[:, h * 2 + c, tok], f.ckvn[:, c, 0:n], c == 0, False)
        mm(out, f.rc[rows, i, tok], f.rc[rows, 4, 0:n], False, True).then_inc(f.att_scores, 1)

    def att_values(u, h, tt):
        pe.wait_ge(f.att_copied, 16 + u + 1)
        if tt == 0 and h > 0:
            pe.wait_ge(*f.odve.at(f"lat{h - 1}"))
        for c in range(2):
            out = k.bank(6)[:, c, tt * P:tt * P + P]
            for kt in range(tt + 1):
                last = mm(out, f.ckv_tok[:, kt, c * P:c * P + P], f.prob_t[u % 2][:, kt * P:kt * P + P],
                          kt == 0, kt == tt)
        last.then_inc(f.att_out, 1)

    def up(h):
        if h % 4 == 0:
            slot = w.n["unit"] % RING
            pe.wait_ge(k.filled[slot], w.filled())
            w.n["unit"] += 1
            f.up_unit = k.ring[:, slot, :].rearrange("p (k c) -> p k c", c=P)
        pe.wait_ge(*f.odve.at(f"lat{h}"))
        if h > 0:
            pe.wait_ge(*f.oact.at(f"up{h - 1}"))
        for c in range(2):
            last = mm(k.bank(7)[:, 0, :], f.up_unit[:, h % 4 * 2 + c, :], f.o_lat[h % 2][:, c, :], c == 0, c == 1)
            if c == 0 and h % 4 == 0:
                last.then_inc(k.freed, w.owed)
                w.owed = 1
        last.then_inc(*f.ope.mark(f"lat{h}"))

    for i in range(16 + 6):
        if i < 16:
            att_scores(i, *MLA_UNITS[i])
        if 2 <= i < 18:
            att.pe_turn(pe, i - 2, MLA_UNITS[i - 2][1])
        if 3 <= i < 19:
            att_values(i - 3, *MLA_UNITS[i - 3])
        if i >= 5 and i % 2 == 1 and i < 21:
            up((i - 5) // 2)
    pe.wait_ge(*f.oact.at("up7"))
    for n in range(KD):
        last = pe_columns(k, pe, w, k.acc[:, n, :], k.cat)
    last.then_inc(k.acc_ready, 1)
    w.n["acc"] += 1


def odd_scalar(k, f, act, w):
    for t in range(0, 8, 2):
        copy_tile(k, act, w, EVEN_TILES + t, odd_tile_out(f, t))
    act.wait_ge(*f.ope.at("sums"))
    act.activation(k.std[:, 0, :], k.bank(1)[:, 0, :], ACT.Sqrt, bias=k.eps(LN_EPS), scale=1.0 / 512)
    act.activation(k.std[:, 1, :], k.bank(1)[:, 1, :], ACT.Sqrt, bias=k.eps(LN_EPS), scale=1.0 / 256).then_inc(
        *f.oact.mark("std"))
    act.wait_ge(*f.ope.at("ik_ss"))
    act.activation(f.iks[:, 0, :], k.bank(3)[:, 0, :], ACT.Sqrt, bias=k.eps(LN_EPS), scale=1.0 / HEAD).then_inc(
        *f.oact.mark("ik_std"))

    def relus(first, last):
        for h in range(first, last):
            act.wait_ge(*f.ope.at(f"i{h}"))
            if h >= 2:
                act.wait_ge(*f.odve.at(f"acc{h - 2}"))
            act.activation(f.relu[h % 2], k.psum[:, h % 4, 0:3 * P], ACT.Relu).then_inc(*f.oact.mark(f"r{h}"))
    for t in range(8, ODD_TILES, 2):
        if t == 20:
            relus(0, 4)
        if t == 22:
            relus(4, 8)
        copy_tile(k, act, w, EVEN_TILES + t, odd_tile_out(f, t))
    att = Attention(k, f, 16, 1, C_SCALE)
    for i in range(16 + 7):
        if i < 16:
            att.act_exp(act, i, MLA_UNITS[i][1])
        if 2 <= i < 18:
            att.act_copy(act, i - 2, MLA_UNITS[i - 2][1])
        if i >= 6 and i % 2 == 0 and (i - 6) // 2 < 8:
            h = (i - 6) // 2
            act.wait_ge(*f.ope.at(f"lat{h}"))
            act.activation(k.cat[:, h, :], k.bank(7)[:, 0, :], ACT.Copy).then_inc(*f.oact.mark(f"up{h}"))


def odd_vector(k, f, dve, w):
    for t in range(1, 8, 2):
        copy_tile(k, dve, w, EVEN_TILES + t, odd_tile_out(f, t))
    dve.drain()
    dve.wait_ge(k.even_out, (EVEN_TILES + 8) // 2)
    dve.tensor_tensor(k.sq[:, 0:4, :], f.cq, f.cq, ALU.mult)
    dve.tensor_tensor(k.sq[:, 4:6, :], f.ckv, f.ckv, ALU.mult)
    dve.wait_ge(*f.ope.at("iw"))
    dve.tensor_scalar(f.wi, k.psum[:, 0, 0:16].rearrange("p (t h) -> p t h", t=2), WI_SCALE, None,
                      ALU.mult).then_inc(*f.odve.mark("sq"))
    dve.wait_ge(*f.ope.at("sums"))
    dve.scalar_tensor_tensor(f.ikc[:, 0, :], k.bank(2)[:, 0, :], -1.0 / HEAD, f.ik[:, 0, :], ALU.mult, ALU.add)
    dve.drain()
    dve.tensor_tensor(k.sq[:, 6, :], f.ikc[:, 0, :], f.ikc[:, 0, :], ALU.mult).then_inc(*f.odve.mark("ik_sq"))
    dve.wait_ge(*f.oact.at("std"))
    dve.reciprocal(k.rstd, k.std)
    dve.drain()
    for i in range(4):
        dve.scalar_tensor_tensor(f.cqn[:, i, :], f.cq[:, i, :], f.p("q_norm", i), k.rstd[:, 0, :],
                                 ALU.mult, ALU.mult)
    for i in range(2):
        last = dve.scalar_tensor_tensor(f.ckvn[:, i, :], f.ckv[:, i, :], f.p("kv_norm", i), k.rstd[:, 1, :],
                                        ALU.mult, ALU.mult)
    last.then_inc(*f.odve.mark("cqn"))
    dve.wait_ge(*f.oact.at("ik_std"))
    dve.reciprocal(f.iks[:, 1, :], f.iks[:, 0, :])
    dve.drain()
    dve.scalar_tensor_tensor(f.ikc[:, 0, :], f.ikc[:, 0, :], f.p("ik_g"), f.iks[:, 1, :], ALU.mult, ALU.mult)
    dve.drain()
    dve.tensor_scalar(f.ri[:, 4, :], f.ikc[:, 0, :], f.p("ik_b"), None, ALU.add).then_inc(*f.odve.mark("ikn"))
    def tiles_out(first, last):
        for t in range(first, last, 2):
            copy_tile(k, dve, w, EVEN_TILES + t, odd_tile_out(f, t))

    def rotate(j, name, x, tiles):
        dve.drain()
        dve.wait_ge(k.even_out, (EVEN_TILES + tiles) // 2)
        dve.wait_ge(*f.ope.at(f"swap_{name}"))
        dve.tensor_tensor(f.rt, x, bc(f.cos[:, j, :], 5), ALU.mult)
        dve.tensor_tensor(k.tmp[:, 0:5, :], k.psum[:, 0:3, :].rearrange("p b (n t) -> p (b n) t", t=T)[:, 0:5, :],
                          bc(f.sin[:, j, :], 5), ALU.mult)
        dve.drain()
        dve.tensor_tensor(x, f.rt, k.tmp[:, 0:5, :], ALU.add).then_inc(*f.odve.mark(f"rope_{name}"))
        dve.drain()

    def weigh(first, last):
        for h in range(first, last):
            dve.wait_ge(*f.oact.at(f"r{h}"))
            for tt, cols in enumerate((slice(0, P), slice(P, 3 * P))):
                weight = f.wi[:, tt, h:h + 1]
                if h == 0:
                    ins = dve.tensor_scalar(f.isc[:, cols], f.relu[0][:, cols], weight, None, ALU.mult)
                else:
                    ins = dve.scalar_tensor_tensor(f.isc[:, cols], f.relu[h % 2][:, cols], weight, f.isc[:, cols],
                                                   ALU.mult, ALU.add)
            ins.then_inc(*f.odve.mark(f"acc{h}"))
            dve.drain()

    tiles_out(9, 16)
    rotate(1, "i", f.ri, 12)
    tiles_out(17, 20)
    weigh(0, 4)
    tiles_out(21, 22)
    weigh(4, 8)
    tiles_out(23, 24)
    diag = lambda x: x.rearrange("p (n t) -> p n t", n=3)[:, 0:3:2, :]
    dve.tensor_tensor(diag(f.isc), diag(f.isc), bc(k.c("causal_qk"), 2), ALU.add)
    rotate(0, "c", f.rc, 16)
    dve.wait_ge(*f.ope.at("turned"))
    dve.tensor_copy(f.ckv_tok, k.bank(3)).then_inc(*f.odve.mark("turned"))
    src = f.isc
    for r in range(TOPK // 8):
        dst = f.work[r % 2]
        for tt, cols in enumerate((slice(0, P), slice(P, 3 * P))):
            dve.max(f.top[:, tt, :], src[:, cols])
        dve.drain()
        for tt, cols in enumerate((slice(0, P), slice(P, 3 * P))):
            dve.match_replace(dst[:, cols], f.top[:, tt, :], src[:, cols], TAKEN)
        tiles_out(25 + 2 * r, 26 + 2 * r)
        dve.drain()
        src = dst
    dve.tensor_scalar(f.sel, src, TAKEN / 2, NEG, ALU.is_gt, ALU.mult)
    dve.drain()
    dve.tensor_tensor(diag(f.sel), diag(f.sel), bc(k.c("causal_qk"), 2), ALU.add).then_inc(*f.odve.mark("sel"))
    dve.drain()

    att = Attention(k, f, 16, 1, C_SCALE)
    for i in range(16 + 5):
        if i < 16:
            tt = MLA_UNITS[i][1]
            dve.wait_ge(f.att_scores, 16 + i + 1)
            s = att.scores(i, tt)[:, 0, :]
            dve.tensor_tensor(s, s, f.sel[:, 0:P] if tt == 0 else f.sel[:, P:3 * P], ALU.add)
            att.dve_max(dve, i, tt)
        if 1 <= i < 17:
            att.dve_prob(dve, i - 1, MLA_UNITS[i - 1][1])
        if i >= 5 and i % 2 == 1:
            h = (i - 5) // 2
            dve.wait_ge(f.att_out, 16 + 2 * h + 2)
            if h >= 2:
                dve.wait_ge(*f.ope.at(f"lat{h - 2}"))
            dve.tensor_copy(f.o_lat[h % 2], k.bank(6)).then_inc(*f.odve.mark(f"lat{h}"))



def tables_vector(k, f, dve):
    dve.tensor_copy(f.pos, f.pos_i.bitcast(I32))
    dve.drain()
    for j in range(2):
        dve.tensor_scalar(f.angle[:, j, :], f.pos, k.c("inv_freq")[:, j:j + 1], None, ALU.mult)
    dve.drain()
    dve.tensor_scalar(f.turns, f.angle, float(1 / (2 * np.pi)), ROUND, ALU.mult, ALU.add)
    dve.drain()
    dve.tensor_scalar(f.turns, f.turns, ROUND, None, ALU.subtract)
    dve.drain()
    for part in TWO_PI:
        dve.scalar_tensor_tensor(f.angle, f.turns, -part, f.angle, ALU.mult, ALU.add)
        dve.drain()
    dve.tensor_scalar(f.turns, f.angle, float(np.pi / 2), float(-2 * np.pi), ALU.is_gt, ALU.mult)
    dve.drain()
    dve.scalar_tensor_tensor(f.red, f.angle, float(np.pi / 2), f.turns, ALU.add, ALU.add)
    dve.drain()
    dve.tensor_scalar(f.red, f.red, -PI, PI, ALU.max, ALU.min)
    dve.tensor_scalar(f.angle, f.angle, -PI, PI, ALU.max, ALU.min).then_inc(f.angles, 1)


def tables_scalar(k, f, act):
    act.wait_ge(f.angles, 1)
    act.activation(f.cos, f.red, ACT.Sin)
    act.activation(f.sin, f.angle, ACT.Sin)



def tail_tensor(k, f, pe, w, layer):
    def embedded(j):
        pe_unit(k, pe, w, [(k.acc[:, 4 * j + n, :], n * 2 + c, f.embed[:, layer * 2 + c, :],
                            c == 0 and n % 2 == 0, c == 1) for n in range(4) for c in range(2)])

    def norm(meanwhile=False):
        for j in range(PARTS):
            pe.wait_ge(f.y_ready, w.value("norm", scale=PARTS) + j + 1)
            for i in part_tiles(j):
                last = pe.matmul(k.bank(7)[:, 0, :], k.c("ones"), k.x[:, i, :], start=(i == 0), stop=(i == KD - 1))
        last.then_inc(f.mean_ready, 1)
        if meanwhile:
            embedded(0)
        pe_square_sum(k, pe, w)
        if meanwhile:
            embedded(1)

    def tile_of_h(i):
        pe.wait_ge(k.h_ready, w.value("pre", scale=KD) + i + 1)
    norm()
    pe_ffn(k, pe, w, k.x, FF1, False, tile_of_h)
    w.n["pre"] += 1
    norm(meanwhile=True)
    for n in range(KD):
        if n >= 4:
            pe.wait_ge(f.ple_used, layer * KD + n - 3)
        pe_columns(k, pe, w, k.bank(4 + n % 4)[:, 0, :], k.x, tile_of_h if n == 0 else None).then_inc(
            f.ple_ready, 1)
    w.n["pre"] += 1


def tail_scalar(k, f, act, w, layer):
    def norm(bias):
        def ready(j):
            act.wait_ge(f.c_ready, w.value("norm", scale=PARTS) + j + 1)
        act_squares(k, act, w, k.x, ready)
        act_std(k, act, w, LN_EPS)
        for i in range(KD):
            act.wait_ge(f.t_ready, w.value("pre", scale=KD) + i + 1)
            act.activation(k.x[:, i, :], k.tmp[:, i, :], ACT.Identity, bias=f.p(bias, layer * KD + i)).then_inc(
                k.h_ready, 1)
        w.n["pre"] += 1
    norm("ln1_b")
    act_ffn(k, act, w, FF1, ACT.Relu)
    norm("ln2_b")
    for n in range(KD):
        act.wait_ge(f.ple_ready, layer * KD + n + 1)
        if n >= 2:
            act.wait_ge(f.ple_used, layer * KD + n - 1)
        act.activation(k.hid_act[:, n % 2, :], k.bank(4 + n % 4)[:, 0, :], ACT.Sigmoid).then_inc(f.gate_ready, 1)
    w.n["acc"] += 2
    w.n["x"] += PARTS


def tail_vector(k, f, dve, w, layer):
    def norm(gain):
        dve.wait_ge(k.acc_ready, w.value("acc", 1))
        w.n["acc"] += 1
        if gain == "ln2_g":
            dve.wait_ge(k.h_ready, w.value("pre", scale=KD))
        for j in range(PARTS):
            dve.scalar_tensor_tensor(part(k.x, j), part(k.x, j), ALPHA, part(k.acc, j),
                                     ALU.mult, ALU.add).then_inc(f.y_ready, 1)
        dve.drain()
        dve.wait_ge(f.mean_ready, w.value("norm", 1))
        for j in range(PARTS):
            dve.scalar_tensor_tensor(part(k.x, j), bc(k.bank(7)[:, 0, :], KD // PARTS), -1.0 / D,
                                     part(k.x, j), ALU.mult, ALU.add).then_inc(f.c_ready, 1)
        dve_rstd(k, dve, w)
        for i in range(KD):
            dve.scalar_tensor_tensor(k.tmp[:, i, :], k.x[:, i, :], f.p(gain, layer * KD + i), k.rstd[:, 0, :],
                                     ALU.mult, ALU.mult).then_inc(f.t_ready, 1)
        w.n["pre"] += 1
    norm("ln1_g")
    dve_ffn(k, dve, w, FF1, False)
    norm("ln2_g")
    for n in range(KD):
        dve.wait_ge(f.gate_ready, layer * KD + n + 1)
        dve.tensor_tensor(k.h[:, n, :], k.hid_act[:, n % 2, :], k.acc[:, n, :], ALU.mult).then_inc(
            f.ple_used, 1)
    dve.drain()
    dve.wait_ge(k.h_ready, w.value("pre", scale=KD))
    for j in range(PARTS):
        dve.tensor_tensor(part(k.x, j), part(k.x, j), part(k.h, j), ALU.add).then_inc(k.x_ready, 1)
    dve.drain()
    w.n["x"] += PARTS



def build(nc, x, consts, weights, params1, positions, params2, out):
    with ExitStack() as ctx:
        k = Core(nc, ctx)
        space = k.sb("space", ARENA)
        f, s = First(k, Arena(space)), Second(k, Arena(space))
        block = ctx.enter_context(nc.Block())
        turns = weights.shape[0] // RING
        assert weights.shape[0] % RING == 0

        def between(w):
            w.n["proj"] = EVEN_TILES + ODD_TILES
            w.n["even"] = w.n["odd"] = w.n["proj"] // 2
            w.n["x"] = (LAYERS - 1) * PARTS

        @block.sync
        def _(sp):
            sp.dma_start(k.x, x).then_inc(k.x_loaded, 16)
            for slot in range(RING):
                sp.dma_start(k.ring[:, slot, :], weights[slot]).then_inc(k.filled[slot], 16)
                if slot == 3:
                    sp.dma_start(k.const, consts).then_inc(k.load, 16)
                    sp.dma_start(f.par, params1).then_inc(f.params, 16)
                    sp.dma_start(f.pos_i.bitcast(I32), positions.broadcast_to([P, T])).then_inc(f.params, 16)
            with sp.Fori(1, turns) as turn:
                for slot in range(RING):
                    sp.wait_ge(k.freed, (turn - 1) * RING + (slot + 1))
                    sp.dma_start(k.ring[:, slot, :], weights[turn * RING + slot]).then_inc(k.filled[slot], 16)
            sp.wait_ge(k.x_ready, PARTS * LAYERS + LAYERS * PER_LAYER["x"])
            sp.dma_start(out, k.x).then_inc(k.saved, 16)
            sp.wait_ge(k.saved, 16)

        @block.tensor
        def _(pe):
            w = Walk()
            pe.wait_ge(k.x_loaded, 16)
            even_tensor(k, f, pe, w)
            tail_tensor(k, f, pe, w, 0)
            odd_tensor(k, f, pe, w)
            tail_tensor(k, f, pe, w, 1)
            between(w)
            pe.wait_ge(k.x_ready, PARTS * LAYERS)
            second_tensor(k, s, pe, w)

        @block.scalar
        def _(act):
            w = Walk()
            even_scalar(k, f, act, w)
            tables_scalar(k, f, act)
            tail_scalar(k, f, act, w, 0)
            odd_scalar(k, f, act, w)
            tail_scalar(k, f, act, w, 1)
            between(w)
            second_scalar(k, s, act, w)

        @block.vector
        def _(dve):
            w = Walk()
            dve.wait_ge(k.x_loaded, 16)
            even_vector(k, f, dve, w)
            tables_vector(k, f, dve)
            tail_vector(k, f, dve, w, 0)
            odd_vector(k, f, dve, w)
            tail_vector(k, f, dve, w, 1)
            between(w)
            second_vector(k, s, dve, w)

        @block.gpsimd
        def _(pool):
            w = Walk()
            even_pool(k, f, pool)
            between(w)
            second_pool(k, s, pool, w, params2)



def constants():
    c = np.zeros((P, NCOLC), np.float32)
    i = np.arange(P)
    s, t = i[:, None], i[None, :]
    near, chunk = s // 16 == t // 16, s // CHUNK == t // CHUNK

    def put(name, a):
        c[:, COLC[name][0]:COLC[name][1]] = a
    put("ident", s == t)
    put("ones", 1)
    put("block64", s // HEAD == t // HEAD)
    put("near_st", (s < t) & near)
    put("near_ts", (s > t) & near)
    put("far_st", (s < t) & chunk & ~near)
    put("before_st", (s < t) & chunk)
    put("upto_st", (s <= t) & chunk)
    put("tril_st", s <= t)
    put("restart", np.arange(2 * T)[None, :] % CHUNK != 0)
    sel = np.zeros((P, 2 * P))
    for ch in range(2 * P):
        sel[ch // HEAD, ch] = 1
    put("headsel", sel)
    put("causal_st", np.where(s <= t, 0, NEG))
    put("causal_qk", np.where(t <= s, 0, NEG))
    q, m = np.arange(2)[None, :, None] * P + i[:, None, None], np.arange(16)[None, None, :]
    put("cmp_mask", np.where((16 * m + 31 <= q) & (m < 15), 0, NEG).reshape(P, 32))
    put("head4", np.arange(4 * P)[None, :] // P == i[:, None])
    for name, half in (("swap64", 32), ("swap32", 16)):
        m = np.zeros((P, P))
        for o in range(P):
            r = o % HEAD
            if r < half:
                m[o + half, o] = -1
            elif r < 2 * half:
                m[o - half, o] = 1
        put(name, m)
    inv = lambda d: (np.float32(10000.0) ** (-np.arange(0, d, 2, dtype=np.float32) / np.float32(d))).astype(np.float32)
    r = i % HEAD
    put("inv_freq", np.stack([inv(64)[r % 32], np.where(r < 32, inv(32)[r % 16], 0)], axis=1))
    a = COLC["eps"][0]
    for value, j in EPS.items():
        c[:, a + j] = value
    return c


def channels(a):
    a = np.asarray(a)
    if a.ndim == 1:
        return a.reshape(-1, P).T
    return a.reshape(a.shape[0], -1, P).transpose(2, 1, 0).reshape(P, -1)


def units_in(wt):
    n = wt.shape[1] // P
    return wt.reshape(KD, P, n, P).transpose(2, 1, 0, 3).reshape(n, P, UNIT)


def ffn_units(ins, down):
    ins, down = [units_in(a) for a in ins], down.reshape(-1, P, UNIT)
    out = []
    for f in range(len(down)):
        out += [a[f] for a in ins]
        if f:
            out.append(down[f - 1])
    return out + [down[-1]]


def second_units(v, l):
    w_in = v["w_in"][l]
    a, b, c, d = np.split(w_in, [768, 1280, 2176], axis=1)
    gate_b, gate_c, xa = np.split(a, 3, axis=1)
    u, vv = np.split(b, 2, axis=1)
    order = np.concatenate([c, d, gate_c, xa, gate_b, vv, u], axis=1)
    units = ffn_units([v["ffn1_w_gate"][l], v["ffn1_w_up"][l]], v["ffn1_w_down"][l])
    units += list(units_in(order)) + list(units_in(v["w_out"][l]))
    units += ffn_units([v["ffn2_w_gate"][l], v["ffn2_w_up"][l]], v["ffn2_w_down"][l])
    units += [np.zeros((P, UNIT), np.float32)] * PAD2
    assert len(units) == UNITS2
    return units


def second_params(v, l):
    out = np.zeros((P, NCOL2), np.float32)
    for name, _ in VEC2:
        a, b = COL2[name]
        if name == "lora_up":
            out[:, a:b] = np.concatenate([v["rk_w_up"][l], v["rk_a_up"][l], v["rk_g_up"][l]], axis=0)
        elif name == "sg_w":
            out[:, a:b] = v["sg_w"][l].transpose(2, 0, 1).reshape(P, -1)
        elif name == "sg_b":
            out[0:4, a:b] = v["sg_b"][l]
        else:
            src = v[name][l]
            out[:, a:b] = channels(src.reshape(-1) if name == "rk_r_k" else src)
    return out


def square_units(wt, inner):
    kt, n = wt.shape[0] // P, wt.shape[1] // inner
    per = UNIT // inner
    a = wt.reshape(kt, P, n, inner).transpose(2, 0, 1, 3)
    a = a.reshape(-1, P, inner)
    return a.reshape(-1, per, P, inner).transpose(0, 2, 1, 3).reshape(-1, P, UNIT)


def first_units(v):
    sizes = (512, 512, 512, 512, 4, 4, 512, 128, 128, 128, 128, 128, 128, 24)
    aq, ak, av, ao, ai, af, bq, kc, vc, ks, vs, kw, vw, bg = np.split(v["e_w_in"][0], np.cumsum(sizes)[:-1], axis=1)
    perm = np.concatenate([np.arange(HEAD) + (g * 4 + j) * HEAD for j in range(4) for g in range(2)])
    gates = np.zeros((D, P), np.float32)
    gates[:, 0:24], gates[:, 24:28], gates[:, 28:32] = bg, ai, af
    units = [*units_in(aq), *units_in(ak), *units_in(gates), *square_units(av, 512)]
    units += [*units_in(bq[:, perm]), *units_in(np.concatenate([kc, vc, ks, kw], axis=1))]
    units += [*square_units(np.concatenate([vs, vw], axis=1), 256), *units_in(ao)]
    for j in range(2):
        units += list(square_units(v["e_b_cmp_w1"][0, j], P))
    w_out = v["e_w_out"][0]
    units += list(units_in(np.concatenate([w_out[0:512], w_out[512:][perm]], axis=0)))
    units += first_tail_units(v, 0)

    cq, ckv, kr, ik, iw = np.split(v["o_w_in"][0], [512, 768, 832, 896], axis=1)
    units += list(units_in(np.concatenate([cq, ckv, kr, kr, ik, ik], axis=1)))
    weights = np.zeros((D, P), np.float32)
    weights[:, 0:8] = iw
    units += list(units_in(weights))
    qb = v["o_w_qb"][0].reshape(512, 8, P + HEAD)
    units += list(square_units(v["o_w_iq"][0], P))
    units += list(square_units(qb[:, :, P:].reshape(512, -1), P))
    units += list(square_units(qb[:, :, 0:P].reshape(512, -1), P))
    uk = v["o_w_uk"][0].transpose(1, 2, 0)
    units += list(uk.reshape(2, 4, P, 256).transpose(0, 2, 1, 3).reshape(2, P, UNIT))
    uv = v["o_w_uv"][0].reshape(2, P, 2, 4, P)
    units += list(uv.transpose(2, 1, 3, 0, 4).reshape(2, P, UNIT))
    units += list(units_in(v["o_w_out"][0]))
    units += first_tail_units(v, 1)
    return units


def first_tail_units(v, l):
    units = ffn_units([v["mlp_w1"][l]], v["mlp_w2"][l])
    gate, ple = list(units_in(v["ple_gate_w"][l])), list(square_units(v["ple_w"][l], P))
    return units + ple + gate


def first_params(v):
    out = np.zeros((P, NCOL1), np.float32)

    def put(name, a, rows=slice(0, P)):
        out[rows, COL1[name][0]:COL1[name][1]] = a
    put("conv_w", channels(v["e_a_conv"][0]))
    put("a_norm", channels(v["e_a_norm"][0]))
    put("i_b", v["e_a_i_b"][0][:, None], slice(0, 4))
    put("f_b", v["e_a_f_b"][0][:, None], slice(0, 4))
    put("g_b", v["e_b_g_b"][0], slice(0, 1))
    put("cmp_pos", v["e_b_cmp_pos"][0].reshape(2, 16, P).transpose(2, 0, 1).reshape(P, 32))
    put("cmp_w2", v["e_b_cmp_w2"][0].transpose(1, 0, 2).reshape(P, P))
    put("q_norm", channels(v["o_q_norm"][0]))
    put("kv_norm", channels(v["o_kv_norm"][0]))
    put("ik_g", np.tile(v["o_ik_g"][0], 2)[:, None])
    put("ik_b", np.tile(v["o_ik_b"][0], 2)[:, None])
    for name in ("ln1_g", "ln1_b", "ln2_g", "ln2_b"):
        put(name, np.concatenate([channels(v[name][l]) for l in range(LAYERS)], axis=1))
    put("embed", v["p"][:, 0].reshape(LAYERS, T, 2, P).transpose(3, 0, 2, 1).reshape(P, -1))
    return out


def kernel(**inputs):
    import concourse.bacc as bacc
    from concourse.bass_utils import run_bass_kernel_spmd as run

    v = {n: np.asarray(a) for n, a in inputs.items()}
    v2 = {n[:-2]: a for n, a in v.items() if n.endswith("_2")}
    units = first_units(v) + [u for l in range(LAYERS) for u in second_units(v2, l)]
    arrays = {
        "x": np.ascontiguousarray(v["x"][0].T.reshape(KD, P, T).transpose(1, 0, 2)),
        "consts": constants(),
        "weights": np.stack(units),
        "params1": first_params(v),
        "positions": np.ascontiguousarray(v["positions"]),
        "params2": np.stack([second_params(v2, l) for l in range(LAYERS)]),
    }
    nc = bacc.Bacc("TRN2", target_bir_lowering=False, num_devices=1)
    args = [nc.dram_tensor(f"in_{n}", a.shape, mybir.dt.from_np(a.dtype), kind="ExternalInput").ap() for n, a in arrays.items()]
    out = nc.dram_tensor("out", (P, KD, T), F32, kind="ExternalOutput").ap()
    build(nc, *args, out)
    got = run(nc, [{f"in_{n}": a for n, a in arrays.items()}], core_ids=[0]).results[0]["out"]
    return np.ascontiguousarray(got.transpose(2, 1, 0).reshape(1, T, D))
```
